# Optimizing a Trainium2 kernel written in Bass

```python
import math
import jax, jax.numpy as jnp
from jax import lax
import numpy as np

D_MODEL = 1024
BATCH = 1
SEQ = 1024
DEPTH = 1

MEM_LEN = 256
RWKV_HEAD_DIM = 64
RWKV_WIDTH = D_MODEL // 2
RWKV_HEADS = RWKV_WIDTH // RWKV_HEAD_DIM
DECAY_LORA = 64
ICLR_LORA = 64
GATE_LORA = 160
RWKV_IN = 3 * RWKV_WIDTH + DECAY_LORA + ICLR_LORA + GATE_LORA
RWKV_GN_EPS = 64e-5
DIFF_HEAD_DIM = 64
DIFF_WIDTH = D_MODEL - RWKV_WIDTH
DIFF_HEADS = DIFF_WIDTH // (2 * DIFF_HEAD_DIM)
DIFF_IN = 3 * DIFF_WIDTH
MIX_IN = RWKV_IN + DIFF_IN
Q_BLOCK = 128
CROSS_HEADS = 4
CROSS_HEAD_DIM = D_MODEL // CROSS_HEADS
N_EXPERTS = 32
TOP_K = 4
D_FF_EXPERT = D_MODEL
SWIGLU_LIMIT = 7.0
SWIGLU_ALPHA = 1.702
MOE_BLOCK = 128
NORM_EPS = 1e-5

kernel_name = 'hymba_rwkv7_diffattn_moe_layer'

def rms_norm(x, g, eps=NORM_EPS):
    xf = x.astype(jnp.float32)
    y = xf * lax.rsqrt(jnp.mean(xf * xf, axis=-1, keepdims=True) + eps)
    return (y * g.astype(jnp.float32)).astype(x.dtype)

def token_shift(y, mu):
    y_prev = jnp.pad(y, ((0, 0), (1, 0), (0, 0)))[:, :-1]
    return y + mu * (y_prev - y)

def alibi_slopes(n):
    return jnp.exp2(-8.0 * jnp.arange(1, n + 1, dtype=jnp.float32) / n)

def diff_lambda_init(layer):
    return 0.8 - 0.6 * math.exp(-0.3 * layer)

def rwkv7_group(u, w0, w_decay_up, a0, w_iclr_up, w_gate_up, k_k, k_a, r_k, lnx_g, lnx_b):
    f32 = jnp.float32
    B, S, _ = u.shape
    H, N, C = RWKV_HEADS, RWKV_HEAD_DIM, RWKV_WIDTH
    r, k, v, xw, xa, xg = jnp.split(
        u, [C, 2 * C, 3 * C, 3 * C + DECAY_LORA, 3 * C + DECAY_LORA + ICLR_LORA], axis=-1)
    w_log = -jax.nn.softplus(-(w0 + jnp.tanh(xw) @ w_decay_up)) - 0.5
    decay = jnp.exp(-jnp.exp(w_log.astype(f32)))
    a = jax.nn.sigmoid(a0 + xa @ w_iclr_up)
    g = jax.nn.sigmoid(xg) @ w_gate_up
    heads = lambda t: t.reshape(B, S, H, N)
    kk = heads(k * k_k).astype(f32)
    kk = kk / jnp.maximum(jnp.linalg.norm(kk, axis=-1, keepdims=True), 1e-12)
    k = k * (1.0 + (a - 1.0) * k_a)
    r_h, k_h, v_h, a_h = heads(r), heads(k), heads(v), heads(a)
    seq_first = lambda t: jnp.moveaxis(t.astype(f32), 1, 0)

    def step(state, inp):
        r_t, w_t, k_t, v_t, kk_t, a_t = inp
        sa = jnp.einsum('bhvk,bhk->bhv', state, -kk_t)
        state = (state * w_t[:, :, None, :]
                 + sa[..., None] * (kk_t * a_t)[:, :, None, :]
                 + v_t[..., None] * k_t[:, :, None, :])
        return state, jnp.einsum('bhvk,bhk->bhv', state, r_t)

    state0 = jnp.zeros((B, H, N, N), f32)
    scan_in = (seq_first(r_h), seq_first(heads(decay)), seq_first(k_h),
               seq_first(v_h), seq_first(kk), seq_first(a_h))
    _, y = lax.scan(step, state0, scan_in)
    y = jnp.moveaxis(y, 0, 1)
    mu = jnp.mean(y, axis=-1, keepdims=True)
    var = jnp.mean(jnp.square(y - mu), axis=-1, keepdims=True)
    y = ((y - mu) * lax.rsqrt(var + RWKV_GN_EPS)).reshape(B, S, C)
    y = y * lnx_g.astype(f32) + lnx_b.astype(f32)
    bonus = jnp.sum((r_h * k_h * r_k).astype(f32), axis=-1, keepdims=True) * v_h.astype(f32)
    y = (y + bonus.reshape(B, S, C)) * g.astype(f32)
    return y.astype(u.dtype)

def diff_attention_group(u, lambda_q1, lambda_k1, lambda_q2, lambda_k2, subln_g, lambda_init):
    f32 = jnp.float32
    B, S, _ = u.shape
    H, d = DIFF_HEADS, DIFF_HEAD_DIM
    q, k, v = jnp.split(u, 3, axis=-1)
    q = q.reshape(B, S, H, 2, d) * (d ** -0.5)
    k = k.reshape(B, S, H, 2, d)
    v = v.reshape(B, S, H, 2 * d)
    lam = (jnp.exp(jnp.sum(lambda_q1 * lambda_k1).astype(f32))
           - jnp.exp(jnp.sum(lambda_q2 * lambda_k2).astype(f32)) + lambda_init)
    slopes = alibi_slopes(H)
    n_blocks = S // Q_BLOCK
    q_blocks = jnp.moveaxis(q.reshape(B, n_blocks, Q_BLOCK, H, 2, d), 1, 0)
    key_pos = jnp.arange(S)

    def block(args):
        qb, bi = args
        q_pos = bi * Q_BLOCK + jnp.arange(Q_BLOCK)
        dist = (q_pos[:, None] - key_pos[None, :]).astype(f32)
        bias = jnp.where(dist[None] >= 0, -slopes[:, None, None] * dist[None], -jnp.inf)
        s = jnp.einsum('bqhcd,bkhcd->bhcqk', qb, k).astype(f32) + bias[None, :, None]
        p = jax.nn.softmax(s, axis=-1)
        attn = p[:, :, 0] - lam * p[:, :, 1]
        return jnp.einsum('bhqk,bkhe->bqhe', attn.astype(v.dtype), v)

    o = lax.map(block, (q_blocks, jnp.arange(n_blocks)))
    o = jnp.moveaxis(o, 0, 1).reshape(B, S, H, 2 * d)
    o = rms_norm(o, subln_g) * (1.0 - lambda_init)
    return o.reshape(B, S, DIFF_WIDTH)

def cross_attention(h, m, w_cq, w_ckv, w_co):
    B, S, D = h.shape
    M = m.shape[1]
    q = (h @ w_cq).reshape(B, S, CROSS_HEADS, CROSS_HEAD_DIM)
    k, v = jnp.split(m @ w_ckv, 2, axis=-1)
    k = k.reshape(B, M, CROSS_HEADS, CROSS_HEAD_DIM)
    v = v.reshape(B, M, CROSS_HEADS, CROSS_HEAD_DIM)
    s = jnp.einsum('bqhd,bkhd->bhqk', q, k).astype(jnp.float32) * (CROSS_HEAD_DIM ** -0.5)
    p = jax.nn.softmax(s, axis=-1).astype(v.dtype)
    o = jnp.einsum('bhqk,bkhd->bqhd', p, v).reshape(B, S, D)
    return o @ w_co

def clamped_swiglu(hid):
    x_glu = jnp.minimum(hid[..., ::2], SWIGLU_LIMIT)
    x_lin = jnp.clip(hid[..., 1::2], -SWIGLU_LIMIT, SWIGLU_LIMIT)
    return x_glu * jax.nn.sigmoid(SWIGLU_ALPHA * x_glu) * (x_lin + 1.0)

def moe_ffn(h, w_router, b_router, w1, b1, w2, b2):
    B, S, D = h.shape
    T = B * S
    n_assign = T * TOP_K
    n_blocks = n_assign // MOE_BLOCK + N_EXPERTS
    n_rows = n_blocks * MOE_BLOCK
    xt = h.reshape(T, D)
    logits = (xt @ w_router + b_router).astype(jnp.float32)
    top_vals, top_idx = lax.top_k(logits, TOP_K)
    gates = jax.nn.softmax(top_vals, axis=-1)
    flat_e = top_idx.reshape(-1)
    flat_tok = jnp.repeat(jnp.arange(T, dtype=jnp.int32), TOP_K)
    flat_gate = gates.reshape(-1)
    order = jnp.argsort(flat_e)
    sorted_e = flat_e[order]
    counts = jnp.bincount(flat_e, length=N_EXPERTS)
    padded = (counts + MOE_BLOCK - 1) // MOE_BLOCK * MOE_BLOCK
    start = jnp.cumsum(counts) - counts
    pad_end = jnp.cumsum(padded)
    pad_start = pad_end - padded
    dest = pad_start[sorted_e] + jnp.arange(n_assign, dtype=jnp.int32) - start[sorted_e]
    row_tok = jnp.full((n_rows,), T, jnp.int32).at[dest].set(flat_tok[order])
    row_gate = jnp.zeros((n_rows,), jnp.float32).at[dest].set(flat_gate[order])
    block_e = jnp.minimum(
        jnp.searchsorted(pad_end, jnp.arange(n_blocks, dtype=jnp.int32) * MOE_BLOCK, side='right'),
        N_EXPERTS - 1)
    x_pad = jnp.concatenate([xt, jnp.zeros((1, D), xt.dtype)], axis=0)

    def expert_block(args):
        tok, e = args
        hid = x_pad[tok] @ w1[e] + b1[e]
        return clamped_swiglu(hid) @ w2[e] + b2[e]

    y = lax.map(expert_block, (row_tok.reshape(n_blocks, MOE_BLOCK), block_e))
    y = y.reshape(n_rows, D) * row_gate[:, None].astype(y.dtype)
    out = jax.ops.segment_sum(y, row_tok, num_segments=T + 1)[:T]
    return out.reshape(B, S, D)

def setup_inputs(seed: int = 0) -> dict:
    key = jax.random.key(seed)
    ks = iter(jax.random.split(key, 48))
    f32 = jnp.float32
    L, D, E, F = DEPTH, D_MODEL, N_EXPERTS, D_FF_EXPERT
    C, d = RWKV_WIDTH, DIFF_HEAD_DIM

    def normal(shape, scale):
        return scale * jax.random.normal(next(ks), shape, f32)

    def gain(shape):
        return 1.0 + 0.02 * jax.random.normal(next(ks), shape, f32)

    def uniform(shape, lo, hi):
        return jax.random.uniform(next(ks), shape, f32, lo, hi)

    return {
        'x': normal((BATCH, SEQ, D), 1.0),
        'mem': normal((BATCH, MEM_LEN, D), 1.0),
        'norm_mix_g': gain((L, D)),
        'w_in': normal((L, D, MIX_IN), D ** -0.5),
        'shift_mu': uniform((L, RWKV_IN), 0.0, 1.0),
        'w0': uniform((L, C), -4.0, 1.0),
        'w_decay_up': normal((L, DECAY_LORA, C), 0.5 * DECAY_LORA ** -0.5),
        'a0': normal((L, C), 0.1),
        'w_iclr_up': normal((L, ICLR_LORA, C), ICLR_LORA ** -0.5),
        'w_gate_up': normal((L, GATE_LORA, C), GATE_LORA ** -0.5),
        'k_k': 0.85 + normal((L, C), 0.02),
        'k_a': gain((L, C)),
        'r_k': normal((L, RWKV_HEADS, RWKV_HEAD_DIM), 0.1),
        'lnx_g': gain((L, C)),
        'lnx_b': normal((L, C), 0.01),
        'lambda_q1': normal((L, d), 0.1),
        'lambda_k1': normal((L, d), 0.1),
        'lambda_q2': normal((L, d), 0.1),
        'lambda_k2': normal((L, d), 0.1),
        'subln_g': gain((L, 2 * d)),
        'w_out': normal((L, D, D), D ** -0.5),
        'norm_cross_g': gain((L, D)),
        'norm_mem_g': gain((L, D)),
        'w_cq': normal((L, D, D), D ** -0.5),
        'w_ckv': normal((L, D, 2 * D), D ** -0.5),
        'w_co': normal((L, D, D), D ** -0.5),
        'norm_ffn_g': gain((L, D)),
        'w_router': normal((L, D, E), D ** -0.5),
        'b_router': normal((L, E), 0.01),
        'w1': normal((L, E, D, 2 * F), D ** -0.5),
        'b1': normal((L, E, 2 * F), 0.01),
        'w2': normal((L, E, F, D), F ** -0.5),
        'b2': normal((L, E, D), 0.01),
        'norm_final_g': gain((D,)),
    }

def reference(x, mem, norm_mix_g, w_in, shift_mu, w0, w_decay_up, a0, w_iclr_up, w_gate_up,
              k_k, k_a, r_k, lnx_g, lnx_b, lambda_q1, lambda_k1, lambda_q2, lambda_k2, subln_g,
              w_out, norm_cross_g, norm_mem_g, w_cq, w_ckv, w_co, norm_ffn_g, w_router, b_router,
              w1, b1, w2, b2, norm_final_g):
    for l in range(DEPTH):
        h = rms_norm(x, norm_mix_g[l])
        proj = h @ w_in[l]
        u_rwkv = token_shift(proj[..., :RWKV_IN], shift_mu[l])
        u_diff = proj[..., RWKV_IN:]
        y_rwkv = rwkv7_group(u_rwkv, w0[l], w_decay_up[l], a0[l], w_iclr_up[l], w_gate_up[l],
                             k_k[l], k_a[l], r_k[l], lnx_g[l], lnx_b[l])
        y_diff = diff_attention_group(u_diff, lambda_q1[l], lambda_k1[l], lambda_q2[l],
                                      lambda_k2[l], subln_g[l], diff_lambda_init(l))
        x = x + jnp.concatenate([y_rwkv, y_diff], axis=-1) @ w_out[l]
        x = x + cross_attention(rms_norm(x, norm_cross_g[l]), rms_norm(mem, norm_mem_g[l]),
                                w_cq[l], w_ckv[l], w_co[l])
        x = x + moe_ffn(rms_norm(x, norm_ffn_g[l]), w_router[l], b_router[l],
                        w1[l], b1[l], w2[l], b2[l])
    return rms_norm(x, norm_final_g)


_drawn_inputs = setup_inputs


def setup_inputs(seed=0):
    import zlib

    import numpy as np

    out = dict(_drawn_inputs(seed))
    spreads = {}
    factors = {'k_k': 3.499,
     'lnx_b': 6.765,
     'norm_cross_g': 6.26,
     'norm_mem_g': 4.999,
     'b1': 44.927,
     'b2': 51.434,
     'norm_final_g': 8.076,
     'norm_ffn_g': 5.462,
     'b_router': 8.0}
    for name, (base, spread) in spreads.items():
        noise = np.random.default_rng([zlib.crc32(name.encode()), seed]).standard_normal(out[name].shape)
        drawn = base * np.exp(spread * noise) if base else spread * noise
        out[name] = __import__('jax').numpy.asarray(drawn.astype(out[name].dtype))
    for name, factor in factors.items():
        out[name] = (out[name] * factor).astype(out[name].dtype)
    return out
```

```python
from contextlib import ExitStack

import numpy as np
import concourse.bass as bass
from concourse import mybir

F32 = mybir.dt.float32
BF16 = mybir.dt.bfloat16
I32 = mybir.dt.int32
U32 = mybir.dt.uint32
ALU = mybir.AluOpType
ACT = mybir.ActivationFunctionType
AX = mybir.AxisListType.X
P = 128
EPS = 1e-5
ds = bass.ds


class Steps:

    def __init__(self, sem, names, back=1):
        self.sem, self.names, self.start = sem, names, max(1, back * len(names))
        self.at = 0

    def round(self):
        self.at = 0

    def value(self, name, i=0):
        return i * len(self.names) + self.start + self.names.index(name) + 1

    def step(self, name):
        self.at %= len(self.names)
        assert self.names[self.at] == name, (self.names[self.at], name)
        self.at += 1
        return self.sem, 1

    def so_far(self, i=0):
        return i * len(self.names) + self.start + self.at

    def end(self, rounds=1):
        return rounds * len(self.names) + self.start


class Scope:

    spent = []

    def __init__(self, nc, ctx, name):
        self.nc, self.ctx, self.name = nc, ctx, name

    def sb(self, name, shape, dt=F32):
        return self.ctx.enter_context(self.nc.sbuf_tensor(f"{self.name}_{name}", shape, dt))

    def ps(self, name, shape, dt=F32):
        return self.ctx.enter_context(self.nc.psum_tensor(f"{self.name}_{name}", shape, dt))

    def sem(self, name):
        made = self.nc.alloc_semaphore(f"{self.name}_{name}")
        self.ctx.callback(Scope.spent.append, made)
        return made

    def steps(self, name, names, back=1):
        return Steps(self.sem(name), names, back)


def recycle(nc):
    nc.all_engine_barrier()
    nc.clear_and_free_semaphores(Scope.spent)
    nc.all_engine_barrier()
    Scope.spent = []


def scope(nc, ctx, name):
    return Scope(nc, ctx, name)


def row_to_all(vec, n=P):
    return vec.rearrange("(a n) -> a n", a=1).partition_broadcast(n).rearrange("p a n -> p (a n)")


def make_constants(nc, S, C):
    C.ident = S.sb("ident", [P, P])
    made = S.steps("pool_made", ["zero", "ident"])
    with nc.Block() as block:
        @block.gpsimd
        def _(pool):
            pool.sem_inc(made.sem, made.start)
            pool.memset(C.ident[:], 0.0).then_inc(*made.step("zero"))
            pool.wait_ge(made.sem, made.so_far())
            pool.affine_select(out=C.ident[:], in_=C.ident[:], compare_op=ALU.not_equal,
                               fill=1.0, base=0, pattern=[[-1, P]], channel_multiplier=1).then_inc(*made.step("ident"))
            pool.wait_ge(made.sem, made.end())


def normalise(nc, name, x, tiles, gain, hT, C, load=None, keep=None):
    D = 1024
    KT = D // P
    with ExitStack() as ctx:
        S = scope(nc, ctx, name)
        gains = S.sb("gains", [P, D])
        rows = S.sb("rows", [P, 2 * D])
        junk = S.sb("junk", [P, D])
        stat = S.sb("stat", [P, 4 * tiles])
        sums, mean, root, rstd = (stat[:, i * tiles:(i + 1) * tiles] for i in range(4))
        flipped = S.ps("flipped", [P, 2, D])
        x_in, gain_in = [S.sem(f"x_in{t}") for t in range(tiles)], S.sem("gain_in")
        rows_out = [S.sem(f"rows_out{j}") for j in range(2)]
        squares = S.steps("squares", ["tile"], back=1)
        rooted = S.sem("rooted")
        stats = S.steps("stats", ["mean", "rstd"])
        scaled = S.steps("scaled", ["even", "odd"])
        turned = S.steps("turned", ["even", "odd"])
        copied = S.steps("copied", ["even", "odd"])
        pair = ["even", "odd"]
        with nc.Block() as block:
            @block.sync
            def _(sp):
                sp.dma_start(gains[:], row_to_all(gain)).then_inc(gain_in, 16)
                if load is not None:
                    for t in range(tiles):
                        sp.dma_start(x[:, t * D:(t + 1) * D], load[t * P:(t + 1) * P, :]).then_inc(x_in[t], 16)
                if keep is not None:
                    for j in range(2):
                        sp.sem_inc(rows_out[j], 16)
                    with sp.Fori(0, tiles // 2) as i:
                        for j in range(2):
                            sp.wait_ge(scaled.sem, scaled.value(pair[j], i))
                            sp.dma_start(keep[ds(i * (2 * P) + j * P, P), :],
                                         rows[:, j * D:(j + 1) * D]).then_inc(rows_out[j], 16)
                    for j in range(2):
                        sp.wait_ge(rows_out[j], 16 * (tiles // 2) + 16)

            @block.scalar
            def _(act):
                act.sem_inc(squares.sem, squares.start)
                act.sem_inc(copied.sem, copied.start)
                for t in range(tiles):
                    if load is not None:
                        act.wait_ge(x_in[t], 16)
                    squares.round()
                    act.wait_ge(squares.sem, squares.so_far(t))
                    act.activation(junk[:], x[:, t * D:(t + 1) * D], ACT.Square,
                                   accum_out=sums[:, t:t + 1]).then_inc(*squares.step("tile"))
                act.wait_ge(stats.sem, stats.value("mean"))
                act.activation(root, mean, ACT.Sqrt).then_inc(rooted, 1)
                with act.Fori(0, tiles // 2) as i:
                    for j in range(2):
                        act.wait_ge(turned.sem, turned.value(pair[j], i))
                        act.copy(hT[:, :, ds(i * (2 * P) + j * P, P)],
                                 flipped[:, j, :].rearrange("p (k n) -> p k n", n=P)).then_inc(*copied.step(pair[j]))
                act.wait_ge(copied.sem, copied.end(tiles // 2))

            @block.vector
            def _(dve):
                dve.sem_inc(stats.sem, stats.start)
                dve.sem_inc(scaled.sem, scaled.start)
                dve.wait_ge(squares.sem, squares.value("tile", tiles - 1))
                dve.tensor_scalar(mean, sums, 1.0 / D, EPS, ALU.mult, ALU.add).then_inc(*stats.step("mean"))
                dve.wait_ge(rooted, 1)
                dve.reciprocal(rstd, root).then_inc(*stats.step("rstd"))
                dve.wait_ge(stats.sem, stats.so_far())
                dve.wait_ge(gain_in, 16)
                with dve.Fori(0, tiles // 2) as i:
                    for j in range(2):
                        dve.wait_ge(turned.sem, turned.value(pair[j], i - 1))
                        if keep is not None:
                            dve.wait_ge(rows_out[j], i * 16 + 16)
                        t = 2 * i + j
                        dve.scalar_tensor_tensor(rows[:, j * D:(j + 1) * D], x[:, ds(t * D, D)],
                                                 rstd[:, ds(t, 1)], gains[:], ALU.mult, ALU.mult).then_inc(*scaled.step(pair[j]))

            @block.tensor
            def _(pe):
                pe.sem_inc(turned.sem, turned.start)
                with pe.Fori(0, tiles // 2) as i:
                    for j in range(2):
                        pe.wait_ge(scaled.sem, scaled.value(pair[j], i))
                        pe.wait_ge(copied.sem, copied.value(pair[j], i - 1))
                        for k in range(KT):
                            ins = pe.transpose(flipped[:, j, k * P:(k + 1) * P],
                                               rows[:, j * D + k * P:j * D + (k + 1) * P], C.ident[:])
                        ins.then_inc(*turned.step(pair[j]))


def project_channels(nc, name, w, rounds, hT, result, scale=None, mu=None):
    T = 1024
    with ExitStack() as ctx:
        S = scope(nc, ctx, name)
        weights = S.sb("weights", [P, 2, 8, 256])
        product = S.ps("product", [P, 2, T])
        w_in = [S.sem(f"w_in{j}") for j in range(2)]
        tiles = ["tile0", "tile1", "tile2", "tile3"]
        multiplied = S.steps("multiplied", tiles)
        copied = S.steps("copied", tiles)
        shifted = S.steps("shifted", tiles)
        if mu is not None:
            keep_mu = S.sb("keep_mu", [P, 4 * rounds])
            kept = S.sem("kept")
        with nc.Block() as block:
            @block.sync
            def _(sp):
                with sp.Fori(0, rounds) as i:
                    for j in range(2):
                        sp.wait_ge(multiplied.sem, multiplied.value(tiles[2 * j + 1], i - 1))
                        sp.dma_start(weights[:, j], w[:, ds(i * 512 + j * 256, 256)]
                                     .rearrange("(k p) n -> p k n", p=P)).then_inc(w_in[j], 16)

            @block.tensor
            def _(pe):
                pe.sem_inc(multiplied.sem, multiplied.start)
                with pe.Fori(0, rounds) as i:
                    for c in range(4):
                        if c % 2 == 0:
                            pe.wait_ge(w_in[c // 2], i * 16 + 16)
                        before = (tiles[c - 2], i) if c >= 2 else (tiles[c + 2], i - 1)
                        pe.wait_ge(copied.sem, copied.value(*before))
                        if mu is not None:
                            pe.wait_ge(shifted.sem, shifted.value(*before))
                        for half in range(2):
                            for k in range(8):
                                ins = pe.matmul(product[:, c % 2, half * 512:(half + 1) * 512],
                                                weights[:, c // 2, k, (c % 2) * P:(c % 2 + 1) * P],
                                                hT[:, k, half * 512:(half + 1) * 512], start=(k == 0), stop=(k == 7))
                        ins.then_inc(*multiplied.step(tiles[c]))

            @block.scalar
            def _(act):
                act.sem_inc(copied.sem, copied.start)
                if mu is not None:
                    act.wait_ge(kept, 1)
                with act.Fori(0, rounds) as i:
                    for c in range(4):
                        act.wait_ge(multiplied.sem, multiplied.value(tiles[c], i))
                        factor = scale[:, ds(i, 1)] if mu is None else keep_mu[:, ds(i * 4 + c, 1)]
                        act.activation(result[:, ds(i * 4 + c, 1), :].rearrange("p a n -> p (a n)"),
                                       product[:, c % 2, :], ACT.Copy, scale=factor).then_inc(*copied.step(tiles[c]))
                act.wait_ge(copied.sem, copied.end(rounds))

            @block.vector
            def _(dve):
                if mu is None:
                    return
                dve.sem_inc(shifted.sem, shifted.start)
                dve.tensor_scalar(keep_mu[:], mu[:, 0:4 * rounds], -1.0, 1.0, ALU.mult, ALU.add).then_inc(kept, 1)
                with dve.Fori(0, rounds) as i:
                    for c in range(4):
                        dve.wait_ge(copied.sem, copied.value(tiles[c], i))
                        later = result[:, ds(i * 4 + c, 1), 1:T].rearrange("p a n -> p (a n)")
                        dve.scalar_tensor_tensor(later, product[:, c % 2, 0:T - 1],
                                                 mu[:, ds(i * 4 + c, 1)], later,
                                                 ALU.mult, ALU.add).then_inc(*shifted.step(tiles[c]))
                dve.wait_ge(shifted.sem, shifted.end(rounds))


def load_vectors(nc, S, I, C):
    wanted = [("mu", I["shift_mu"][0, 0:1792], 14), ("w0", I["w0"][0], 4), ("a0", I["a0"][0], 4),
              ("k_k", I["k_k"][0], 4), ("k_a", I["k_a"][0], 4),
              ("r_k", I["r_k"][0].rearrange("h n -> (h n)"), 4), ("lnx_g", I["lnx_g"][0], 4),
              ("lnx_b", I["lnx_b"][0], 4), ("subln_g", I["subln_g"][0], 1)]
    vectors = S.sb("vectors", [P, sum(n for _, _, n in wanted)])
    at = 0
    loaded = S.sem("vectors_in")
    places = []
    for name, source, n in wanted:
        part = vectors[:, at:at + n]
        C.vector[name] = part
        places.append((part, source.rearrange("(c p) -> p c", p=P)))
        at += n
    C.mu_tail = S.sb("mu_tail", [32, 1])
    places.append((C.mu_tail[:], I["shift_mu"][0, 1792:1824].rearrange("(c p) -> p c", p=32)))
    C.qk_scale = S.sb("qk_scale", [P, 2])
    C.cross_scale = S.sb("cross_scale", [P, 2])
    C.lam = S.sb("lam", [P, 1])
    lam_in = S.sb("lam_in", [P, 4 * 64])
    products = S.sb("lam_products", [P, 2 * 64])
    sums = S.sb("lam_sums", [P, 4])
    for n, v in enumerate(["lambda_q1", "lambda_k1", "lambda_q2", "lambda_k2"]):
        places.append((lam_in[:, n * 64:(n + 1) * 64], row_to_all(I[v][0])))
    made = S.steps("lambda", ["q_scale", "k_scale", "cross_scale", "product1", "product2", "sums", "difference", "sum"])
    powers = S.sem("lambda_powers")
    with nc.Block() as block:
        @block.sync
        def _(sp):
            for place, source in places:
                sp.dma_start(place, source, allow_slow_non_contiguous=True).then_inc(loaded, 16)

        @block.vector
        def _(dve):
            dve.sem_inc(made.sem, made.start)
            dve.memset(C.qk_scale[:, 0:1], 64 ** -0.5).then_inc(*made.step("q_scale"))
            dve.memset(C.qk_scale[:, 1:2], 1.0).then_inc(*made.step("k_scale"))
            dve.memset(C.cross_scale[:], 256 ** -0.5).then_inc(*made.step("cross_scale"))
            dve.wait_ge(loaded, 16 * len(places))
            for n in range(2):
                dve.tensor_tensor(products[:, n * 64:(n + 1) * 64], lam_in[:, n * 128:n * 128 + 64],
                                  lam_in[:, n * 128 + 64:n * 128 + 128], ALU.mult).then_inc(*made.step(f"product{n + 1}"))
            dve.wait_ge(made.sem, made.so_far())
            dve.tensor_reduce(sums[:, 0:2], products[:].rearrange("p (a n) -> p a n", a=2), AX, ALU.add).then_inc(*made.step("sums"))
            dve.wait_ge(powers, 1)
            dve.tensor_tensor(sums[:, 0:1], sums[:, 2:3], sums[:, 3:4], ALU.subtract).then_inc(*made.step("difference"))
            dve.wait_ge(made.sem, made.so_far())
            dve.tensor_scalar(C.lam[:], sums[:, 0:1], LAMBDA_INIT, None, ALU.add).then_inc(*made.step("sum"))
            dve.wait_ge(made.sem, made.so_far())

        @block.scalar
        def _(act):
            act.wait_ge(made.sem, made.value("sums"))
            act.activation(sums[:, 2:4], sums[:, 0:2], ACT.Exp).then_inc(powers, 1)


def diff_values(nc, w, hT, v):
    with ExitStack() as ctx:
        S = scope(nc, ctx, "diff_v")
        weights = S.sb("weights", [P, 8, 512])
        product = S.ps("product", [P, 2, 512])
        w_in = S.sem("w_in")
        multiplied = S.steps("multiplied", ["tile"], back=2)
        copied = S.steps("copied", ["tile"], back=2)
        with nc.Block() as block:
            @block.sync
            def _(sp):
                sp.dma_start(weights[:], w.rearrange("(k p) n -> p k n", p=P)).then_inc(w_in, 16)

            @block.tensor
            def _(pe):
                pe.sem_inc(multiplied.sem, multiplied.start)
                pe.wait_ge(w_in, 16)
                for t in range(8):
                    pe.wait_ge(copied.sem, copied.value("tile", t - 2))
                    for k in range(8):
                        ins = pe.matmul(product[:, t % 2, :], hT[:, k, t * P:(t + 1) * P], weights[:, k, :],
                                        start=(k == 0), stop=(k == 7))
                    ins.then_inc(*multiplied.step("tile"))

            @block.scalar
            def _(act):
                act.sem_inc(copied.sem, copied.start)
                for t in range(8):
                    act.wait_ge(multiplied.sem, multiplied.value("tile", t))
                    act.copy(v[:, t, :], product[:, t % 2, :]).then_inc(*copied.step("tile"))
                act.wait_ge(copied.sem, copied.end(8))


def diff_attention(nc, q, k, v, oT, C):
    H, T, B = 4, 1024, 8
    HIDDEN = -1.0e30
    units = [(b, h) for b in range(B) for h in range(H)]
    N = len(units)
    with ExitStack() as ctx:
        S = scope(nc, ctx, "attn")
        bias = S.sb("bias", [P, H, T])
        dist = S.sb("dist", [P, T])
        score = S.sb("score", [P, 2, 2, T])
        flipT = S.sb("flipT", [P, T])
        heads = S.sb("heads", [P, B, 512])
        high = S.sb("high", [P, 2, 2])
        total = S.sb("total", [P, 2, 2])
        weight = S.sb("weight", [P, 2, 2])
        square = S.sb("square", [P, 2, P])
        stat = S.sb("stat", [P, 3 * N])
        sums, mean, rstd = (stat[:, i * N:(i + 1) * N] for i in range(3))
        gain = S.sb("gain", [P, 1])
        scores = S.ps("scores", [P, 2, T])
        flipped = S.ps("flipped", [P, T])
        values = S.ps("values", [P, 2, 512])
        ready = S.steps("ready", ["dist", "masked"])
        biased = S.steps("biased", [f"slope{h}" for h in range(H)])
        scored = S.steps("scored", ["unit"], back=1)
        turned = S.steps("turned", ["unit"], back=1)
        valued = S.steps("valued", ["unit"], back=2)
        softened = S.steps("softened", ["bias0", "bias1", "negate"], back=2)
        softened_mix = S.steps("mixed", ["recip", "lambda", "scale", "mix"], back=2)
        raised = S.steps("raised", ["exp0", "exp1"], back=2)
        copied = S.steps("copied", ["weights", "values", "square"], back=2)
        normed = S.steps("normed", ["gain", "mean", "rstd"])
        rooted = S.sem("rooted")
        scaled = S.steps("scaled", ["block"], back=1)
        crossed = S.steps("crossed", ["block"], back=2)
        stored = S.steps("stored", ["block"], back=2)

        with nc.Block() as block:
            @block.gpsimd
            def _(pool):
                pool.sem_inc(ready.sem, ready.start)
                pool.iota(dist[:], pattern=[[1, T]], base=P - T, channel_multiplier=-1,
                          allow_small_or_imprecise_dtypes=True).then_inc(*ready.step("dist"))
                pool.wait_ge(ready.sem, ready.so_far())
                pool.affine_select(out=dist[:], in_=dist[:], compare_op=ALU.is_ge, fill=HIDDEN * 256,
                                   base=T - P, pattern=[[-1, T]], channel_multiplier=1).then_inc(*ready.step("masked"))
                pool.wait_ge(ready.sem, ready.so_far())

            @block.vector
            def _(dve):
                dve.sem_inc(biased.sem, biased.start)
                dve.sem_inc(softened.sem, softened.start)
                dve.wait_ge(ready.sem, ready.value("masked"))
                for h in range(H):
                    dve.tensor_scalar(bias[:, h, :], dist[:], 2.0 ** (-8.0 * (h + 1) / H), None,
                                      ALU.mult).then_inc(*biased.step(f"slope{h}"))
                dve.wait_ge(biased.sem, biased.so_far())

                def bias_and_max(u):
                    b, h = units[u]
                    n, par = (b + 1) * P, u % 2
                    dve.wait_ge(scored.sem, scored.value("unit", u))
                    softened.round()
                    for c in range(2):
                        if u >= 2 and c == 0:
                            dve.wait_ge(turned.sem, turned.value("unit", u - 2))
                        dve.tensor_tensor_reduce(
                            score[:, par, c, 0:n], scores[:, c, 0:n], bias[:, h, T - n:T], 1.0, -3.0e38,
                            ALU.add, ALU.max, high[:, par, c:c + 1]).then_inc(*softened.step(f"bias{c}"))
                    dve.wait_ge(softened.sem, softened.so_far(u))
                    dve.tensor_scalar(high[:, par, :], high[:, par, :], -1.0, None, ALU.mult).then_inc(*softened.step("negate"))

                def mix(u):
                    b, h = units[u]
                    n, par = (b + 1) * P, u % 2
                    dve.wait_ge(raised.sem, raised.value("exp1", u))
                    dve.reciprocal(weight[:, par, :], total[:, par, :]).then_inc(*softened_mix.step("recip"))
                    dve.wait_ge(softened_mix.sem, softened_mix.so_far(u))
                    dve.tensor_scalar(weight[:, par, 1:2], weight[:, par, 1:2], C.lam[:, 0:1], -1.0,
                                      ALU.mult, ALU.mult).then_inc(*softened_mix.step("lambda"))
                    dve.tensor_scalar(score[:, par, 0, 0:n], score[:, par, 0, 0:n],
                                      weight[:, par, 0:1], None, ALU.mult).then_inc(*softened_mix.step("scale"))
                    dve.wait_ge(softened_mix.sem, softened_mix.so_far(u))
                    dve.scalar_tensor_tensor(score[:, par, 0, 0:n], score[:, par, 1, 0:n],
                                             weight[:, par, 1:2], score[:, par, 0, 0:n],
                                             ALU.mult, ALU.add).then_inc(*softened_mix.step("mix"))
                dve.sem_inc(softened_mix.sem, softened_mix.start)
                for u in range(N + 1):
                    if u < N:
                        bias_and_max(u)
                    if u >= 1:
                        softened_mix.round()
                        mix(u - 1)
                dve.sem_inc(normed.sem, normed.start)
                dve.sem_inc(scaled.sem, scaled.start)
                dve.tensor_scalar(gain[:], C.vector["subln_g"], 1.0 - LAMBDA_INIT, None, ALU.mult).then_inc(*normed.step("gain"))
                dve.wait_ge(copied.sem, copied.end(N))
                dve.tensor_scalar(mean, sums, 1.0 / P, EPS, ALU.mult, ALU.add).then_inc(*normed.step("mean"))
                dve.wait_ge(rooted, 1)
                dve.reciprocal(rstd, mean).then_inc(*normed.step("rstd"))
                dve.wait_ge(normed.sem, normed.so_far())
                for b in range(B):
                    scaled.round()
                    part = heads[:, b, :].rearrange("p (h n) -> p h n", h=H)
                    dve.tensor_tensor(part, part, rstd[:, b * H:(b + 1) * H].unsqueeze(2)
                                      .to_broadcast([P, H, P]), ALU.mult).then_inc(*scaled.step("block"))
                dve.wait_ge(scaled.sem, scaled.end(B))

            @block.scalar
            def _(act):
                act.sem_inc(raised.sem, raised.start)
                act.sem_inc(copied.sem, copied.start)
                act.sem_inc(stored.sem, stored.start)

                def raise_(u):
                    b, h = units[u]
                    n, par = (b + 1) * P, u % 2
                    act.wait_ge(softened.sem, softened.value("negate", u))
                    raised.round()
                    for c in range(2):
                        act.wait_ge(raised.sem, raised.so_far(u))
                        act.activation(score[:, par, c, 0:n], score[:, par, c, 0:n], ACT.Exp,
                                       bias=high[:, par, c:c + 1],
                                       accum_out=total[:, par, c:c + 1]).then_inc(*raised.step(f"exp{c}"))

                def copy_out(u):
                    b, h = units[u]
                    n = (b + 1) * P
                    copied.round()
                    act.wait_ge(turned.sem, turned.value("unit", u))
                    act.wait_ge(valued.sem, valued.value("unit", u - 1))
                    act.copy(flipT[:, 0:n], flipped[:, 0:n]).then_inc(*copied.step("weights"))
                    act.wait_ge(valued.sem, valued.value("unit", u))
                    act.copy(heads[:, b, h * P:(h + 1) * P], values[:, u % 2, 0:P]).then_inc(*copied.step("values"))
                    act.wait_ge(copied.sem, copied.so_far(u))
                    act.activation(square[:, u % 2, :], heads[:, b, h * P:(h + 1) * P], ACT.Square,
                                   accum_out=sums[:, u:u + 1]).then_inc(*copied.step("square"))
                for u in range(N + 1):
                    if u < N:
                        raise_(u)
                    if u >= 1:
                        copy_out(u - 1)
                act.wait_ge(normed.sem, normed.value("mean"))
                act.activation(mean, mean, ACT.Sqrt).then_inc(rooted, 1)
                for b in range(B):
                    act.wait_ge(crossed.sem, crossed.value("block", b))
                    if b == 0:
                        act.wait_ge(normed.sem, normed.value("gain"))
                    act.activation(oT[:, :, b * P:(b + 1) * P],
                                   flipped[:, (b % 2) * 512:(b % 2 + 1) * 512]
                                   .rearrange("p (h n) -> p h n", h=H),
                                   ACT.Copy, scale=gain[:, 0:1]).then_inc(*stored.step("block"))
                act.wait_ge(stored.sem, stored.end(B))

            @block.tensor
            def _(pe):
                pe.sem_inc(scored.sem, scored.start)
                pe.sem_inc(turned.sem, turned.start)
                pe.sem_inc(valued.sem, valued.start)
                pe.sem_inc(crossed.sem, crossed.start)

                def score_unit(u):
                    b, h = units[u]
                    n = (b + 1) * P
                    pe.wait_ge(softened.sem, softened.value("bias1", u - 1))
                    for c in range(2):
                        rows = slice(64 * c, 64 * c + 64)
                        for at in range(0, n, 512):
                            to = min(n, at + 512)
                            ins = pe.matmul(scores[:, c, at:to], q[rows, h, b * P:(b + 1) * P], k[rows, h, at:to],
                                            start=True, stop=True)
                    ins.then_inc(*scored.step("unit"))

                def apply_unit(u):
                    b, h = units[u]
                    pe.wait_ge(softened_mix.sem, softened_mix.value("mix", u))
                    pe.wait_ge(copied.sem, copied.value("weights", u - 1))
                    for j in range(b + 1):
                        ins = pe.transpose(flipped[:, j * P:(j + 1) * P], score[:, u % 2, 0, j * P:(j + 1) * P],
                                           C.ident[:])
                    ins.then_inc(*turned.step("unit"))
                    pe.wait_ge(copied.sem, copied.value("weights", u))
                    pe.wait_ge(copied.sem, copied.value("values", u - 2))
                    for j in range(b + 1):
                        ins = pe.matmul(values[:, u % 2, 0:P], flipT[:, j * P:(j + 1) * P],
                                        v[:, j, h * P:(h + 1) * P], start=(j == 0), stop=(j == b))
                    ins.then_inc(*valued.step("unit"))
                for u in range(N + 1):
                    if u < N:
                        score_unit(u)
                    if u >= 1:
                        apply_unit(u - 1)
                for b in range(B):
                    pe.wait_ge(scaled.sem, scaled.value("block", b))
                    pe.wait_ge(stored.sem, stored.value("block", b - 2))
                    for h in range(H):
                        ins = pe.transpose(flipped[:, (b % 2) * 512 + h * P:(b % 2) * 512 + (h + 1) * P],
                                           heads[:, b, h * P:(h + 1) * P], C.ident[:])
                    ins.then_inc(*crossed.step("block"))


def rwkv_low_rank(nc, I, hT, u, sig, a, gate, C):
    T = 1024
    with ExitStack() as ctx:
        S = scope(nc, ctx, "lora")
        weights = S.sb("weights", [P, 8, 288])
        low = S.sb("low", [P, 3, T])
        up_wa = S.sb("up_wa", [P, 512])
        up_g = S.sb("up_g", [P, 512])
        up_g2 = S.sb("up_g2", [32, 512])
        keep_mu = S.sb("keep_mu", [P, 3])
        product = S.ps("product", [P, 2, T])
        raised = S.ps("raised", [P, 2, T])
        w_in, up_in = S.sem("w_in"), S.sem("up_in")
        kept = S.sem("kept")
        names = ["xwa", "xg", "xg2"]
        multiplied = S.steps("multiplied", names)
        copied = S.steps("copied", names)
        shifted = S.steps("shifted", [f"{n}_{what}" for n in names for what in ("first", "rest")])
        bent = S.steps("bent", names)
        lifted = S.steps("lifted", ["unit"], back=2)
        stored = S.steps("stored", ["unit"], back=2)
        rows = {"xwa": P, "xg": P, "xg2": 32}
        mu = {"xwa": C.vector["mu"][:, 12:13], "xg": C.vector["mu"][:, 13:14], "xg2": C.mu_tail[:]}
        with nc.Block() as block:
            @block.sync
            def _(sp):
                sp.dma_start(weights[:], I["w_in"][0][:, 1536:1824].rearrange("(k p) n -> p k n", p=P)).then_inc(w_in, 16)
                sp.dma_start(up_wa[0:64, :], I["w_decay_up"][0]).then_inc(up_in, 16)
                sp.dma_start(up_wa[64:128, :], I["w_iclr_up"][0]).then_inc(up_in, 16)
                sp.dma_start(up_g[:], I["w_gate_up"][0][0:P, :]).then_inc(up_in, 16)
                sp.dma_start(up_g2[:], I["w_gate_up"][0][P:160, :]).then_inc(up_in, 16)

            @block.tensor
            def _(pe):
                pe.sem_inc(multiplied.sem, multiplied.start)
                pe.sem_inc(lifted.sem, lifted.start)
                pe.wait_ge(w_in, 16)
                for n, name in enumerate(names):
                    if n == 2:
                        pe.wait_ge(shifted.sem, shifted.value("xwa_rest"))
                    for half in range(2):
                        for k in range(8):
                            ins = pe.matmul(product[0:rows[name], n % 2, half * 512:(half + 1) * 512],
                                            weights[:, k, n * P:n * P + rows[name]],
                                            hT[:, k, half * 512:(half + 1) * 512], start=(k == 0), stop=(k == 7))
                    ins.then_inc(*multiplied.step(name))
                pe.wait_ge(up_in, 64)
                pe.wait_ge(bent.sem, bent.value("xg2"))
                for n in range(12):
                    kind, ct = n // 4, n % 4
                    pe.wait_ge(stored.sem, stored.value("unit", n - 2))
                    cols = slice(ct * P, (ct + 1) * P)
                    for half in range(2):
                        to = raised[:, n % 2, half * 512:(half + 1) * 512]
                        at = slice(half * 512, (half + 1) * 512)
                        if kind < 2:
                            part = slice(64 * kind, 64 * kind + 64)
                            ins = pe.matmul(to, up_wa[part, cols], low[part, 0, at], start=True, stop=True)
                        else:
                            pe.matmul(to, up_g[:, cols], low[:, 1, at], start=True, stop=False)
                            ins = pe.matmul(to, up_g2[:, cols], low[0:32, 2, at], start=False, stop=True)
                    ins.then_inc(*lifted.step("unit"))

            @block.scalar
            def _(act):
                act.sem_inc(copied.sem, copied.start)
                act.sem_inc(bent.sem, bent.start)
                act.sem_inc(stored.sem, stored.start)
                act.wait_ge(kept, 2)
                for n, name in enumerate(names):
                    act.wait_ge(multiplied.sem, multiplied.value(name))
                    r = rows[name]
                    act.activation(low[0:r, n, :], product[0:r, n % 2, :], ACT.Copy,
                                   scale=keep_mu[0:r, n:n + 1]).then_inc(*copied.step(name))
                for n, name in enumerate(names):
                    act.wait_ge(shifted.sem, shifted.value(f"{name}_rest"))
                    r = 64 if n == 0 else rows[name]
                    act.activation(low[0:r, n, :], low[0:r, n, :], ACT.Tanh if n == 0 else ACT.Sigmoid).then_inc(*bent.step(name))
                for n in range(12):
                    kind, ct = n // 4, n % 4
                    act.wait_ge(lifted.sem, lifted.value("unit", n))
                    if kind < 2:
                        base = C.vector["w0" if kind == 0 else "a0"][:, ct:ct + 1]
                        ins = act.activation((sig, a)[kind][:, ct, :], raised[:, n % 2, :], ACT.Sigmoid, bias=base)
                    else:
                        ins = act.copy(gate[:, ct, :], raised[:, n % 2, :])
                    ins.then_inc(*stored.step("unit"))
                act.wait_ge(stored.sem, stored.end(12))

            @block.vector
            def _(dve):
                dve.tensor_scalar(keep_mu[:, 0:2], C.vector["mu"][:, 12:14], -1.0, 1.0, ALU.mult, ALU.add).then_inc(kept, 1)
                dve.tensor_scalar(keep_mu[0:32, 2:3], C.mu_tail[:], -1.0, 1.0, ALU.mult, ALU.add).then_inc(kept, 1)
                dve.sem_inc(shifted.sem, shifted.start)
                for n, name in enumerate(names):
                    dve.wait_ge(copied.sem, copied.value(name))
                    r = rows[name]
                    for what, lo, hi in (("first", 1, 512), ("rest", 512, T)):
                        dve.scalar_tensor_tensor(low[0:r, n, lo:hi], product[0:r, n % 2, lo - 1:hi - 1],
                                                 mu[name][0:r, :], low[0:r, n, lo:hi],
                                                 ALU.mult, ALU.add).then_inc(*shifted.step(f"{name}_{what}"))


def rwkv_keys(nc, u, a, sig, kkn, fall, blocks, C):
    T = 1024
    with ExitStack() as ctx:
        S = scope(nc, ctx, "keys")
        square = S.sb("square", [P, 2, T])
        root = S.sb("root", [P, 2, T])
        grow = S.sb("grow", [P, 2, T])
        restart = S.sb("restart", [P, T])
        other = S.sb("other", [P, 4])
        norm = S.ps("norm", [P, 2, T])
        made = S.steps("made", ["ones", "zeros", "other"])
        grown = S.sem("grown")
        squared = S.steps("squared", ["square"], back=2)
        summed = S.steps("summed", ["sum"], back=2)
        rooted = S.steps("rooted", ["root"], back=2)
        keyed = S.steps("keyed", ["scan", "grow", "k", "floor", "inverse", "kkn"])
        with nc.Block() as block:
            @block.scalar
            def _(act):
                act.sem_inc(squared.sem, squared.start)
                act.sem_inc(rooted.sem, rooted.start)
                for c in range(4):
                    if c >= 2:
                        act.wait_ge(summed.sem, summed.value("sum", c - 2))
                    act.activation(square[:, c % 2, :], u[:, 4 + c, :], ACT.Square,
                                   scale=C.vector["k_k"][:, c:c + 1]).then_inc(*squared.step("square"))
                for c in range(4):
                    act.wait_ge(summed.sem, summed.value("sum", c))
                    act.wait_ge(keyed.sem, keyed.value("kkn", c - 2)) if c >= 2 else None
                    act.activation(root[:, c % 2, :], norm[:, c % 2, :], ACT.Sqrt).then_inc(*rooted.step("root"))

            @block.tensor
            def _(pe):
                pe.sem_inc(summed.sem, summed.start)
                for c in range(4):
                    pe.wait_ge(squared.sem, squared.value("square", c))
                    pe.wait_ge(rooted.sem, rooted.value("root", c - 2))
                    for half in range(2):
                        ins = pe.matmul(norm[:, c % 2, half * 512:(half + 1) * 512], blocks[:],
                                        square[:, c % 2, half * 512:(half + 1) * 512], start=True, stop=True)
                    ins.then_inc(*summed.step("sum"))

            @block.vector
            def _(dve):
                dve.sem_inc(made.sem, made.start)
                dve.memset(restart[:], 1.0).then_inc(*made.step("ones"))
                dve.wait_ge(made.sem, made.so_far())
                dve.memset(restart[:].rearrange("p (c n) -> p c n", n=P)[:, :, 0:1], 0.0).then_inc(*made.step("zeros"))
                dve.tensor_scalar(other[:], C.vector["k_a"], -1.0, 1.0, ALU.mult, ALU.add).then_inc(*made.step("other"))
                dve.wait_ge(made.sem, made.so_far())
                dve.sem_inc(keyed.sem, keyed.start)
                for c in range(4):
                    keyed.round()
                    k = u[:, 4 + c, :]
                    dve.tensor_tensor_scan(fall[:, c, :], restart[:], sig[:, c, :], 0.0, ALU.mult, ALU.add).then_inc(*keyed.step("scan"))
                    if c >= 2:
                        dve.wait_ge(grown, c - 1)
                    dve.tensor_scalar(grow[:, c % 2, :], a[:, c, :], C.vector["k_a"][:, c:c + 1],
                                      other[:, c:c + 1], ALU.mult, ALU.add).then_inc(*keyed.step("grow"))
                    dve.wait_ge(keyed.sem, keyed.so_far(c))
                    dve.tensor_scalar(kkn[:, c, :], k, C.vector["k_k"][:, c:c + 1], None, ALU.mult).then_inc(*keyed.step("k"))
                    dve.wait_ge(keyed.sem, keyed.so_far(c))
                    dve.wait_ge(squared.sem, squared.value("square", c))
                    dve.wait_ge(rooted.sem, rooted.value("root", c))
                    dve.tensor_scalar(root[:, c % 2, :], root[:, c % 2, :], 1e-12, None, ALU.max).then_inc(*keyed.step("floor"))
                    dve.wait_ge(keyed.sem, keyed.so_far(c))
                    dve.reciprocal(root[:, c % 2, :], root[:, c % 2, :]).then_inc(*keyed.step("inverse"))
                    dve.wait_ge(keyed.sem, keyed.so_far(c))
                    dve.tensor_tensor(kkn[:, c, :], kkn[:, c, :], root[:, c % 2, :], ALU.mult).then_inc(*keyed.step("kkn"))
                    dve.wait_ge(keyed.sem, keyed.so_far(c))

            @block.gpsimd
            def _(pool):
                for c in range(4):
                    pool.wait_ge(keyed.sem, keyed.value("k", c))
                    pool.wait_ge(squared.sem, squared.value("square", c))
                    pool.tensor_tensor(u[:, 4 + c, :], u[:, 4 + c, :], grow[:, c % 2, :], ALU.mult).then_inc(grown, 1)
                    pool.wait_ge(grown, c + 1)


def rwkv_masks(nc, M):
    corr = M.sb("corr_mask", [P, 4, P], BF16)
    level = M.sb("level_mask", [P, 7, P], BF16)
    blocks = M.sb("head_blocks", [P, P])
    names = ["corr1", "corr2", "corr3", "corr4", "corr5", "zero", "b0", "b1", "b2"]
    made = M.steps("masks_made", names + [f"l{l}_{w}" for l in range(7) for w in ("one", "low", "high")])
    with nc.Block() as block:
        @block.gpsimd
        def _(pool):
            pool.sem_inc(made.sem, made.start)
            pool.memset(corr[:], 1.0).then_inc(*made.step("corr1"))
            for n in range(4):
                pool.wait_ge(made.sem, made.so_far())
                pool.affine_select(out=corr[:, n, :], in_=corr[:, n, :], compare_op=ALU.is_ge, fill=0.0,
                                   base=-1 if n % 2 == 0 else 0, pattern=[[1, P]], channel_multiplier=-1).then_inc(*made.step(f"corr{n + 2}"))
            pool.memset(level[:], 0.0).then_inc(*made.step("zero"))
            pool.memset(blocks[:], 0.0).then_inc(*made.step("b0"))
            pool.wait_ge(made.sem, made.so_far())
            pool.memset(blocks[0:64, 0:64], 1.0).then_inc(*made.step("b1"))
            pool.memset(blocks[64:128, 64:128], 1.0).then_inc(*made.step("b2"))
            for l in range(7):
                m, n = 2 ** l, P // 2 ** (l + 1)
                second = level[:, l, :].rearrange("p (b h r) -> p b h r", h=2, r=m)[:, :, 1, :]
                pool.wait_ge(made.sem, made.so_far())
                pool.memset(second, 1.0).then_inc(*made.step(f"l{l}_one"))
                pool.wait_ge(made.sem, made.so_far())
                pool.affine_select(out=second, in_=second, compare_op=ALU.is_ge, fill=0.0, base=0,
                                   pattern=[[-2 * m, n], [0, m]], channel_multiplier=1).then_inc(*made.step(f"l{l}_low"))
                pool.wait_ge(made.sem, made.so_far())
                pool.affine_select(out=second, in_=second, compare_op=ALU.is_ge, fill=0.0, base=m - 1,
                                   pattern=[[2 * m, n], [0, m]], channel_multiplier=-1).then_inc(*made.step(f"l{l}_high"))
            pool.wait_ge(made.sem, made.so_far())
    return corr, level, blocks


KAPPA = float(np.exp(-0.5))


def rwkv_chunks(nc, u, a, sig, kkn, fall, masks, centred, C):
    corr_mask, level_mask, blocks = masks
    NCH, H, CT = 8, 8, 4
    LEVELS = 7
    with ExitStack() as ctx:
        S = scope(nc, ctx, "chunk")
        early = S.sb("early", [P, 2, CT, P])
        centre, lag = early[:, 0], early[:, 1]
        power = S.sb("power", [P, 3, CT, P])
        ar = S.sb("ar", [P, CT, 2, P])
        kc = S.sb("kc", [P, CT, P])
        bc = S.sb("bc", [P, CT, P])
        vc = S.sb("vc", [P, CT, P])
        rk = power[:, 2]
        edge = S.sb("edge", [P, 8])
        vkb = S.sb("vkb", [P, 3, 512])
        corr = S.sb("corr", [P, H, 4, P])
        part = S.sb("part", [P, H, P])
        inv = S.sb("inv", [P, H, P])
        invT = S.sb("invT", [P, H, P])
        prod = early[:].rearrange("p a c n -> p (a c) n")
        rhs = power[:, 0].rearrange("p c n -> p (c n)")
        sol = power[:, 1].rearrange("p c n -> p (c n)")
        state = S.sb("state", [P, CT, P])
        stat = S.sb("stat", [P, 2, H])
        pairs = S.ps("pairs", [P, 2, 512])
        straight = S.ps("straight", [P, 2, 512])
        crossed = S.ps("crossed", [P, 2, 512])
        mixed = S.ps("mixed", [P, 2, 512])

        groups = range(2)
        level_names = [f"l{l}_{what}{g}" for l in range(1, LEVELS) for what in ("p", "q") for g in groups]
        pe_steps = S.steps("products", ["turn", "bonus"] + [f"corr{h}" for h in range(H)] +
                           ["l0_0", "l0_1", "rhs"] + level_names + ["solve", "state", "y"])
        act_steps = S.steps("act", ["exp_r", "exp_k", "exp_a", "exp_edge", "v", "k", "b", "rhs"] +
                            [f"l{l}_p{g}" for l in range(1, LEVELS) for g in groups] + ["solve", "y"])
        pool_steps = S.steps("pool", ["v"] + [f"part{l}" for l in range(LEVELS)])
        dve_steps = S.steps("vector", ["centre", "lag", "edge_end", "edge_mid", "b0", "r", "k", "b", "a", "rk0", "rk1",
                                       "state_in"] + [f"mask{h}" for h in range(H)] + ["bonus"] +
                            [f"l0_{w}{g}" for g in groups for w in ("t", "s")] +
                            [f"l{l}_{w}{g}" for l in range(1, LEVELS) for g in groups for w in ("s", "t")
                             if not (l == LEVELS - 1 and w == "s")] +
                            ["add0", "add1", "scale0", "scale1", "mean", "mean_scale", "subtract", "square", "var"])
        wiped, held = S.sem("wiped"), S.sem("held")
        wide = [P, CT, P]

        def channel(v):
            return v.unsqueeze(2).to_broadcast(wide)

        with nc.Block() as block:
            @block.gpsimd
            def _(pool):
                pool.sem_inc(pool_steps.sem, pool_steps.start)
                with pool.Fori(0, NCH) as i:
                    now = ds(i * P, P)
                    pool.wait_ge(dve_steps.sem, dve_steps.value("bonus", i - 1))
                    pool.wait_ge(pe_steps.sem, pe_steps.value("turn", i - 1))
                    pool.wait_ge(pool_steps.sem, pool_steps.so_far(i))
                    pool.tensor_copy(vc[:], u[:, 8:12, now]).then_inc(*pool_steps.step("v"))
                    pool.wait_ge(dve_steps.sem, dve_steps.value(f"mask{H - 1}", i))
                    for l in range(LEVELS):
                        if l >= 1:
                            pool.wait_ge(pe_steps.sem, pe_steps.value("l0_1" if l == 1 else f"l{l - 1}_p1", i))
                            if l == 1:
                                pool.wait_ge(dve_steps.sem, dve_steps.value("l0_s1", i))
                        pool.wait_ge(pool_steps.sem, pool_steps.so_far(i))
                        pool.tensor_tensor(
                            part[:], corr[:, :, 0, :],
                            level_mask[:, l, :].unsqueeze(1).to_broadcast([P, H, P]), ALU.mult).then_inc(*pool_steps.step(f"part{l}"))

            @block.scalar
            def _(act):
                act.sem_inc(act_steps.sem, act_steps.start)
                with act.Fori(0, NCH) as i:
                    act.wait_ge(dve_steps.sem, dve_steps.value("lag", i))
                    act.activation(power[:, 0], centre, ACT.Exp, scale=-KAPPA).then_inc(*act_steps.step("exp_r"))
                    act.activation(power[:, 1], centre, ACT.Exp, scale=KAPPA).then_inc(*act_steps.step("exp_k"))
                    act.activation(power[:, 2], lag, ACT.Exp, scale=-KAPPA).then_inc(*act_steps.step("exp_a"))
                    act.wait_ge(dve_steps.sem, dve_steps.value("edge_mid", i))
                    act.activation(edge[:], edge[:], ACT.Exp, scale=-KAPPA).then_inc(*act_steps.step("exp_edge"))
                    act.wait_ge(pe_steps.sem, pe_steps.value("turn", i))
                    for n, (name, source) in enumerate((("v", straight[:, 0, :]), ("k", straight[:, 1, :]),
                                                        ("b", crossed[:, 0, :]))):
                        act.copy(vkb[:, n, :], source).then_inc(*act_steps.step(name))
                    act.wait_ge(pe_steps.sem, pe_steps.value("rhs", i))
                    act.copy(rhs, mixed[:, 0, :]).then_inc(*act_steps.step("rhs"))
                    for l in range(1, LEVELS):
                        for g in groups:
                            act.wait_ge(pe_steps.sem, pe_steps.value(f"l{l}_p{g}", i))
                            act.copy(prod[:, g * 4:g * 4 + 4, :],
                                     pairs[:, g, :].rearrange("p (h n) -> p h n", n=P)).then_inc(*act_steps.step(f"l{l}_p{g}"))
                    act.wait_ge(pe_steps.sem, pe_steps.value("solve", i))
                    act.copy(sol, mixed[:, 1, :]).then_inc(*act_steps.step("solve"))
                    act.wait_ge(pe_steps.sem, pe_steps.value("y", i))
                    act.copy(centred[:, :, ds(i * P, P)],
                             mixed[:, 0, :].rearrange("p (c n) -> p c n", n=P)).then_inc(*act_steps.step("y"))
                act.wait_ge(act_steps.sem, act_steps.end(NCH))

            @block.vector
            def _(dve):
                dve.sem_inc(dve_steps.sem, dve_steps.start)
                dve.memset(state[:], 0.0).then_inc(wiped, 1)
                dve.wait_ge(wiped, 1)
                with dve.Fori(0, NCH) as i:
                    now = ds(i * P, P)
                    mid = ds(i * P + 63, 1)
                    L, sg = fall[:, :, now], sig[:, :, now]
                    r, k, av, kk = u[:, 0:4, now], u[:, 4:8, now], a[:, :, now], kkn[:, :, now]
                    dve.wait_ge(dve_steps.sem, dve_steps.so_far(i))
                    dve.tensor_tensor(centre, L, fall[:, :, mid].to_broadcast(wide), ALU.subtract).then_inc(*dve_steps.step("centre"))
                    dve.wait_ge(dve_steps.sem, dve_steps.so_far(i))
                    dve.tensor_tensor(lag, centre, sg, ALU.subtract).then_inc(*dve_steps.step("lag"))
                    dve.tensor_copy(edge[:, 0:4], centre[:, :, P - 1:P].rearrange("p c a -> p (c a)")).then_inc(*dve_steps.step("edge_end"))
                    dve.tensor_copy(edge[:, 4:8], fall[:, :, mid].rearrange("p c a -> p (c a)")).then_inc(*dve_steps.step("edge_mid"))
                    dve.wait_ge(pe_steps.sem, pe_steps.value("y", i - 1))
                    dve.tensor_tensor(bc[:], kk, av, ALU.mult).then_inc(*dve_steps.step("b0"))
                    dve.wait_ge(act_steps.sem, act_steps.value("exp_edge", i))
                    dve.tensor_tensor(ar[:, :, 1, :], r, power[:, 0], ALU.mult).then_inc(*dve_steps.step("r"))
                    dve.tensor_tensor(kc[:], k, power[:, 1], ALU.mult).then_inc(*dve_steps.step("k"))
                    dve.wait_ge(dve_steps.sem, dve_steps.so_far(i))
                    dve.tensor_tensor(bc[:], bc[:], power[:, 1], ALU.mult).then_inc(*dve_steps.step("b"))
                    dve.scalar_tensor_tensor(ar[:, :, 0, :], kk, -1.0, power[:, 2], ALU.mult, ALU.mult).then_inc(*dve_steps.step("a"))
                    dve.wait_ge(dve_steps.sem, dve_steps.so_far(i))
                    dve.tensor_tensor(rk, r, k, ALU.mult).then_inc(*dve_steps.step("rk0"))
                    dve.wait_ge(dve_steps.sem, dve_steps.so_far(i))
                    dve.tensor_tensor(rk, rk, channel(C.vector["r_k"]), ALU.mult).then_inc(*dve_steps.step("rk1"))
                    dve.tensor_tensor(state[:], state[:], channel(edge[:, 4:8]), ALU.mult).then_inc(*dve_steps.step("state_in"))
                    for h in range(H):
                        dve.wait_ge(pe_steps.sem, pe_steps.value(f"corr{h}", i))
                        dve.tensor_tensor(corr[:, h], pairs[:, h % 2, :].rearrange("p (c n) -> p c n", n=P),
                                          corr_mask[:], ALU.mult).then_inc(*dve_steps.step(f"mask{h}"))
                    dve.wait_ge(pe_steps.sem, pe_steps.value("bonus", i))
                    dve.tensor_tensor(r, crossed[:, 1, :].rearrange("p (c n) -> p c n", n=P), vc[:],
                                      ALU.mult).then_inc(*dve_steps.step("bonus"))
                    eye = C.ident[:].unsqueeze(1).to_broadcast([P, 4, P])

                    def four(x, g):
                        return x[:, g * 4:g * 4 + 4, :]

                    def bank(x, g):
                        return x[:, g, :].rearrange("p (h n) -> p h n", n=P)
                    dve.wait_ge(pool_steps.sem, pool_steps.value("part0", i))
                    for g in groups:
                        dve.tensor_tensor(four(invT, g), four(part[:], g), eye, ALU.add).then_inc(*dve_steps.step(f"l0_t{g}"))
                        dve.wait_ge(pe_steps.sem, pe_steps.value(f"l0_{g}", i))
                        dve.tensor_tensor(four(inv, g), bank(straight, g), eye, ALU.add).then_inc(*dve_steps.step(f"l0_s{g}"))
                    for l in range(1, LEVELS):
                        for g in groups:
                            dve.wait_ge(pe_steps.sem, pe_steps.value(f"l{l}_q{g}", i))
                            if g == 0:
                                dve.wait_ge(dve_steps.sem, dve_steps.so_far(i))
                            if l < LEVELS - 1:
                                dve.tensor_tensor(four(inv, g), four(inv, g), bank(straight, g), ALU.add).then_inc(*dve_steps.step(f"l{l}_s{g}"))
                            dve.tensor_tensor(four(invT, g), four(invT, g), bank(crossed, g), ALU.add).then_inc(*dve_steps.step(f"l{l}_t{g}"))
                    dve.wait_ge(pe_steps.sem, pe_steps.value("state", i))
                    halves = [slice(0, 64), slice(64, 128)]
                    for n, part_ in enumerate(halves):
                        to = state[part_, :, part_]
                        dve.tensor_tensor(to, to, bank(pairs, 0)[part_, :, part_], ALU.add).then_inc(*dve_steps.step(f"add{n}"))
                    dve.wait_ge(dve_steps.sem, dve_steps.so_far(i))
                    for n, part_ in enumerate(halves):
                        to = state[part_, :, part_]
                        dve.tensor_tensor(to, to, edge[part_, 0:4].unsqueeze(2).to_broadcast([64, 4, 64]),
                                          ALU.mult).then_inc(*dve_steps.step(f"scale{n}"))
                    dve.wait_ge(act_steps.sem, act_steps.value("y", i))
                    dve.sem_inc(held, 1)
                    y = centred[:, :, now].rearrange("p c (h n) -> p c h n", n=64)
                    mean = stat[:, 0, :].rearrange("p (c h) -> p c h", h=2)
                    dve.tensor_reduce(mean, y, AX, ALU.add).then_inc(*dve_steps.step("mean"))
                    dve.wait_ge(dve_steps.sem, dve_steps.so_far(i))
                    dve.tensor_scalar(stat[:, 0, :], stat[:, 0, :], 1.0 / 64, None, ALU.mult).then_inc(*dve_steps.step("mean_scale"))
                    dve.wait_ge(dve_steps.sem, dve_steps.so_far(i))
                    dve.tensor_tensor(y, y, mean.unsqueeze(3).to_broadcast([P, 4, 2, 64]), ALU.subtract).then_inc(*dve_steps.step("subtract"))
                    dve.wait_ge(dve_steps.sem, dve_steps.so_far(i))
                    dve.tensor_tensor(rk, centred[:, :, now], centred[:, :, now], ALU.mult).then_inc(*dve_steps.step("square"))
                    dve.wait_ge(dve_steps.sem, dve_steps.so_far(i))
                    dve.sem_inc(held, 1)
                    dve.tensor_reduce(C.variance[:, ds(i * H, H)].rearrange("p (c h) -> p c h", h=2),
                                      rk.rearrange("p c (h n) -> p c h n", n=64), AX, ALU.add).then_inc(*dve_steps.step("var"))
                dve.wait_ge(dve_steps.sem, dve_steps.end(NCH))

            @block.tensor
            def _(pe):
                pe.sem_inc(pe_steps.sem, pe_steps.start)
                with pe.Fori(0, NCH) as i:
                    pe.wait_ge(dve_steps.sem, dve_steps.value("state_in", i))
                    pe.wait_ge(pool_steps.sem, pool_steps.value("v", i))
                    for to, source in ((straight[:, 0, :], vc), (straight[:, 1, :], kc), (crossed[:, 0, :], bc)):
                        for c in range(CT):
                            ins = pe.transpose(to[:, c * P:(c + 1) * P], source[:, c, :], C.ident[:])
                    ins.then_inc(*pe_steps.step("turn"))
                    pe.matmul(crossed[:, 1, :], blocks[:], rk.rearrange("p c n -> p (c n)"),
                              start=True, stop=True).then_inc(*pe_steps.step("bonus"))
                    for h in range(H):
                        rows, c = slice(64 * (h % 2), 64 * (h % 2) + 64), h // 2
                        if h >= 2:
                            pe.wait_ge(dve_steps.sem, dve_steps.value(f"mask{h - 2}", i))
                        both = ar[rows, c, :, :].rearrange("p a n -> p (a n)")
                        pe.matmul(pairs[:, h % 2, 0:256], bc[rows, c, :], both, start=True, stop=False, skip_group_check=True)
                        pe.matmul(pairs[:, h % 2, 256:512], kc[rows, c, :], both, start=False, stop=True,
                                  skip_group_check=True).then_inc(*pe_steps.step(f"corr{h}"))
                    pe.wait_ge(act_steps.sem, act_steps.value("b", i))
                    pe.wait_ge(pool_steps.sem, pool_steps.value("part0", i))
                    for g in groups:
                        for j in range(4):
                            ins = pe.matmul(straight[:, g, j * P:(j + 1) * P], part[:, g * 4 + j, :], C.ident[:],
                                            start=(j == 0), stop=(j == 3), skip_group_check=True)
                        ins.then_inc(*pe_steps.step(f"l0_{g}"))
                    for c in range(CT):
                        pe.matmul(mixed[:, 0, c * P:(c + 1) * P], ar[:, c, 0, :], state[:, c, :], start=(c == 0),
                                  stop=False, skip_group_check=True)
                    for h in range(H):
                        ins = pe.matmul(mixed[:, 0, h * 64:(h + 1) * 64], corr[:, h, 2, :], vkb[:, 0, h * 64:(h + 1) * 64],
                                        start=False, stop=(h == H - 1), skip_group_check=True)
                    ins.then_inc(*pe_steps.step("rhs"))
                    for l in range(1, LEVELS):
                        pe.wait_ge(pool_steps.sem, pool_steps.value(f"part{l}", i))
                        for g in groups:
                            pe.wait_ge(dve_steps.sem, dve_steps.value(f"l{l - 1}_s{g}", i))
                            for j in range(4):
                                h = g * 4 + j
                                ins = pe.matmul(pairs[:, g, j * P:(j + 1) * P], part[:, h, :], inv[:, h, :],
                                                start=(j == 0), stop=(j == 3), skip_group_check=True)
                            ins.then_inc(*pe_steps.step(f"l{l}_p{g}"))
                        for g in groups:
                            pe.wait_ge(act_steps.sem, act_steps.value(f"l{l}_p{g}", i))
                            pe.wait_ge(dve_steps.sem, dve_steps.value(f"l{l - 1}_t{g}", i))
                            if l < LEVELS - 1:
                                for j in range(4):
                                    h = g * 4 + j
                                    pe.matmul(straight[:, g, j * P:(j + 1) * P], invT[:, h, :], prod[:, h, :],
                                              start=(j == 0), stop=(j == 3), skip_group_check=True)
                            for j in range(4):
                                h = g * 4 + j
                                ins = pe.matmul(crossed[:, g, j * P:(j + 1) * P], prod[:, h, :], invT[:, h, :],
                                                start=(j == 0), stop=(j == 3), skip_group_check=True)
                            ins.then_inc(*pe_steps.step(f"l{l}_q{g}"))
                    pe.wait_ge(act_steps.sem, act_steps.value("rhs", i))
                    pe.wait_ge(dve_steps.sem, dve_steps.value(f"l{LEVELS - 1}_t1", i))
                    for h in range(H):
                        cols = slice(h * 64, (h + 1) * 64)
                        ins = pe.matmul(mixed[:, 1, cols], invT[:, h, :], rhs[:, cols], start=(h == 0), stop=(h == H - 1),
                                        skip_group_check=True)
                    ins.then_inc(*pe_steps.step("solve"))
                    for c in range(CT):
                        cols = slice(c * P, (c + 1) * P)
                        pe.matmul(pairs[:, 0, cols], vkb[:, 1, cols], vkb[:, 0, cols], start=(c == 0), stop=False,
                                  skip_group_check=True)
                    for c in range(CT):
                        pe.matmul(mixed[:, 0, c * P:(c + 1) * P], ar[:, c, 1, :], state[:, c, :], start=(c == 0),
                                  stop=False, skip_group_check=True)
                    for h in range(H):
                        cols = slice(h * 64, (h + 1) * 64)
                        pe.matmul(mixed[:, 0, cols], corr[:, h, 3, :], vkb[:, 0, cols], start=False, stop=False,
                                  skip_group_check=True)
                    pe.wait_ge(act_steps.sem, act_steps.value("solve", i))
                    for c in range(CT):
                        cols = slice(c * P, (c + 1) * P)
                        ins = pe.matmul(pairs[:, 0, cols], vkb[:, 2, cols], sol[:, cols], start=False, stop=(c == CT - 1),
                                        skip_group_check=True)
                    ins.then_inc(*pe_steps.step("state"))
                    for h in range(H):
                        cols = slice(h * 64, (h + 1) * 64)
                        ins = pe.matmul(mixed[:, 0, cols], corr[:, h, 1, :], sol[:, cols], start=False,
                                        stop=(h == H - 1), skip_group_check=True)
                    ins.then_inc(*pe_steps.step("y"))


def rwkv_outputs(nc, centred, bonus, gate, C):
    with ExitStack() as ctx:
        S = scope(nc, ctx, "routs")
        rstd = S.sb("rstd", [P, 64])
        rows = S.sb("rows", [P, 2, 512])
        cols = S.sb("cols", [P, 2, 4, P])
        flipped = S.ps("flipped", [P, 2, 512])
        pair = ["even", "odd"]
        stats = S.steps("stats", ["var", "rstd"])
        rooted = S.sem("rooted")
        scaled = S.steps("scaled", pair)
        turned = S.steps("turned", pair)
        gained = S.steps("gained", [f"{j}{c}" for j in pair for c in range(4)])
        gated = S.steps("gated", [j + w for j in pair for w in ("_add", "_gate")])
        with nc.Block() as block:
            @block.vector
            def _(dve):
                dve.sem_inc(stats.sem, stats.start)
                dve.sem_inc(scaled.sem, scaled.start)
                dve.sem_inc(gated.sem, gated.start)
                dve.tensor_scalar(C.variance[:], C.variance[:], 1.0 / 64, 64e-5, ALU.mult, ALU.add).then_inc(*stats.step("var"))
                dve.wait_ge(rooted, 1)
                dve.reciprocal(rstd[:], C.variance[:]).then_inc(*stats.step("rstd"))
                dve.wait_ge(stats.sem, stats.so_far())
                with dve.Fori(0, 4) as i:
                    for j in range(2):
                        t = 2 * i + j
                        dve.wait_ge(turned.sem, turned.value(pair[j], i - 1))
                        dve.tensor_tensor(
                            rows[:, j, :].rearrange("p (c h n) -> p c h n", h=2, n=64),
                            centred[:, :, ds(t * P, P)].rearrange("p c (h n) -> p c h n", n=64),
                            rstd[:, ds(t * 8, 8)].rearrange("p (c h) -> p c h", h=2).unsqueeze(3).to_broadcast([P, 4, 2, 64]),
                            ALU.mult).then_inc(*scaled.step(pair[j]))
                    for j in range(2):
                        now = ds((2 * i + j) * P, P)
                        dve.wait_ge(gained.sem, gained.value(f"{pair[j]}3", i))
                        dve.tensor_tensor(cols[:, j], cols[:, j], bonus[:, :, now], ALU.add).then_inc(*gated.step(pair[j] + "_add"))
                        dve.wait_ge(gated.sem, gated.so_far(i))
                        dve.tensor_tensor(gate[:, :, now], cols[:, j], gate[:, :, now], ALU.mult).then_inc(*gated.step(pair[j] + "_gate"))
                dve.wait_ge(gated.sem, gated.end(4))

            @block.scalar
            def _(act):
                act.sem_inc(gained.sem, gained.start)
                act.wait_ge(stats.sem, stats.value("var"))
                act.activation(C.variance[:], C.variance[:], ACT.Sqrt).then_inc(rooted, 1)
                with act.Fori(0, 4) as i:
                    for j in range(2):
                        act.wait_ge(turned.sem, turned.value(pair[j], i))
                        act.wait_ge(gated.sem, gated.value(pair[j] + "_gate", i - 1))
                        for c in range(4):
                            act.activation(cols[:, j, c, :], flipped[:, j, c * P:(c + 1) * P], ACT.Identity,
                                           bias=C.vector["lnx_b"][:, c:c + 1],
                                           scale=C.vector["lnx_g"][:, c:c + 1]).then_inc(*gained.step(f"{pair[j]}{c}"))

            @block.tensor
            def _(pe):
                pe.sem_inc(turned.sem, turned.start)
                with pe.Fori(0, 4) as i:
                    for j in range(2):
                        pe.wait_ge(scaled.sem, scaled.value(pair[j], i))
                        pe.wait_ge(gained.sem, gained.value(f"{pair[j]}3", i - 1))
                        for c in range(4):
                            ins = pe.transpose(flipped[:, j, c * P:(c + 1) * P], rows[:, j, c * P:(c + 1) * P], C.ident[:])
                        ins.then_inc(*turned.step(pair[j]))


def add_projection(nc, name, lhs, w, x, load=None):
    D = 1024
    with ExitStack() as ctx:
        S = scope(nc, ctx, name)
        weights = S.sb("weights", [P, 8, D])
        product = S.ps("product", [P, 3, D])
        w_in = [S.sem(f"w_in{j}") for j in range(2)]
        x_in = S.sem("x_in")
        multiplied = S.steps("multiplied", ["tile"], back=3)
        added = S.steps("added", ["tile"], back=3)
        with nc.Block() as block:
            @block.sync
            def _(sp):
                for j in range(2):
                    sp.dma_start(weights[:, 4 * j:4 * j + 4, :], w[j * 512:(j + 1) * 512, :]
                                 .rearrange("(k p) n -> p k n", p=P)).then_inc(w_in[j], 16)
                if load is not None:
                    sp.dma_start(x[:].rearrange("p (t n) -> p t n", n=D),
                                 load.rearrange("(t p) n -> p t n", p=P)).then_inc(x_in, 16)

            @block.tensor
            def _(pe):
                pe.sem_inc(multiplied.sem, multiplied.start)
                for t in range(8):
                    pe.wait_ge(added.sem, added.value("tile", t - 3))
                    for half in range(2):
                        for k in range(8):
                            if t == 0 and half == 0 and k % 4 == 0:
                                pe.wait_ge(w_in[k // 4], 16)
                            ins = pe.matmul(product[:, t % 3, half * 512:(half + 1) * 512], lhs[:, k, t * P:(t + 1) * P],
                                            weights[:, k, half * 512:(half + 1) * 512], start=(k == 0), stop=(k == 7))
                    ins.then_inc(*multiplied.step("tile"))

            @block.vector
            def _(dve):
                dve.sem_inc(added.sem, added.start)
                if load is not None:
                    dve.wait_ge(x_in, 16)
                for t in range(8):
                    dve.wait_ge(multiplied.sem, multiplied.value("tile", t))
                    rows = x[:, t * D:(t + 1) * D]
                    dve.tensor_tensor(rows, rows, product[:, t % 3, :], ALU.add).then_inc(*added.step("tile"))
                dve.wait_ge(added.sem, added.end(8))


def cross_keys_values(nc, w, memT, kT, v):
    with ExitStack() as ctx:
        S = scope(nc, ctx, "ckv")
        weights = S.sb("weights", [P, 2, 8, 512])
        product = S.ps("product", [P, 2, 512])
        w_in = [S.sem(f"w_in{j}") for j in range(2)]
        parts = [("k", n) for n in range(4)] + [("v", n) for n in range(4)]
        multiplied = S.steps("multiplied", ["part"], back=2)
        copied = S.steps("copied", ["part"], back=2)
        with nc.Block() as block:
            @block.sync
            def _(sp):
                for j in range(4):
                    if j >= 2:
                        sp.wait_ge(multiplied.sem, multiplied.value("part", 2 * (j - 2) + 1))
                    sp.dma_start(weights[:, j % 2], w[:, j * 512:(j + 1) * 512]
                                 .rearrange("(k p) n -> p k n", p=P)).then_inc(w_in[j % 2], 16)

            @block.tensor
            def _(pe):
                pe.sem_inc(multiplied.sem, multiplied.start)
                for n, (kind, m) in enumerate(parts):
                    slot = (n // 2) % 2
                    if n % 2 == 0:
                        pe.wait_ge(w_in[slot], 16 * (n // 4 + 1))
                    pe.wait_ge(copied.sem, copied.value("part", n - 2))
                    for c in range(2 if kind == "k" else 1):
                        for k in range(8):
                            if kind == "k":
                                col = (2 * m + c) % 4 * P
                                ins = pe.matmul(product[:, n % 2, c * 256:(c + 1) * 256],
                                                weights[:, slot, k, col:col + P], memT[:, k, :],
                                                start=(k == 0), stop=(k == 7))
                            else:
                                ins = pe.matmul(product[:, n % 2, :], memT[:, k, (m % 2) * P:(m % 2 + 1) * P],
                                                weights[:, slot, k, :], start=(k == 0), stop=(k == 7))
                    ins.then_inc(*multiplied.step("part"))

            @block.scalar
            def _(act):
                act.sem_inc(copied.sem, copied.start)
                for n, (kind, m) in enumerate(parts):
                    act.wait_ge(multiplied.sem, multiplied.value("part", n))
                    to = (kT[:, 2 * m:2 * m + 2, :].rearrange("p c n -> p (c n)") if kind == "k"
                          else v[:, m % 2, (m // 2) * 512:(m // 2 + 1) * 512])
                    act.copy(to, product[:, n % 2, :]).then_inc(*copied.step("part"))
                act.wait_ge(copied.sem, copied.end(len(parts)))


def cross_attention(nc, qT, kT, v, oT, C):
    H, M = 4, 256
    with ExitStack() as ctx:
        S = scope(nc, ctx, "cross")
        prob = S.sb("prob", [P, 2, H * M])
        probT = S.sb("probT", [P, 2 * H, P])
        high = S.sb("high", [P, 2, H])
        total = S.sb("total", [P, 2, H])
        scores = S.ps("scores", [P, 2, H * M])
        flipped = S.ps("flipped", [P, 2 * H, P])
        mixed = S.ps("mixed", [P, 8, P])
        scored = S.steps("scored", ["tile"])
        turned = S.steps("turned", ["tile"])
        valued = S.steps("valued", ["tile"])
        topped = S.steps("topped", ["max", "negate"], back=2)
        raised = S.steps("raised", [f"exp{h}" for h in range(H)], back=2)
        divided = S.steps("divided", ["reciprocal", "divide"], back=2)
        copied = S.steps("copied", ["weights"])
        stored = S.steps("stored", ["tile"])
        with nc.Block() as block:
            @block.tensor
            def _(pe):
                for s in (scored, turned, valued):
                    pe.sem_inc(s.sem, s.start)

                def score(t):
                    pe.wait_ge(raised.sem, raised.value(f"exp{H - 1}", t - 2))
                    for h in range(H):
                        for c in range(2):
                            ins = pe.matmul(scores[:, t % 2, h * M:(h + 1) * M], qT[:, 2 * h + c, t * P:(t + 1) * P],
                                            kT[:, 2 * h + c, :], start=(c == 0), stop=(c == 1))
                    ins.then_inc(*scored.step("tile"))

                def apply(t):
                    pe.wait_ge(divided.sem, divided.value("divide", t))
                    pe.wait_ge(copied.sem, copied.value("weights", t - 1))
                    for n in range(2 * H):
                        ins = pe.transpose(flipped[:, n, :], prob[:, t % 2, n * P:(n + 1) * P], C.ident[:])
                    ins.then_inc(*turned.step("tile"))
                    pe.wait_ge(copied.sem, copied.value("weights", t))
                    pe.wait_ge(stored.sem, stored.value("tile", t - 1))
                    for n in range(8):
                        for m in range(2):
                            ins = pe.matmul(mixed[:, n, :], v[:, m, n * P:(n + 1) * P], probT[:, n // 2 * 2 + m, :],
                                            start=(m == 0), stop=(m == 1))
                    ins.then_inc(*valued.step("tile"))
                for t in range(9):
                    if t < 8:
                        score(t)
                    if t >= 1:
                        apply(t - 1)

            @block.vector
            def _(dve):
                for s in (topped, divided, stored):
                    dve.sem_inc(s.sem, s.start)

                def top(t):
                    dve.wait_ge(scored.sem, scored.value("tile", t))
                    topped.round()
                    dve.wait_ge(raised.sem, raised.value(f"exp{H - 1}", t - 2))
                    dve.wait_ge(topped.sem, topped.so_far(t))
                    dve.tensor_reduce(high[:, t % 2, :], scores[:, t % 2, :].rearrange("p (h m) -> p h m", h=H),
                                      AX, ALU.max).then_inc(*topped.step("max"))
                    dve.wait_ge(topped.sem, topped.so_far(t))
                    dve.tensor_scalar(high[:, t % 2, :], high[:, t % 2, :], -1.0, None, ALU.mult).then_inc(*topped.step("negate"))

                def divide(t):
                    dve.wait_ge(raised.sem, raised.value(f"exp{H - 1}", t))
                    divided.round()
                    dve.reciprocal(total[:, t % 2, :], total[:, t % 2, :]).then_inc(*divided.step("reciprocal"))
                    dve.wait_ge(divided.sem, divided.so_far(t))
                    part = prob[:, t % 2, :].rearrange("p (h m) -> p h m", h=H)
                    dve.tensor_tensor(part, part, total[:, t % 2, :].unsqueeze(2).to_broadcast([P, H, M]),
                                      ALU.mult).then_inc(*divided.step("divide"))

                def store(t):
                    dve.wait_ge(valued.sem, valued.value("tile", t))
                    dve.tensor_copy(oT[:, :, t * P:(t + 1) * P], mixed[:]).then_inc(*stored.step("tile"))
                for t in range(9):
                    if t < 8:
                        top(t)
                    if t >= 2:
                        store(t - 2)
                    if t >= 1:
                        divide(t - 1)
                store(7)
                dve.wait_ge(stored.sem, stored.end(8))

            @block.scalar
            def _(act):
                act.sem_inc(raised.sem, raised.start)
                act.sem_inc(copied.sem, copied.start)
                for t in range(9):
                    if t < 8:
                        act.wait_ge(topped.sem, topped.value("negate", t))
                        act.wait_ge(turned.sem, turned.value("tile", t - 2)) if t >= 2 else None
                        act.wait_ge(divided.sem, divided.value("divide", t - 2))
                        for h in range(H):
                            cols = slice(h * M, (h + 1) * M)
                            act.activation(prob[:, t % 2, cols], scores[:, t % 2, cols], ACT.Exp,
                                           bias=high[:, t % 2, h:h + 1],
                                           accum_out=total[:, t % 2, h:h + 1]).then_inc(*raised.step(f"exp{h}"))
                    if t >= 1:
                        act.wait_ge(turned.sem, turned.value("tile", t - 1))
                        act.wait_ge(valued.sem, valued.value("tile", t - 2))
                        act.copy(probT[:], flipped[:]).then_inc(*copied.step("weights"))


NE, TOPK, T_ALL, F_ALL = 32, 4, 1024, 1024


def route(nc, I, hT, row_token, R, C):
    TT = 8
    with ExitStack() as ctx:
        S = scope(nc, ctx, "route")
        weights = S.sb("weights", [P, 8, NE])
        base = S.sb("base", [P, NE])
        logits = S.sb("logits", [P, TT, NE])
        best = S.sb("best", [P, TT, 8])
        index = S.sb("index", [P, TT, 8], U32)
        index_f = S.sb("index_f", [P, TT, TOPK])
        number = S.sb("number", [P, NE])
        region = S.sb("region", [P, NE])
        chosen = S.sb("chosen", [P, TT, TOPK, NE])
        member = S.sb("member", [P, TT, NE])
        before = S.sb("before", [P, TT + 1, NE])
        earlier = S.sb("earlier", [P, P])
        ones = S.sb("ones", [P, P])
        rank = S.sb("rank", [P, TT, NE])
        place = S.sb("place", [P, TT, NE])
        spot = S.sb("spot", [P, TT, TOPK, NE])
        dest = S.sb("dest", [P, TT * TOPK])
        dest_i = S.sb("dest_i", [P, TT * TOPK], I32)
        token = S.sb("token", [P, TT], I32)
        zeros = S.sb("zeros", [P, NE * T_ALL // P], I32)
        blocks = S.sb("blocks", [P, NE])
        blocks_i = S.sb("blocks_i", [P, NE], I32)
        first = S.sb("first", [P, NE + 2])
        lead = S.sb("lead", [P, TT])
        total = S.sb("total", [P, TT])
        product = S.ps("product", [P, TT * NE])
        counted = S.ps("counted", [P, 2, 512])
        w_in, base_in, cleared, scattered = S.sem("w_in"), S.sem("base_in"), S.sem("cleared"), S.sem("scattered")
        made = S.steps("made", ["zeros", "number", "region", "token", "ones", "earlier", "triangle"])
        multiplied = S.steps("multiplied", ["logits", "rank", "count"])
        raised = S.sem("raised")
        names = (["logits"] + [f"{w}{t}" for t in range(TT) for w in ("best", "index")] +
                 ["float", "lead", "chosen", "member", "none"] + [f"before{t}" for t in range(TT)] +
                 ["rank", "place", "spot", "dest", "dest_i", "gate_sum", "gate_inverse", "gate",
                  "round", "int", "least", "zero", "scan", "unused", "first", "start", "row", "spot2", "dest2", "dest2_i"])
        sorted_ = S.steps("sorted", names)
        with nc.Block() as block:
            @block.gpsimd
            def _(pool):
                pool.sem_inc(made.sem, made.start)
                pool.memset(zeros[:], 0).then_inc(*made.step("zeros"))
                pool.wait_ge(made.sem, made.so_far())
                pool.iota(number[:], pattern=[[1, NE]], base=0, channel_multiplier=0,
                          allow_small_or_imprecise_dtypes=True).then_inc(*made.step("number"))
                pool.wait_ge(made.sem, made.so_far())
                pool.iota(region[:], pattern=[[T_ALL, NE]], base=0, channel_multiplier=0,
                          allow_small_or_imprecise_dtypes=True).then_inc(*made.step("region"))
                pool.wait_ge(made.sem, made.so_far())
                pool.iota(token[:], pattern=[[P, TT]], base=0, channel_multiplier=1).then_inc(*made.step("token"))
                pool.wait_ge(made.sem, made.so_far())
                pool.memset(ones[:], 1.0).then_inc(*made.step("ones"))
                pool.wait_ge(made.sem, made.so_far())
                pool.memset(earlier[:], 1.0).then_inc(*made.step("earlier"))
                pool.wait_ge(made.sem, made.so_far())
                pool.affine_select(out=earlier[:], in_=earlier[:], compare_op=ALU.is_ge, fill=0.0,
                                   base=-1, pattern=[[1, P]], channel_multiplier=-1).then_inc(*made.step("triangle"))
                pool.wait_ge(cleared, 16)
                pool.wait_ge(sorted_.sem, sorted_.value("dest_i"))
                for n in range(TT * TOPK):
                    pool.indirect_dma_start(row_token, bass.IndirectOffsetOnAxis(ap=dest_i[:, n:n + 1], axis=0),
                                            token[:, n // TOPK:n // TOPK + 1], None).then_inc(scattered, 16)
                pool.wait_ge(scattered, 16 * TT * TOPK)

            @block.sync
            def _(sp):
                sp.dma_start(weights[:], I["w_router"][0].rearrange("(k p) n -> p k n", p=P)).then_inc(w_in, 16)
                sp.dma_start(base[:], row_to_all(I["b_router"][0])).then_inc(base_in, 16)
                sp.wait_ge(made.sem, made.value("zeros"))
                sp.dma_start(row_token.rearrange("(p n) a -> p (n a)", p=P), zeros[:]).then_inc(cleared, 16)

            @block.tensor
            def _(pe):
                pe.sem_inc(multiplied.sem, multiplied.start)
                pe.wait_ge(w_in, 16)
                for t in range(TT):
                    for k in range(8):
                        ins = pe.matmul(product[:, t * NE:(t + 1) * NE], hT[:, k, t * P:(t + 1) * P], weights[:, k, :],
                                        start=(k == 0), stop=(k == 7))
                ins.then_inc(*multiplied.step("logits"))
                pe.wait_ge(sorted_.sem, sorted_.value(f"before{TT - 1}"))
                pe.wait_ge(made.sem, made.value("triangle"))
                pe.matmul(counted[:, 0, 0:TT * NE], earlier[:], member[:].rearrange("p t e -> p (t e)"), start=True, stop=False)
                pe.matmul(counted[:, 0, 0:TT * NE], ones[:],
                          before[:, 0:TT, :].rearrange("p t e -> p (t e)"), start=False, stop=True).then_inc(*multiplied.step("rank"))
                pe.matmul(counted[:, 1, 0:NE], ones[:], before[:, TT, :], start=True, stop=True).then_inc(*multiplied.step("count"))

            @block.scalar
            def _(act):
                act.wait_ge(sorted_.sem, sorted_.value("lead"))
                act.activation(R.gate[:], R.gate[:], ACT.Exp).then_inc(raised, 1)

            @block.vector
            def _(dve):
                dve.sem_inc(sorted_.sem, sorted_.start)
                dve.wait_ge(base_in, 16)
                dve.wait_ge(multiplied.sem, multiplied.value("logits"))
                dve.tensor_tensor(logits[:], product[:].rearrange("p (t e) -> p t e", e=NE),
                          base[:].unsqueeze(1).to_broadcast([P, TT, NE]), ALU.add).then_inc(*sorted_.step("logits"))
                dve.wait_ge(sorted_.sem, sorted_.so_far())
                for t in range(TT):
                    dve.max(best[:, t, :], logits[:, t, :]).then_inc(*sorted_.step(f"best{t}"))
                    dve.wait_ge(sorted_.sem, sorted_.so_far())
                    dve.max_index(index[:, t, :], best[:, t, :], logits[:, t, :]).then_inc(*sorted_.step(f"index{t}"))
                dve.wait_ge(sorted_.sem, sorted_.so_far())
                dve.tensor_copy(index_f[:], index[:, :, 0:TOPK]).then_inc(*sorted_.step("float"))
                dve.tensor_tensor(R.gate[:].rearrange("p (t j) -> p t j", j=TOPK), best[:, :, 0:TOPK],
                          best[:, :, 0:1].to_broadcast([P, TT, TOPK]), ALU.subtract).then_inc(*sorted_.step("lead"))
                dve.wait_ge(sorted_.sem, sorted_.so_far())
                dve.wait_ge(made.sem, made.value("token"))
                dve.tensor_tensor(chosen[:], number[:].unsqueeze(1).unsqueeze(1).to_broadcast([P, TT, TOPK, NE]),
                          index_f[:].unsqueeze(3).to_broadcast([P, TT, TOPK, NE]), ALU.is_equal).then_inc(*sorted_.step("chosen"))
                dve.wait_ge(sorted_.sem, sorted_.so_far())
                dve.tensor_reduce(member[:], chosen[:].rearrange("p t j e -> p t e j"), AX, ALU.add).then_inc(*sorted_.step("member"))
                dve.memset(before[:, 0, :], 0.0).then_inc(*sorted_.step("none"))
                for t in range(TT):
                    dve.wait_ge(sorted_.sem, sorted_.so_far())
                    dve.tensor_tensor(before[:, t + 1, :], before[:, t, :], member[:, t, :], ALU.add).then_inc(*sorted_.step(f"before{t}"))
                dve.wait_ge(multiplied.sem, multiplied.value("count"))
                dve.tensor_copy(rank[:], counted[:, 0, 0:TT * NE].rearrange("p (t e) -> p t e", e=NE)).then_inc(*sorted_.step("rank"))
                dve.wait_ge(sorted_.sem, sorted_.so_far())
                dve.tensor_tensor(place[:], rank[:], region[:].unsqueeze(1).to_broadcast([P, TT, NE]), ALU.add).then_inc(*sorted_.step("place"))
                dve.wait_ge(sorted_.sem, sorted_.so_far())
                dve.tensor_tensor(spot[:], chosen[:], place[:].unsqueeze(2).to_broadcast([P, TT, TOPK, NE]), ALU.mult).then_inc(*sorted_.step("spot"))
                dve.wait_ge(sorted_.sem, sorted_.so_far())
                dve.tensor_reduce(dest[:], spot[:].rearrange("p t j e -> p (t j) e"), AX, ALU.add).then_inc(*sorted_.step("dest"))
                dve.wait_ge(sorted_.sem, sorted_.so_far())
                dve.tensor_copy(dest_i[:], dest[:]).then_inc(*sorted_.step("dest_i"))
                dve.wait_ge(raised, 1)
                gates = R.gate[:].rearrange("p (t j) -> p t j", j=TOPK)
                dve.tensor_reduce(total[:], gates, AX, ALU.add).then_inc(*sorted_.step("gate_sum"))
                dve.wait_ge(sorted_.sem, sorted_.so_far())
                dve.reciprocal(total[:], total[:]).then_inc(*sorted_.step("gate_inverse"))
                dve.wait_ge(sorted_.sem, sorted_.so_far())
                dve.tensor_tensor(gates, gates, total[:].unsqueeze(2).to_broadcast([P, TT, TOPK]), ALU.mult).then_inc(*sorted_.step("gate"))
                dve.tensor_scalar(blocks[:], counted[:, 1, 0:NE], 1.0 / P, (P - 1) / P - (P - 1) / (2 * P),
                          ALU.mult, ALU.add).then_inc(*sorted_.step("round"))
                dve.wait_ge(sorted_.sem, sorted_.so_far())
                dve.tensor_copy(blocks_i[:], blocks[:]).then_inc(*sorted_.step("int"))
                dve.wait_ge(sorted_.sem, sorted_.so_far())
                dve.tensor_scalar(blocks[:], blocks_i[:], 1.0, None, ALU.max).then_inc(*sorted_.step("least"))
                dve.memset(first[:], 0.0).then_inc(*sorted_.step("zero"))
                dve.wait_ge(sorted_.sem, sorted_.so_far())
                dve.tensor_tensor_scan(first[:, 1:NE + 1], ones[:, 0:NE], blocks[:], 0.0, ALU.mult, ALU.add).then_inc(*sorted_.step("scan"))
                dve.wait_ge(sorted_.sem, sorted_.so_far())
                dve.tensor_scalar(first[:, NE + 1:NE + 2], first[:, NE:NE + 1], -1.0, 2 * NE + 1.0, ALU.mult, ALU.add).then_inc(*sorted_.step("unused"))
                dve.wait_ge(sorted_.sem, sorted_.so_far())
                dve.tensor_copy(R.first[:], first[:]).then_inc(*sorted_.step("first"))
                dve.tensor_scalar(blocks[:], first[:, 0:NE], float(P), None, ALU.mult).then_inc(*sorted_.step("start"))
                dve.wait_ge(sorted_.sem, sorted_.so_far())
                dve.tensor_tensor(place[:], rank[:], blocks[:].unsqueeze(1).to_broadcast([P, TT, NE]), ALU.add).then_inc(*sorted_.step("row"))
                dve.wait_ge(sorted_.sem, sorted_.so_far())
                dve.tensor_tensor(spot[:], chosen[:], place[:].unsqueeze(2).to_broadcast([P, TT, TOPK, NE]), ALU.mult).then_inc(*sorted_.step("spot2"))
                dve.wait_ge(sorted_.sem, sorted_.so_far())
                dve.tensor_reduce(dest[:], spot[:].rearrange("p t j e -> p (t j) e"), AX, ALU.add).then_inc(*sorted_.step("dest2"))
                dve.wait_ge(sorted_.sem, sorted_.so_far())
                dve.tensor_copy(R.row[:], dest[:]).then_inc(*sorted_.step("dest2_i"))
                dve.wait_ge(sorted_.sem, sorted_.so_far())


def split_biases(nc, I, R):
    with ExitStack() as ctx:
        S = scope(nc, ctx, "biases")
        whole = S.sb("whole", [96, 3072])
        loaded = S.sem("loaded")
        names = ["first"] + [f"{w}{g}_{n}" for g in (1, 2) for n in range(g) for w in ("rest", "part")]
        split = S.steps("split", names)
        picked = S.steps("picked", ["zero", "g0", "g1", "g2"])
        with nc.Block() as block:
            @block.sync
            def _(sp):
                for g in range(3):
                    sp.dma_start(whole[32 * g:32 * g + 32, 0:2048], I["b1"][0]).then_inc(loaded, 16)
                    sp.dma_start(whole[32 * g:32 * g + 32, 2048:3072], I["b2"][0]).then_inc(loaded, 16)

            @block.gpsimd
            def _(pool):
                pool.sem_inc(picked.sem, picked.start)
                pool.memset(R.pick[:], 0.0).then_inc(*picked.step("zero"))
                for g in range(3):
                    pool.wait_ge(picked.sem, picked.so_far())
                    part = R.pick[32 * g:32 * g + 32, :].rearrange("p (e n) -> p e n", n=P)
                    pool.affine_select(out=part, in_=part, compare_op=ALU.not_equal, fill=1.0, base=0,
                                       pattern=[[-1, NE], [0, P]], channel_multiplier=1).then_inc(*picked.step(f"g{g}"))
                pool.wait_ge(picked.sem, picked.so_far())

            @block.vector
            def _(dve):
                dve.sem_inc(split.sem, split.start)
                dve.wait_ge(loaded, 96)
                dve.tensor_copy(R.bias[:], whole[:]).then_inc(*split.step("first"))
                for g in (1, 2):
                    rows = slice(32 * g, 32 * g + 32)
                    for n in range(g):
                        dve.wait_ge(split.sem, split.so_far())
                        dve.tensor_tensor(whole[rows, :], whole[rows, :], R.bias[rows, :], ALU.subtract).then_inc(*split.step(f"rest{g}_{n}"))
                        dve.wait_ge(split.sem, split.so_far())
                        dve.tensor_copy(R.bias[rows, :], whole[rows, :]).then_inc(*split.step(f"part{g}_{n}"))
                dve.wait_ge(split.sem, split.so_far())


def load_expert(sp, I, slots, loaded, e, c):
    if c < 4:
        source = I["w1"][0][ds(e, 1), :, c * 512:(c + 1) * 512].rearrange("a (k p) n -> p (a k) n", p=P)
        return sp.dma_start(slots[:, c, :].rearrange("p (k n) -> p k n", n=512), source).then_inc(loaded[c], 16)
    source = I["w2"][0][ds(e, 1), (c - 4) * 512:(c - 3) * 512, :].rearrange("a (k p) n -> p (a k) n", p=P)
    return sp.dma_start(slots[:, c, :].rearrange("p (k n) -> p k n", n=1024), source).then_inc(loaded[c], 16)


def experts(nc, I, h_rows, row_token, y_rows, slots, loaded, R, C):
    D, G = 1024, 4
    LIMIT, ALPHA = 7.0, 1.702
    with ExitStack() as ctx:
        S = scope(nc, ctx, "experts")
        index = S.sb("index", [P, 1], I32)
        x = S.sb("x", [P, D])
        xT = S.sb("xT", [P, 8, P])
        glu = S.sb("glu", [P, 2, 256])
        lin = S.sb("lin", [P, 2, 256])
        sig = S.sb("sig", [P, 2, 256])
        hid = S.sb("hid", [P, D])
        hidT = S.sb("hidT", [P, 8, P])
        y = S.sb("y", [P, D])
        flipped = S.ps("flipped", [P, 8, P])
        up = S.ps("up", [P, 2, 512])
        hid_flipped = S.ps("hid_flipped", [P, 8, P])
        down = S.ps("down", [P, 2, 512])
        blank = S.sb("blank", [P, D])
        index_in, x_in, y_out = S.sem("index_in"), S.sem("x_in"), S.sem("y_out")
        blanked, blank_out = S.sem("blanked"), S.sem("blank_out")
        held = S.sem("held")
        pe_steps = S.steps("products", ["x"] + [f"up{g}" for g in range(G)] + ["hid0", "hid1", "down"])
        act_steps = S.steps("act", ["xT"] + [f"sig{g}" for g in range(G)] + ["hidT0", "hidT1", "y"])
        dve_steps = S.steps("vector", [f"{w}{g}" for g in range(G) for w in ("glu", "lin", "both", "hid")] + ["y"])

        def blocks_of(eng, e):
            lo = eng.value_load(R.first[0:1, ds(e, 1)], min_val=0, max_val=2 * NE)
            hi = eng.value_load(R.first[0:1, ds(e + 1, 1)], min_val=1, max_val=2 * NE)
            return lo, hi

        with nc.Block() as block:
            @block.sync
            def _(sp):
                last = sp.value_load(R.first[0:1, NE:NE + 1], min_val=1, max_val=2 * NE)
                sp.wait_ge(blanked, 1)
                with sp.Fori(last, 2 * NE + 1) as b:
                    sp.dma_start(y_rows[ds((b * P).with_bounds(min_val=0, max_val=2 * NE * P), P), :], blank[:]).then_inc(blank_out, 16)
                with sp.Fori(1, NE) as e:
                    lo, _ = blocks_of(sp, e)
                    for c in range(6):
                        sp.wait_ge(pe_steps.sem, pe_steps.value(f"up{c}" if c < 4 else "down", lo - 1))
                        load_expert(sp, I, slots, loaded, e, c)
                unused = sp.value_load(R.first[0:1, NE + 1:NE + 2], min_val=1, max_val=2 * NE + 1)
                sp.wait_ge(blank_out, unused * 16)
                sp.sem_inc(held, 1)

            @block.gpsimd
            def _(pool):
                with pool.Fori(0, NE) as e:
                    lo, hi = blocks_of(pool, e)
                    with pool.Fori(lo, hi) as b:
                        pool.wait_ge(pe_steps.sem, pe_steps.value("x", b - 1))
                        pool.dma_start(index[:], row_token[ds((e * T_ALL + (b - lo) * P).with_bounds(min_val=0, max_val=(NE * 8 - 1) * P), P), :],
                                       allow_slow_non_contiguous=True).then_inc(index_in, 16)
                        pool.wait_ge(index_in, b * 16 + 16)
                        pool.sem_inc(held, 1)
                        pool.indirect_dma_start(x[:], None, h_rows,
                                                bass.IndirectOffsetOnAxis(ap=index[:, 0:1], axis=0)).then_inc(x_in, 16)
                        pool.wait_ge(x_in, b * 16 + 16)

            @block.scalar
            def _(act):
                act.sem_inc(act_steps.sem, act_steps.start)
                with act.Fori(0, NE) as e:
                    lo, hi = blocks_of(act, e)
                    with act.Fori(lo, hi) as b:
                        act.wait_ge(pe_steps.sem, pe_steps.value("x", b))
                        act.copy(xT[:], flipped[:]).then_inc(*act_steps.step("xT"))
                        for g in range(G):
                            act.wait_ge(dve_steps.sem, dve_steps.value(f"glu{g}", b))
                            act.activation(sig[:, g % 2, :], glu[:, g % 2, :], ACT.Sigmoid, scale=ALPHA).then_inc(*act_steps.step(f"sig{g}"))
                        act.wait_ge(pe_steps.sem, pe_steps.value("hid0", b))
                        act.copy(hidT[:, 0:6, :], hid_flipped[:, 0:6, :]).then_inc(*act_steps.step("hidT0"))
                        act.wait_ge(pe_steps.sem, pe_steps.value("hid1", b))
                        act.copy(hidT[:, 6:8, :], hid_flipped[:, 6:8, :]).then_inc(*act_steps.step("hidT1"))
                        act.wait_ge(pe_steps.sem, pe_steps.value("down", b))
                        act.wait_ge(y_out, b * 16 + 16)
                        act.copy(y[:, 0:512], down[:, 0, :]).then_inc(*act_steps.step("y"))
                        act.wait_ge(dve_steps.sem, dve_steps.value("y", b))
                        act.wait_ge(act_steps.sem, act_steps.so_far(b))
                        act.dma_start(y_rows[ds((b * P).with_bounds(min_val=0, max_val=(2 * NE - 1) * P), P), :], y[:]).then_inc(y_out, 16)
                last = act.value_load(R.first[0:1, NE:NE + 1], min_val=1, max_val=2 * NE)
                act.wait_ge(y_out, last * 16 + 16)
                act.sem_inc(held, 1)

            @block.vector
            def _(dve):
                dve.sem_inc(dve_steps.sem, dve_steps.start)
                dve.sem_inc(y_out, 16)
                dve.memset(blank[:], 0.0).then_inc(blanked, 1)
                with dve.Fori(0, NE) as e:
                    lo, hi = blocks_of(dve, e)
                    with dve.Fori(lo, hi) as b:
                        for g in range(G):
                            s = g % 2
                            pair = up[:, s, :].rearrange("p (n two) -> p n two", two=2)
                            dve.wait_ge(pe_steps.sem, pe_steps.value(f"up{g}", b))
                            dve.wait_ge(dve_steps.sem, dve_steps.so_far(b))
                            dve.tensor_scalar(glu[:, s, :], pair[:, :, 0], LIMIT, None, ALU.min).then_inc(*dve_steps.step(f"glu{g}"))
                            dve.tensor_scalar(lin[:, s, :], pair[:, :, 1], -LIMIT, LIMIT, ALU.max, ALU.min).then_inc(*dve_steps.step(f"lin{g}"))
                            dve.wait_ge(dve_steps.sem, dve_steps.so_far(b))
                            dve.scalar_tensor_tensor(lin[:, s, :], lin[:, s, :], 1.0, glu[:, s, :],
                                                     ALU.add, ALU.mult).then_inc(*dve_steps.step(f"both{g}"))
                            dve.wait_ge(act_steps.sem, act_steps.value(f"sig{g}", b))
                            dve.wait_ge(dve_steps.sem, dve_steps.so_far(b))
                            if g == 0:
                                dve.wait_ge(pe_steps.sem, pe_steps.value("hid1", b - 1))
                            dve.tensor_tensor(hid[:, g * 256:(g + 1) * 256], lin[:, s, :], sig[:, s, :],
                                              ALU.mult).then_inc(*dve_steps.step(f"hid{g}"))
                        dve.wait_ge(pe_steps.sem, pe_steps.value("down", b))
                        dve.wait_ge(y_out, b * 16 + 16)
                        dve.tensor_copy(y[:, 512:1024], down[:, 1, :]).then_inc(*dve_steps.step("y"))

            @block.tensor
            def _(pe):
                pe.sem_inc(pe_steps.sem, pe_steps.start)
                with pe.Fori(0, NE) as e:
                    lo, hi = blocks_of(pe, e)
                    pick = R.pick[:, ds(e * P, P)]
                    with pe.Fori(lo, hi) as b:
                        pe.wait_ge(x_in, b * 16 + 16)
                        pe.wait_ge(act_steps.sem, act_steps.value("xT", b - 1))
                        for k in range(8):
                            ins = pe.transpose(flipped[:, k, :], x[:, k * P:(k + 1) * P], C.ident[:])
                        ins.then_inc(*pe_steps.step("x"))
                        pe.wait_ge(act_steps.sem, act_steps.value("xT", b))
                        for g in range(G):
                            if g < 2:
                                pe.wait_ge(dve_steps.sem, dve_steps.value(f"lin{g + 2}", b - 1))
                            else:
                                pe.wait_ge(dve_steps.sem, dve_steps.value(f"lin{g - 2}", b))
                            pe.wait_ge(loaded[g], e * 16 + 16)
                            w = slots[:, g, :].rearrange("p (k n) -> p k n", n=512)
                            pe.matmul(up[:, g % 2, :], pick, R.bias[:, g * 512:(g + 1) * 512], start=True, stop=False)
                            for k in range(8):
                                ins = pe.matmul(up[:, g % 2, :], xT[:, k, :], w[:, k, :], start=False, stop=(k == 7))
                            ins.then_inc(*pe_steps.step(f"up{g}"))
                        pe.wait_ge(dve_steps.sem, dve_steps.value("hid2", b))
                        pe.wait_ge(act_steps.sem, act_steps.value("hidT1", b - 1))
                        for k in range(6):
                            ins = pe.transpose(hid_flipped[:, k, :], hid[:, k * P:(k + 1) * P], C.ident[:])
                        ins.then_inc(*pe_steps.step("hid0"))
                        pe.wait_ge(act_steps.sem, act_steps.value("hidT0", b))
                        pe.wait_ge(act_steps.sem, act_steps.value("y", b - 1))
                        pe.wait_ge(dve_steps.sem, dve_steps.value("y", b - 1))
                        for part in range(2):
                            pe.wait_ge(loaded[4 + part], e * 16 + 16)
                            w = slots[:, 4 + part, :].rearrange("p (k n) -> p k n", n=1024)
                            for k in range(4):
                                kk = 4 * part + k
                                if kk == 6:
                                    pe.wait_ge(dve_steps.sem, dve_steps.value("hid3", b))
                                    for kt in (6, 7):
                                        ins = pe.transpose(hid_flipped[:, kt, :], hid[:, kt * P:(kt + 1) * P], C.ident[:])
                                    ins.then_inc(*pe_steps.step("hid1"))
                                    pe.wait_ge(act_steps.sem, act_steps.value("hidT1", b))
                                for half in range(2):
                                    if kk == 0:
                                        pe.matmul(down[:, half, :], pick, R.bias[:, 2048 + half * 512:2560 + half * 512],
                                                  start=True, stop=False)
                                    ins = pe.matmul(down[:, half, :], hidT[:, kk, :], w[:, k, half * 512:(half + 1) * 512],
                                                    start=False, stop=(kk == 7))
                        ins.then_inc(*pe_steps.step("down"))


def combine(nc, I, x, y_rows, out, R, C):
    D, TT, SLOTS = 1024, 8, 8
    with ExitStack() as ctx:
        S = scope(nc, ctx, "combine")
        rows = S.sb("rows", [P, SLOTS, D])
        gains = S.sb("gains", [P, D])
        junk = S.sb("junk", [P, D])
        stat = S.sb("stat", [P, 4, TT])
        gathered = [S.sem(f"gathered{n}") for n in range(SLOTS)]
        gain_in, stored = S.sem("gain_in"), S.sem("stored")
        added = S.steps("added", [f"add{j}" for j in range(TOPK)])
        squared = S.steps("squared", ["sum", "root"], back=1)
        scaled = S.steps("scaled", ["mean", "inverse", "scale"], back=1)
        N = TT * TOPK
        with nc.Block() as block:
            @block.gpsimd
            def _(pool):
                for n in range(N):
                    if n >= SLOTS:
                        pool.wait_ge(added.sem, added.value(f"add{n % TOPK}", n // TOPK - SLOTS // TOPK))
                    pool.indirect_dma_start(rows[:, n % SLOTS, :], None, y_rows,
                                            bass.IndirectOffsetOnAxis(ap=R.row[:, n:n + 1], axis=0)).then_inc(gathered[n % SLOTS], 16)

            @block.vector
            def _(dve):
                dve.sem_inc(added.sem, added.start)
                dve.sem_inc(scaled.sem, scaled.start)
                dve.wait_ge(gain_in, 16)

                def add(t):
                    tile = x[:, t * D:(t + 1) * D]
                    added.round()
                    for j in range(TOPK):
                        n = t * TOPK + j
                        dve.wait_ge(gathered[n % SLOTS], 16 * (n // SLOTS + 1))
                        dve.wait_ge(added.sem, added.so_far(t))
                        dve.scalar_tensor_tensor(tile, rows[:, n % SLOTS, :], R.gate[:, n:n + 1], tile,
                                                 ALU.mult, ALU.add).then_inc(*added.step(f"add{j}"))

                def scale(t):
                    tile = x[:, t * D:(t + 1) * D]
                    scaled.round()
                    dve.wait_ge(squared.sem, squared.value("sum", t))
                    dve.tensor_scalar(stat[:, 1, t:t + 1], stat[:, 0, t:t + 1], 1.0 / D, EPS, ALU.mult, ALU.add).then_inc(*scaled.step("mean"))
                    dve.wait_ge(squared.sem, squared.value("root", t))
                    dve.reciprocal(stat[:, 3, t:t + 1], stat[:, 2, t:t + 1]).then_inc(*scaled.step("inverse"))
                    dve.wait_ge(scaled.sem, scaled.so_far(t))
                    dve.scalar_tensor_tensor(tile, tile, stat[:, 3, t:t + 1], gains[:], ALU.mult, ALU.mult).then_inc(*scaled.step("scale"))
                for t in range(TT + 1):
                    if t < TT:
                        add(t)
                    if t >= 1:
                        scale(t - 1)

            @block.scalar
            def _(act):
                act.sem_inc(squared.sem, squared.start)
                for t in range(TT):
                    act.wait_ge(added.sem, added.value(f"add{TOPK - 1}", t))
                    squared.round()
                    act.wait_ge(squared.sem, squared.so_far(t))
                    act.activation(junk[:], x[:, t * D:(t + 1) * D], ACT.Square,
                                   accum_out=stat[:, 0, t:t + 1]).then_inc(*squared.step("sum"))
                    act.wait_ge(scaled.sem, scaled.value("mean", t))
                    act.activation(stat[:, 2, t:t + 1], stat[:, 1, t:t + 1], ACT.Sqrt).then_inc(*squared.step("root"))

            @block.sync
            def _(sp):
                sp.dma_start(gains[:], row_to_all(I["norm_final_g"])).then_inc(gain_in, 16)
                for t in range(TT):
                    sp.wait_ge(scaled.sem, scaled.value("scale", t))
                    sp.dma_start(out[0, t * P:(t + 1) * P, :], x[:, t * D:(t + 1) * D]).then_inc(stored, 16)
                sp.wait_ge(stored, 16 * TT)


LAMBDA_INIT = 0.8 - 0.6


class Constants:
    def __init__(self):
        self.vector = {}


def build(nc, I, out, stop=99):
    C = Constants()
    Scope.spent = []
    with ExitStack() as top:
        G = scope(nc, top, "g")
        make_constants(nc, G, C)
        load_vectors(nc, G, I, C)
        across = G.sb("across", [P, 8, 1024])
        yT, oT = across[:, 0:4, :], across[:, 4:8, :]
        with ExitStack() as mix:
            M = scope(nc, mix, "m")
            hT = M.sb("hT", [P, 8, 1024])
            with ExitStack() as c:
                S = scope(nc, c, "xs")
                x = S.sb("x", [P, 8 * 1024])
                normalise(nc, "norm_mix", x, 8, I["norm_mix_g"][0], hT, C, load=I["x"][0])
            if stop < 1:
                return
            w_in = I["w_in"][0]
            with ExitStack() as c:
                S = scope(nc, c, "diff")
                qk = S.sb("qk", [P, 8, 1024])
                v = S.sb("v", [P, 8, 512])
                project_channels(nc, "diff_qk", w_in[:, 1824:2848], 2, hT, qk, scale=C.qk_scale)
                diff_values(nc, w_in[:, 2848:3360], hT, v)
                diff_attention(nc, qk[:, 0:4, :], qk[:, 4:8, :], v, oT, C)
            recycle(nc)
            if stop < 2:
                return
            with ExitStack() as c:
                S = scope(nc, c, "rwkv")
                C.variance = S.sb("variance", [P, 64])
                masks = rwkv_masks(nc, S)
                u = S.sb("u", [P, 12, 1024])
                sig = S.sb("sig", [P, 4, 1024])
                a = S.sb("a", [P, 4, 1024])
                project_channels(nc, "rkv", w_in[:, 0:1536], 3, hT, u, mu=C.vector["mu"])
                rwkv_low_rank(nc, I, hT, u, sig, a, yT, C)
                if stop < 3:
                    return
                kkn, fall = hT[:, 0:4, :], hT[:, 4:8, :]
                rwkv_keys(nc, u, a, sig, kkn, fall, masks[2], C)
                rwkv_chunks(nc, u, a, sig, kkn, fall, masks, u[:, 4:8, :], C)
                rwkv_outputs(nc, u[:, 4:8, :], u[:, 0:4, :], yT, C)
            if stop < 4:
                return
        recycle(nc)
        x = G.sb("x", [P, 8 * 1024])
        add_projection(nc, "w_out", across, I["w_out"][0], x, load=I["x"][0])
        if stop < 5:
            return
        with ExitStack() as c:
            S = scope(nc, c, "cr")
            memT = S.sb("memT", [P, 8, 256])
            kT = S.sb("kT", [P, 8, 256])
            v = S.sb("v", [P, 2, 1024])
            qT = S.sb("qT", [P, 8, 1024])
            with ExitStack() as c2:
                mem = scope(nc, c2, "mem").sb("rows", [P, 2 * 1024])
                normalise(nc, "norm_mem", mem, 2, I["norm_mem_g"][0], memT, C, load=I["mem"][0])
            cross_keys_values(nc, I["w_ckv"][0], memT, kT, v)
            normalise(nc, "norm_cross", x, 8, I["norm_cross_g"][0], across, C)
            project_channels(nc, "cross_q", I["w_cq"][0], 2, across, qT, scale=C.cross_scale)
            cross_attention(nc, qT, kT, v, across, C)
        add_projection(nc, "w_co", across, I["w_co"][0], x)
        if stop < 6:
            return
        recycle(nc)
        R = Constants()
        R.gate = G.sb("gate", [P, 8 * TOPK])
        R.row = G.sb("row", [P, 8 * TOPK], I32)
        R.first = G.sb("first", [P, NE + 2], I32)
        h_rows = nc.dram_tensor("h_rows", [T_ALL, 1024], F32).ap()
        row_token = nc.dram_tensor("row_token", [NE * T_ALL, 1], I32).ap()
        y_rows = nc.dram_tensor("y_rows", [(2 * NE + 1) * P, 1024], F32).ap()
        with ExitStack() as c:
            S = scope(nc, c, "moe")
            slots = S.sb("slots", [P, 6, 4096])
            R.bias = S.sb("bias", [96, 3072], BF16)
            R.pick = S.sb("pick", [96, NE * P], BF16)
            loaded = [S.sem(f"loaded{n}") for n in range(6)]
            with nc.Block() as block:
                @block.sync
                def _(sp):
                    for n in range(6):
                        load_expert(sp, I, slots, loaded, 0, n)
            normalise(nc, "norm_ffn", x, 8, I["norm_ffn_g"][0], across, C, keep=h_rows)
            split_biases(nc, I, R)
            route(nc, I, across, row_token, R, C)
            if stop < 8:
                return
            experts(nc, I, h_rows, row_token, y_rows, slots, loaded, R, C)
        combine(nc, I, x, y_rows, out, R, C)


_OUT = (1, 1024, 1024)


def kernel(**inputs):
    import numpy as _np
    import concourse.bacc as _bacc
    from concourse import mybir as _mybir
    from concourse.bass_utils import run_bass_kernel_spmd as _run

    nc = _bacc.Bacc("TRN2", target_bir_lowering=False, num_devices=1)
    arrays, given = {}, {}
    for name, value in inputs.items():
        a = _np.ascontiguousarray(value)
        arrays[f"in_{name}_dram"] = a
        given[name] = nc.dram_tensor(f"in_{name}_dram", a.shape, _mybir.dt.from_np(a.dtype), kind="ExternalInput").ap()
    out = nc.dram_tensor("out_dram", _OUT, _mybir.dt.from_np(_np.dtype("float32")), kind="ExternalOutput").ap()
    build(nc, given, out)
    r = _run(nc, [arrays], core_ids=[0])
    return r.results[0]["out_dram"]
```

```python
from contextlib import ExitStack

import numpy as np
import concourse.bass as bass
from concourse import mybir

F32 = mybir.dt.float32
BF16 = mybir.dt.bfloat16
F32R = mybir.dt.float32r
I32 = mybir.dt.int32
U32 = mybir.dt.uint32
ALU = mybir.AluOpType
ACT = mybir.ActivationFunctionType
AX = mybir.AxisListType.X
P = 128
EPS = 1e-5
ds = bass.ds


class Steps:

    def __init__(self, sem, names, back=1):
        self.sem, self.names, self.start = sem, names, max(1, back * len(names))
        self.at = 0

    def round(self):
        self.at = 0

    def value(self, name, i=0):
        return i * len(self.names) + self.start + self.names.index(name) + 1

    def step(self, name):
        self.at %= len(self.names)
        assert self.names[self.at] == name, (self.names[self.at], name)
        self.at += 1
        return self.sem, 1

    def so_far(self, i=0):
        return i * len(self.names) + self.start + self.at

    def end(self, rounds=1):
        return rounds * len(self.names) + self.start


class Scope:

    spent = []

    def __init__(self, nc, ctx, name):
        self.nc, self.ctx, self.name = nc, ctx, name

    def sb(self, name, shape, dt=F32):
        return self.ctx.enter_context(self.nc.sbuf_tensor(f"{self.name}_{name}", shape, dt))

    def ps(self, name, shape, dt=F32):
        return self.ctx.enter_context(self.nc.psum_tensor(f"{self.name}_{name}", shape, dt))

    def sem(self, name):
        made = self.nc.alloc_semaphore(f"{self.name}_{name}")
        self.ctx.callback(Scope.spent.append, made)
        return made

    def steps(self, name, names, back=1):
        return Steps(self.sem(name), names, back)


def recycle(nc):
    nc.all_engine_barrier()
    nc.clear_and_free_semaphores(Scope.spent)
    nc.all_engine_barrier()
    Scope.spent = []


def scope(nc, ctx, name):
    return Scope(nc, ctx, name)


def row_to_all(vec, n=P):
    return vec.rearrange("(a n) -> a n", a=1).partition_broadcast(n).rearrange("p a n -> p (a n)")


def make_constants(nc, S, C):
    C.ident = S.sb("ident", [P, P])
    made = S.steps("pool_made", ["zero", "ident"])
    with nc.Block() as block:
        @block.gpsimd
        def _(pool):
            pool.sem_inc(made.sem, made.start)
            pool.memset(C.ident[:], 0.0).then_inc(*made.step("zero"))
            pool.wait_ge(made.sem, made.so_far())
            pool.affine_select(out=C.ident[:], in_=C.ident[:], compare_op=ALU.not_equal,
                               fill=1.0, base=0, pattern=[[-1, P]], channel_multiplier=1).then_inc(*made.step("ident"))
            pool.wait_ge(made.sem, made.end())


def normalise(nc, name, x, tiles, gain, hT, C, load=None, keep=None):
    D = 1024
    KT = D // P
    with ExitStack() as ctx:
        S = scope(nc, ctx, name)
        gains = S.sb("gains", [P, D])
        rows = S.sb("rows", [P, 2 * D])
        junk = S.sb("junk", [P, D])
        stat = S.sb("stat", [P, 4 * tiles])
        sums, mean, root, rstd = (stat[:, i * tiles:(i + 1) * tiles] for i in range(4))
        flipped = S.ps("flipped", [P, 2, D])
        x_in, gain_in = [S.sem(f"x_in{t}") for t in range(tiles)], S.sem("gain_in")
        rows_out = [S.sem(f"rows_out{j}") for j in range(2)]
        squares = S.steps("squares", ["tile"], back=1)
        rooted = S.sem("rooted")
        stats = S.steps("stats", ["mean", "rstd"])
        scaled = S.steps("scaled", ["even", "odd"])
        turned = S.steps("turned", ["even", "odd"])
        copied = S.steps("copied", ["even", "odd"])
        pair = ["even", "odd"]
        with nc.Block() as block:
            @block.sync
            def _(sp):
                sp.dma_start(gains[:], row_to_all(gain)).then_inc(gain_in, 16)
                if load is not None:
                    for t in range(tiles):
                        sp.dma_start(x[:, t * D:(t + 1) * D], load[t * P:(t + 1) * P, :]).then_inc(x_in[t], 16)
                if keep is not None:
                    for j in range(2):
                        sp.sem_inc(rows_out[j], 16)
                    with sp.Fori(0, tiles // 2) as i:
                        for j in range(2):
                            sp.wait_ge(scaled.sem, scaled.value(pair[j], i))
                            sp.dma_start(keep[ds(i * (2 * P) + j * P, P), :],
                                         rows[:, j * D:(j + 1) * D]).then_inc(rows_out[j], 16)
                    for j in range(2):
                        sp.wait_ge(rows_out[j], 16 * (tiles // 2) + 16)

            @block.scalar
            def _(act):
                act.sem_inc(squares.sem, squares.start)
                act.sem_inc(copied.sem, copied.start)
                for t in range(tiles):
                    if load is not None:
                        act.wait_ge(x_in[t], 16)
                    squares.round()
                    act.wait_ge(squares.sem, squares.so_far(t))
                    act.activation(junk[:], x[:, t * D:(t + 1) * D], ACT.Square,
                                   accum_out=sums[:, t:t + 1]).then_inc(*squares.step("tile"))
                act.wait_ge(stats.sem, stats.value("mean"))
                act.activation(root, mean, ACT.Sqrt).then_inc(rooted, 1)
                with act.Fori(0, tiles // 2) as i:
                    for j in range(2):
                        act.wait_ge(turned.sem, turned.value(pair[j], i))
                        act.copy(hT[:, :, ds(i * (2 * P) + j * P, P)],
                                 flipped[:, j, :].rearrange("p (k n) -> p k n", n=P)).then_inc(*copied.step(pair[j]))
                act.wait_ge(copied.sem, copied.end(tiles // 2))

            @block.vector
            def _(dve):
                dve.sem_inc(stats.sem, stats.start)
                dve.sem_inc(scaled.sem, scaled.start)
                dve.wait_ge(squares.sem, squares.value("tile", tiles - 1))
                dve.tensor_scalar(mean, sums, 1.0 / D, EPS, ALU.mult, ALU.add).then_inc(*stats.step("mean"))
                dve.wait_ge(rooted, 1)
                dve.reciprocal(rstd, root).then_inc(*stats.step("rstd"))
                dve.wait_ge(stats.sem, stats.so_far())
                dve.wait_ge(gain_in, 16)
                with dve.Fori(0, tiles // 2) as i:
                    for j in range(2):
                        dve.wait_ge(turned.sem, turned.value(pair[j], i - 1))
                        if keep is not None:
                            dve.wait_ge(rows_out[j], i * 16 + 16)
                        t = 2 * i + j
                        dve.scalar_tensor_tensor(rows[:, j * D:(j + 1) * D], x[:, ds(t * D, D)],
                                                 rstd[:, ds(t, 1)], gains[:], ALU.mult, ALU.mult).then_inc(*scaled.step(pair[j]))

            @block.tensor
            def _(pe):
                pe.sem_inc(turned.sem, turned.start)
                with pe.Fori(0, tiles // 2) as i:
                    for j in range(2):
                        pe.wait_ge(scaled.sem, scaled.value(pair[j], i))
                        pe.wait_ge(copied.sem, copied.value(pair[j], i - 1))
                        for k in range(KT):
                            ins = pe.transpose(flipped[:, j, k * P:(k + 1) * P],
                                               rows[:, j * D + k * P:j * D + (k + 1) * P], C.ident[:])
                        ins.then_inc(*turned.step(pair[j]))


def project_channels(nc, name, w, rounds, hT, result, scale=None, mu=None):
    T = 1024
    with ExitStack() as ctx:
        S = scope(nc, ctx, name)
        weights = S.sb("weights", [P, 2, 8, 256])
        product = S.ps("product", [P, 2, T])
        w_in = [S.sem(f"w_in{j}") for j in range(2)]
        tiles = ["tile0", "tile1", "tile2", "tile3"]
        multiplied = S.steps("multiplied", tiles)
        copied = S.steps("copied", tiles)
        shifted = S.steps("shifted", tiles)
        if mu is not None:
            keep_mu = S.sb("keep_mu", [P, 4 * rounds])
            kept = S.sem("kept")
        with nc.Block() as block:
            @block.sync
            def _(sp):
                with sp.Fori(0, rounds) as i:
                    for j in range(2):
                        sp.wait_ge(multiplied.sem, multiplied.value(tiles[2 * j + 1], i - 1))
                        sp.dma_start(weights[:, j], w[:, ds(i * 512 + j * 256, 256)]
                                     .rearrange("(k p) n -> p k n", p=P)).then_inc(w_in[j], 16)

            @block.tensor
            def _(pe):
                pe.sem_inc(multiplied.sem, multiplied.start)
                with pe.Fori(0, rounds) as i:
                    for c in range(4):
                        if c % 2 == 0:
                            pe.wait_ge(w_in[c // 2], i * 16 + 16)
                        before = (tiles[c - 2], i) if c >= 2 else (tiles[c + 2], i - 1)
                        pe.wait_ge(copied.sem, copied.value(*before))
                        if mu is not None:
                            pe.wait_ge(shifted.sem, shifted.value(*before))
                        for half in range(2):
                            for k in range(8):
                                ins = pe.matmul(product[:, c % 2, half * 512:(half + 1) * 512],
                                                weights[:, c // 2, k, (c % 2) * P:(c % 2 + 1) * P],
                                                hT[:, k, half * 512:(half + 1) * 512], start=(k == 0), stop=(k == 7))
                        ins.then_inc(*multiplied.step(tiles[c]))

            @block.scalar
            def _(act):
                act.sem_inc(copied.sem, copied.start)
                if mu is not None:
                    act.wait_ge(kept, 1)
                with act.Fori(0, rounds) as i:
                    for c in range(4):
                        act.wait_ge(multiplied.sem, multiplied.value(tiles[c], i))
                        factor = scale[:, ds(i, 1)] if mu is None else keep_mu[:, ds(i * 4 + c, 1)]
                        act.activation(result[:, ds(i * 4 + c, 1), :].rearrange("p a n -> p (a n)"),
                                       product[:, c % 2, :], ACT.Copy, scale=factor).then_inc(*copied.step(tiles[c]))
                act.wait_ge(copied.sem, copied.end(rounds))

            @block.vector
            def _(dve):
                if mu is None:
                    return
                dve.sem_inc(shifted.sem, shifted.start)
                dve.tensor_scalar(keep_mu[:], mu[:, 0:4 * rounds], -1.0, 1.0, ALU.mult, ALU.add).then_inc(kept, 1)
                with dve.Fori(0, rounds) as i:
                    for c in range(4):
                        dve.wait_ge(copied.sem, copied.value(tiles[c], i))
                        later = result[:, ds(i * 4 + c, 1), 1:T].rearrange("p a n -> p (a n)")
                        dve.scalar_tensor_tensor(later, product[:, c % 2, 0:T - 1],
                                                 mu[:, ds(i * 4 + c, 1)], later,
                                                 ALU.mult, ALU.add).then_inc(*shifted.step(tiles[c]))
                dve.wait_ge(shifted.sem, shifted.end(rounds))


def load_vectors(nc, S, I, C):
    wanted = [("mu", I["shift_mu"][0, 0:1792], 14), ("w0", I["w0"][0], 4), ("a0", I["a0"][0], 4),
              ("k_k", I["k_k"][0], 4), ("k_a", I["k_a"][0], 4),
              ("r_k", I["r_k"][0].rearrange("h n -> (h n)"), 4), ("lnx_g", I["lnx_g"][0], 4),
              ("lnx_b", I["lnx_b"][0], 4), ("subln_g", I["subln_g"][0], 1)]
    vectors = S.sb("vectors", [P, sum(n for _, _, n in wanted)])
    at = 0
    loaded = S.sem("vectors_in")
    places = []
    for name, source, n in wanted:
        part = vectors[:, at:at + n]
        C.vector[name] = part
        places.append((part, source.rearrange("(c p) -> p c", p=P)))
        at += n
    C.mu_tail = S.sb("mu_tail", [32, 1])
    places.append((C.mu_tail[:], I["shift_mu"][0, 1792:1824].rearrange("(c p) -> p c", p=32)))
    C.qk_scale = S.sb("qk_scale", [P, 2])
    C.cross_scale = S.sb("cross_scale", [P, 2])
    C.lam = S.sb("lam", [P, 1])
    lam_in = S.sb("lam_in", [P, 4 * 64])
    products = S.sb("lam_products", [P, 2 * 64])
    sums = S.sb("lam_sums", [P, 4])
    for n, v in enumerate(["lambda_q1", "lambda_k1", "lambda_q2", "lambda_k2"]):
        places.append((lam_in[:, n * 64:(n + 1) * 64], row_to_all(I[v][0])))
    made = S.steps("lambda", ["q_scale", "k_scale", "cross_scale", "product1", "product2", "sums", "difference", "sum"])
    powers = S.sem("lambda_powers")
    with nc.Block() as block:
        @block.sync
        def _(sp):
            for place, source in places:
                sp.dma_start(place, source, allow_slow_non_contiguous=True).then_inc(loaded, 16)

        @block.vector
        def _(dve):
            dve.sem_inc(made.sem, made.start)
            dve.memset(C.qk_scale[:, 0:1], 64 ** -0.5).then_inc(*made.step("q_scale"))
            dve.memset(C.qk_scale[:, 1:2], 1.0).then_inc(*made.step("k_scale"))
            dve.memset(C.cross_scale[:], 256 ** -0.5).then_inc(*made.step("cross_scale"))
            dve.wait_ge(loaded, 16 * len(places))
            for n in range(2):
                dve.tensor_tensor(products[:, n * 64:(n + 1) * 64], lam_in[:, n * 128:n * 128 + 64],
                                  lam_in[:, n * 128 + 64:n * 128 + 128], ALU.mult).then_inc(*made.step(f"product{n + 1}"))
            dve.wait_ge(made.sem, made.so_far())
            dve.tensor_reduce(sums[:, 0:2], products[:].rearrange("p (a n) -> p a n", a=2), AX, ALU.add).then_inc(*made.step("sums"))
            dve.wait_ge(powers, 1)
            dve.tensor_tensor(sums[:, 0:1], sums[:, 2:3], sums[:, 3:4], ALU.subtract).then_inc(*made.step("difference"))
            dve.wait_ge(made.sem, made.so_far())
            dve.tensor_scalar(C.lam[:], sums[:, 0:1], LAMBDA_INIT, None, ALU.add).then_inc(*made.step("sum"))
            dve.wait_ge(made.sem, made.so_far())

        @block.scalar
        def _(act):
            act.wait_ge(made.sem, made.value("sums"))
            act.activation(sums[:, 2:4], sums[:, 0:2], ACT.Exp).then_inc(powers, 1)


def diff_values(nc, w, hT, v):
    with ExitStack() as ctx:
        S = scope(nc, ctx, "diff_v")
        weights = S.sb("weights", [P, 8, 512])
        product = S.ps("product", [P, 2, 512])
        w_in = S.sem("w_in")
        multiplied = S.steps("multiplied", ["tile"], back=2)
        copied = S.steps("copied", ["tile"], back=2)
        with nc.Block() as block:
            @block.sync
            def _(sp):
                sp.dma_start(weights[:], w.rearrange("(k p) n -> p k n", p=P)).then_inc(w_in, 16)

            @block.tensor
            def _(pe):
                pe.sem_inc(multiplied.sem, multiplied.start)
                pe.wait_ge(w_in, 16)
                for t in range(8):
                    pe.wait_ge(copied.sem, copied.value("tile", t - 2))
                    for k in range(8):
                        ins = pe.matmul(product[:, t % 2, :], hT[:, k, t * P:(t + 1) * P], weights[:, k, :],
                                        start=(k == 0), stop=(k == 7))
                    ins.then_inc(*multiplied.step("tile"))

            @block.scalar
            def _(act):
                act.sem_inc(copied.sem, copied.start)
                for t in range(8):
                    act.wait_ge(multiplied.sem, multiplied.value("tile", t))
                    act.copy(v[:, t, :], product[:, t % 2, :]).then_inc(*copied.step("tile"))
                act.wait_ge(copied.sem, copied.end(8))


def diff_attention(nc, q, k, v, oT, C):
    H, T, B = 4, 1024, 8
    HIDDEN = -1.0e30
    units = [(b, h) for b in range(B) for h in range(H)]
    N = len(units)
    with ExitStack() as ctx:
        S = scope(nc, ctx, "attn")
        bias = S.sb("bias", [P, H, T])
        dist = S.sb("dist", [P, T])
        score = S.sb("score", [P, 2, 2, T])
        flipT = S.sb("flipT", [P, 2, T])
        heads = S.sb("heads", [P, B, 512])
        high = S.sb("high", [P, 2, 2])
        total = S.sb("total", [P, 2, 2])
        weight = S.sb("weight", [P, 2, 2])
        square = S.sb("square", [P, 2, P])
        stat = S.sb("stat", [P, 3 * N])
        sums, mean, rstd = (stat[:, i * N:(i + 1) * N] for i in range(3))
        gain = S.sb("gain", [P, 1])
        scores = S.ps("scores", [P, 2, T])
        flipped = S.ps("flipped", [P, T])
        values = S.ps("values", [P, 2, 512])
        ready = S.steps("ready", ["dist", "masked"])
        biased = S.steps("biased", [f"slope{h}" for h in range(H)])
        scored = S.steps("scored", ["unit"], back=1)
        turned = S.steps("turned", ["unit"], back=1)
        valued = S.steps("valued", ["unit"], back=2)
        softened = S.steps("softened", ["bias0", "bias1", "negate"], back=2)
        softened_mix = S.steps("mixed", ["recip", "lambda", "scale", "mix"], back=2)
        raised = S.steps("raised", ["exp0", "exp1"], back=2)
        copied = S.steps("copied", ["weights"], back=2)
        taken = S.steps("taken", ["values", "square"], back=2)
        normed = S.steps("normed", ["gain", "mean", "rstd"])
        rooted = S.sem("rooted")
        scaled = S.steps("scaled", ["block"], back=1)
        crossed = S.steps("crossed", ["block"], back=2)
        stored = S.steps("stored", ["block"], back=2)

        with nc.Block() as block:
            @block.gpsimd
            def _(pool):
                pool.sem_inc(ready.sem, ready.start)
                pool.iota(dist[:], pattern=[[1, T]], base=P - T, channel_multiplier=-1,
                          allow_small_or_imprecise_dtypes=True).then_inc(*ready.step("dist"))
                pool.wait_ge(ready.sem, ready.so_far())
                pool.affine_select(out=dist[:], in_=dist[:], compare_op=ALU.is_ge, fill=HIDDEN * 256,
                                   base=T - P, pattern=[[-1, T]], channel_multiplier=1).then_inc(*ready.step("masked"))
                pool.wait_ge(ready.sem, ready.so_far())

            @block.vector
            def _(dve):
                dve.sem_inc(biased.sem, biased.start)
                dve.sem_inc(softened.sem, softened.start)
                dve.wait_ge(ready.sem, ready.value("masked"))
                for h in range(H):
                    dve.tensor_scalar(bias[:, h, :], dist[:], 2.0 ** (-8.0 * (h + 1) / H), None,
                                      ALU.mult).then_inc(*biased.step(f"slope{h}"))
                dve.wait_ge(biased.sem, biased.so_far())

                def bias_and_max(u):
                    b, h = units[u]
                    n, par = (b + 1) * P, u % 2
                    dve.wait_ge(scored.sem, scored.value("unit", u))
                    softened.round()
                    for c in range(2):
                        if u >= 2 and c == 0:
                            dve.wait_ge(turned.sem, turned.value("unit", u - 2))
                        dve.tensor_tensor_reduce(
                            score[:, par, c, 0:n], scores[:, c, 0:n], bias[:, h, T - n:T], 1.0, -3.0e38,
                            ALU.add, ALU.max, high[:, par, c:c + 1]).then_inc(*softened.step(f"bias{c}"))
                    dve.wait_ge(softened.sem, softened.so_far(u))
                    dve.tensor_scalar(high[:, par, :], high[:, par, :], -1.0, None, ALU.mult).then_inc(*softened.step("negate"))

                def mix(u):
                    b, h = units[u]
                    n, par = (b + 1) * P, u % 2
                    dve.wait_ge(raised.sem, raised.value("exp1", u))
                    dve.reciprocal(weight[:, par, :], total[:, par, :]).then_inc(*softened_mix.step("recip"))
                    dve.wait_ge(softened_mix.sem, softened_mix.so_far(u))
                    dve.tensor_scalar(weight[:, par, 1:2], weight[:, par, 1:2], C.lam[:, 0:1], -1.0,
                                      ALU.mult, ALU.mult).then_inc(*softened_mix.step("lambda"))
                    dve.tensor_scalar(score[:, par, 0, 0:n], score[:, par, 0, 0:n],
                                      weight[:, par, 0:1], None, ALU.mult).then_inc(*softened_mix.step("scale"))
                    dve.wait_ge(softened_mix.sem, softened_mix.so_far(u))
                    dve.scalar_tensor_tensor(score[:, par, 0, 0:n], score[:, par, 1, 0:n],
                                             weight[:, par, 1:2], score[:, par, 0, 0:n],
                                             ALU.mult, ALU.add).then_inc(*softened_mix.step("mix"))
                dve.sem_inc(softened_mix.sem, softened_mix.start)
                for u in range(N + 1):
                    if u < N:
                        bias_and_max(u)
                    if u >= 1:
                        softened_mix.round()
                        mix(u - 1)
                dve.sem_inc(normed.sem, normed.start)
                dve.sem_inc(scaled.sem, scaled.start)
                dve.tensor_scalar(gain[:], C.vector["subln_g"], 1.0 - LAMBDA_INIT, None, ALU.mult).then_inc(*normed.step("gain"))
                dve.wait_ge(taken.sem, taken.end(N))
                dve.tensor_scalar(mean, sums, 1.0 / P, EPS, ALU.mult, ALU.add).then_inc(*normed.step("mean"))
                dve.wait_ge(rooted, 1)
                dve.reciprocal(rstd, mean).then_inc(*normed.step("rstd"))
                dve.wait_ge(normed.sem, normed.so_far())
                for b in range(B):
                    scaled.round()
                    part = heads[:, b, :].rearrange("p (h n) -> p h n", h=H)
                    dve.tensor_tensor(part, part, rstd[:, b * H:(b + 1) * H].unsqueeze(2)
                                      .to_broadcast([P, H, P]), ALU.mult).then_inc(*scaled.step("block"))
                dve.wait_ge(scaled.sem, scaled.end(B))

            @block.scalar
            def _(act):
                act.sem_inc(raised.sem, raised.start)
                act.sem_inc(copied.sem, copied.start)
                act.sem_inc(stored.sem, stored.start)

                def raise_(u):
                    b, h = units[u]
                    n, par = (b + 1) * P, u % 2
                    act.wait_ge(softened.sem, softened.value("negate", u))
                    raised.round()
                    for c in range(2):
                        act.wait_ge(raised.sem, raised.so_far(u))
                        act.activation(score[:, par, c, 0:n], score[:, par, c, 0:n], ACT.Exp,
                                       bias=high[:, par, c:c + 1],
                                       accum_out=total[:, par, c:c + 1]).then_inc(*raised.step(f"exp{c}"))

                def copy_weights(u):
                    b, h = units[u]
                    n = (b + 1) * P
                    act.wait_ge(turned.sem, turned.value("unit", u))
                    act.wait_ge(valued.sem, valued.value("unit", u - 2))
                    act.copy(flipT[:, u % 2, 0:n], flipped[:, 0:n]).then_inc(*copied.step("weights"))

                def take_values(u):
                    b, h = units[u]
                    taken.round()
                    act.wait_ge(valued.sem, valued.value("unit", u))
                    act.copy(heads[:, b, h * P:(h + 1) * P], values[:, u % 2, 0:P]).then_inc(*taken.step("values"))
                    act.wait_ge(taken.sem, taken.so_far(u))
                    act.activation(square[:, u % 2, :], heads[:, b, h * P:(h + 1) * P], ACT.Square,
                                   accum_out=sums[:, u:u + 1]).then_inc(*taken.step("square"))
                act.sem_inc(taken.sem, taken.start)
                for u in range(N + 2):
                    if u < N:
                        raise_(u)
                    if u >= 2:
                        take_values(u - 2)
                    if 1 <= u <= N:
                        copy_weights(u - 1)
                act.wait_ge(normed.sem, normed.value("mean"))
                act.activation(mean, mean, ACT.Sqrt).then_inc(rooted, 1)
                for b in range(B):
                    act.wait_ge(crossed.sem, crossed.value("block", b))
                    if b == 0:
                        act.wait_ge(normed.sem, normed.value("gain"))
                    act.activation(oT[:, :, b * P:(b + 1) * P],
                                   flipped[:, (b % 2) * 512:(b % 2 + 1) * 512]
                                   .rearrange("p (h n) -> p h n", h=H),
                                   ACT.Copy, scale=gain[:, 0:1]).then_inc(*stored.step("block"))
                act.wait_ge(stored.sem, stored.end(B))

            @block.tensor
            def _(pe):
                pe.sem_inc(scored.sem, scored.start)
                pe.sem_inc(turned.sem, turned.start)
                pe.sem_inc(valued.sem, valued.start)
                pe.sem_inc(crossed.sem, crossed.start)

                def score_unit(u):
                    b, h = units[u]
                    n = (b + 1) * P
                    pe.wait_ge(softened.sem, softened.value("bias1", u - 1))
                    for c in range(2):
                        rows = slice(64 * c, 64 * c + 64)
                        for at in range(0, n, 512):
                            to = min(n, at + 512)
                            ins = pe.matmul(scores[:, c, at:to], q[rows, h, b * P:(b + 1) * P], k[rows, h, at:to],
                                            start=True, stop=True)
                    ins.then_inc(*scored.step("unit"))

                def turn_unit(u):
                    b, h = units[u]
                    pe.wait_ge(softened_mix.sem, softened_mix.value("mix", u))
                    pe.wait_ge(copied.sem, copied.value("weights", u - 1))
                    for j in range(b + 1):
                        ins = pe.transpose(flipped[:, j * P:(j + 1) * P], score[:, u % 2, 0, j * P:(j + 1) * P],
                                           C.ident[:])
                    ins.then_inc(*turned.step("unit"))

                def apply_unit(u):
                    b, h = units[u]
                    pe.wait_ge(copied.sem, copied.value("weights", u))
                    pe.wait_ge(taken.sem, taken.value("values", u - 2))
                    for j in range(b + 1):
                        ins = pe.matmul(values[:, u % 2, 0:P], flipT[:, u % 2, j * P:(j + 1) * P],
                                        v[:, j, h * P:(h + 1) * P], start=(j == 0), stop=(j == b))
                    ins.then_inc(*valued.step("unit"))
                for u in range(N + 2):
                    if u < N:
                        score_unit(u)
                    if u >= 2:
                        apply_unit(u - 2)
                    if 1 <= u <= N:
                        turn_unit(u - 1)
                for b in range(B):
                    pe.wait_ge(scaled.sem, scaled.value("block", b))
                    pe.wait_ge(stored.sem, stored.value("block", b - 2))
                    for h in range(H):
                        ins = pe.transpose(flipped[:, (b % 2) * 512 + h * P:(b % 2) * 512 + (h + 1) * P],
                                           heads[:, b, h * P:(h + 1) * P], C.ident[:])
                    ins.then_inc(*crossed.step("block"))


def rwkv_low_rank(nc, I, hT, u, sig, a, gate, C):
    T = 1024
    with ExitStack() as ctx:
        S = scope(nc, ctx, "lora")
        weights = S.sb("weights", [P, 8, 288])
        low = S.sb("low", [P, 3, T])
        up_wa = S.sb("up_wa", [P, 512])
        up_g = S.sb("up_g", [P, 512])
        up_g2 = S.sb("up_g2", [32, 512])
        keep_mu = S.sb("keep_mu", [P, 3])
        product = S.ps("product", [P, 2, T])
        raised = S.ps("raised", [P, 2, T])
        w_in, up_in = S.sem("w_in"), S.sem("up_in")
        kept = S.sem("kept")
        names = ["xwa", "xg", "xg2"]
        multiplied = S.steps("multiplied", names)
        copied = S.steps("copied", names)
        shifted = S.steps("shifted", [f"{n}_{what}" for n in names for what in ("first", "rest")])
        bent = S.steps("bent", names)
        lifted = S.steps("lifted", ["unit"], back=2)
        stored = S.steps("stored", ["unit"], back=2)
        rows = {"xwa": P, "xg": P, "xg2": 32}
        mu = {"xwa": C.vector["mu"][:, 12:13], "xg": C.vector["mu"][:, 13:14], "xg2": C.mu_tail[:]}
        with nc.Block() as block:
            @block.sync
            def _(sp):
                sp.dma_start(weights[:], I["w_in"][0][:, 1536:1824].rearrange("(k p) n -> p k n", p=P)).then_inc(w_in, 16)
                sp.dma_start(up_wa[0:64, :], I["w_decay_up"][0]).then_inc(up_in, 16)
                sp.dma_start(up_wa[64:128, :], I["w_iclr_up"][0]).then_inc(up_in, 16)
                sp.dma_start(up_g[:], I["w_gate_up"][0][0:P, :]).then_inc(up_in, 16)
                sp.dma_start(up_g2[:], I["w_gate_up"][0][P:160, :]).then_inc(up_in, 16)

            @block.tensor
            def _(pe):
                pe.sem_inc(multiplied.sem, multiplied.start)
                pe.sem_inc(lifted.sem, lifted.start)
                pe.wait_ge(w_in, 16)
                for n, name in enumerate(names):
                    if n == 2:
                        pe.wait_ge(shifted.sem, shifted.value("xwa_rest"))
                    for half in range(2):
                        for k in range(8):
                            ins = pe.matmul(product[0:rows[name], n % 2, half * 512:(half + 1) * 512],
                                            weights[:, k, n * P:n * P + rows[name]],
                                            hT[:, k, half * 512:(half + 1) * 512], start=(k == 0), stop=(k == 7))
                    ins.then_inc(*multiplied.step(name))
                pe.wait_ge(up_in, 64)
                pe.wait_ge(bent.sem, bent.value("xg2"))
                for n in range(12):
                    kind, ct = n // 4, n % 4
                    pe.wait_ge(stored.sem, stored.value("unit", n - 2))
                    cols = slice(ct * P, (ct + 1) * P)
                    for half in range(2):
                        to = raised[:, n % 2, half * 512:(half + 1) * 512]
                        at = slice(half * 512, (half + 1) * 512)
                        if kind < 2:
                            part = slice(64 * kind, 64 * kind + 64)
                            ins = pe.matmul(to, up_wa[part, cols], low[part, 0, at], start=True, stop=True)
                        else:
                            pe.matmul(to, up_g[:, cols], low[:, 1, at], start=True, stop=False)
                            ins = pe.matmul(to, up_g2[:, cols], low[0:32, 2, at], start=False, stop=True)
                    ins.then_inc(*lifted.step("unit"))

            @block.scalar
            def _(act):
                act.sem_inc(copied.sem, copied.start)
                act.sem_inc(bent.sem, bent.start)
                act.sem_inc(stored.sem, stored.start)
                act.wait_ge(kept, 2)
                for n, name in enumerate(names):
                    act.wait_ge(multiplied.sem, multiplied.value(name))
                    r = rows[name]
                    act.activation(low[0:r, n, :], product[0:r, n % 2, :], ACT.Copy,
                                   scale=keep_mu[0:r, n:n + 1]).then_inc(*copied.step(name))
                for n, name in enumerate(names):
                    act.wait_ge(shifted.sem, shifted.value(f"{name}_rest"))
                    r = 64 if n == 0 else rows[name]
                    act.activation(low[0:r, n, :], low[0:r, n, :], ACT.Tanh if n == 0 else ACT.Sigmoid).then_inc(*bent.step(name))
                for n in range(12):
                    kind, ct = n // 4, n % 4
                    act.wait_ge(lifted.sem, lifted.value("unit", n))
                    if kind < 2:
                        base = C.vector["w0" if kind == 0 else "a0"][:, ct:ct + 1]
                        ins = act.activation((sig, a)[kind][:, ct, :], raised[:, n % 2, :], ACT.Sigmoid, bias=base)
                    else:
                        ins = act.copy(gate[:, ct, :], raised[:, n % 2, :])
                    ins.then_inc(*stored.step("unit"))
                act.wait_ge(stored.sem, stored.end(12))

            @block.vector
            def _(dve):
                dve.tensor_scalar(keep_mu[:, 0:2], C.vector["mu"][:, 12:14], -1.0, 1.0, ALU.mult, ALU.add).then_inc(kept, 1)
                dve.tensor_scalar(keep_mu[0:32, 2:3], C.mu_tail[:], -1.0, 1.0, ALU.mult, ALU.add).then_inc(kept, 1)
                dve.sem_inc(shifted.sem, shifted.start)
                for n, name in enumerate(names):
                    dve.wait_ge(copied.sem, copied.value(name))
                    r = rows[name]
                    for what, lo, hi in (("first", 1, 512), ("rest", 512, T)):
                        dve.scalar_tensor_tensor(low[0:r, n, lo:hi], product[0:r, n % 2, lo - 1:hi - 1],
                                                 mu[name][0:r, :], low[0:r, n, lo:hi],
                                                 ALU.mult, ALU.add).then_inc(*shifted.step(f"{name}_{what}"))


def rwkv_keys(nc, u, a, sig, kkn, fall, blocks, C):
    T = 1024
    with ExitStack() as ctx:
        S = scope(nc, ctx, "keys")
        square = S.sb("square", [P, 2, T])
        root = S.sb("root", [P, 2, T])
        grow = S.sb("grow", [P, 2, T])
        restart = S.sb("restart", [P, T])
        other = S.sb("other", [P, 4])
        norm = S.ps("norm", [P, 2, T])
        made = S.steps("made", ["ones", "zeros", "other"])
        grown = S.sem("grown")
        squared = S.steps("squared", ["square"], back=2)
        summed = S.steps("summed", ["sum"], back=2)
        rooted = S.steps("rooted", ["root"], back=2)
        keyed = S.steps("keyed", ["scan", "grow", "k", "floor", "inverse", "kkn"])
        with nc.Block() as block:
            @block.scalar
            def _(act):
                act.sem_inc(squared.sem, squared.start)
                act.sem_inc(rooted.sem, rooted.start)
                for c in range(4):
                    if c >= 2:
                        act.wait_ge(summed.sem, summed.value("sum", c - 2))
                    act.activation(square[:, c % 2, :], u[:, 4 + c, :], ACT.Square,
                                   scale=C.vector["k_k"][:, c:c + 1]).then_inc(*squared.step("square"))
                for c in range(4):
                    act.wait_ge(summed.sem, summed.value("sum", c))
                    act.wait_ge(keyed.sem, keyed.value("kkn", c - 2)) if c >= 2 else None
                    act.activation(root[:, c % 2, :], norm[:, c % 2, :], ACT.Sqrt).then_inc(*rooted.step("root"))

            @block.tensor
            def _(pe):
                pe.sem_inc(summed.sem, summed.start)
                for c in range(4):
                    pe.wait_ge(squared.sem, squared.value("square", c))
                    pe.wait_ge(rooted.sem, rooted.value("root", c - 2))
                    for half in range(2):
                        ins = pe.matmul(norm[:, c % 2, half * 512:(half + 1) * 512], blocks[:],
                                        square[:, c % 2, half * 512:(half + 1) * 512], start=True, stop=True)
                    ins.then_inc(*summed.step("sum"))

            @block.vector
            def _(dve):
                dve.sem_inc(made.sem, made.start)
                dve.memset(restart[:], 1.0).then_inc(*made.step("ones"))
                dve.wait_ge(made.sem, made.so_far())
                dve.memset(restart[:].rearrange("p (c n) -> p c n", n=P)[:, :, 0:1], 0.0).then_inc(*made.step("zeros"))
                dve.tensor_scalar(other[:], C.vector["k_a"], -1.0, 1.0, ALU.mult, ALU.add).then_inc(*made.step("other"))
                dve.wait_ge(made.sem, made.so_far())
                dve.sem_inc(keyed.sem, keyed.start)
                for c in range(4):
                    keyed.round()
                    k = u[:, 4 + c, :]
                    dve.tensor_tensor_scan(fall[:, c, :], restart[:], sig[:, c, :], 0.0, ALU.mult, ALU.add).then_inc(*keyed.step("scan"))
                    if c >= 2:
                        dve.wait_ge(grown, c - 1)
                    dve.tensor_scalar(grow[:, c % 2, :], a[:, c, :], C.vector["k_a"][:, c:c + 1],
                                      other[:, c:c + 1], ALU.mult, ALU.add).then_inc(*keyed.step("grow"))
                    dve.wait_ge(keyed.sem, keyed.so_far(c))
                    dve.tensor_scalar(kkn[:, c, :], k, C.vector["k_k"][:, c:c + 1], None, ALU.mult).then_inc(*keyed.step("k"))
                    dve.wait_ge(keyed.sem, keyed.so_far(c))
                    dve.wait_ge(squared.sem, squared.value("square", c))
                    dve.wait_ge(rooted.sem, rooted.value("root", c))
                    dve.tensor_scalar(root[:, c % 2, :], root[:, c % 2, :], 1e-12, None, ALU.max).then_inc(*keyed.step("floor"))
                    dve.wait_ge(keyed.sem, keyed.so_far(c))
                    dve.reciprocal(root[:, c % 2, :], root[:, c % 2, :]).then_inc(*keyed.step("inverse"))
                    dve.wait_ge(keyed.sem, keyed.so_far(c))
                    dve.tensor_tensor(kkn[:, c, :], kkn[:, c, :], root[:, c % 2, :], ALU.mult).then_inc(*keyed.step("kkn"))
                    dve.wait_ge(keyed.sem, keyed.so_far(c))

            @block.gpsimd
            def _(pool):
                for c in range(4):
                    pool.wait_ge(keyed.sem, keyed.value("k", c))
                    pool.wait_ge(squared.sem, squared.value("square", c))
                    pool.tensor_tensor(u[:, 4 + c, :], u[:, 4 + c, :], grow[:, c % 2, :], ALU.mult).then_inc(grown, 1)
                    pool.wait_ge(grown, c + 1)


def rwkv_masks(nc, M):
    corr = M.sb("corr_mask", [P, 4, P], BF16)
    level = M.sb("level_mask", [P, 7, P], BF16)
    blocks = M.sb("head_blocks", [P, P])
    names = ["corr1", "corr2", "corr3", "corr4", "corr5", "zero", "b0", "b1", "b2"]
    made = M.steps("masks_made", names + [f"l{l}_{w}" for l in range(7) for w in ("one", "low", "high")])
    with nc.Block() as block:
        @block.gpsimd
        def _(pool):
            pool.sem_inc(made.sem, made.start)
            pool.memset(corr[:], 1.0).then_inc(*made.step("corr1"))
            for n in range(4):
                pool.wait_ge(made.sem, made.so_far())
                pool.affine_select(out=corr[:, n, :], in_=corr[:, n, :], compare_op=ALU.is_ge, fill=0.0,
                                   base=-1 if n % 2 == 0 else 0, pattern=[[1, P]], channel_multiplier=-1).then_inc(*made.step(f"corr{n + 2}"))
            pool.memset(level[:], 0.0).then_inc(*made.step("zero"))
            pool.memset(blocks[:], 0.0).then_inc(*made.step("b0"))
            pool.wait_ge(made.sem, made.so_far())
            pool.memset(blocks[0:64, 0:64], 1.0).then_inc(*made.step("b1"))
            pool.memset(blocks[64:128, 64:128], 1.0).then_inc(*made.step("b2"))
            for l in range(7):
                m, n = 2 ** l, P // 2 ** (l + 1)
                second = level[:, l, :].rearrange("p (b h r) -> p b h r", h=2, r=m)[:, :, 1, :]
                pool.wait_ge(made.sem, made.so_far())
                pool.memset(second, 1.0).then_inc(*made.step(f"l{l}_one"))
                pool.wait_ge(made.sem, made.so_far())
                pool.affine_select(out=second, in_=second, compare_op=ALU.is_ge, fill=0.0, base=0,
                                   pattern=[[-2 * m, n], [0, m]], channel_multiplier=1).then_inc(*made.step(f"l{l}_low"))
                pool.wait_ge(made.sem, made.so_far())
                pool.affine_select(out=second, in_=second, compare_op=ALU.is_ge, fill=0.0, base=m - 1,
                                   pattern=[[2 * m, n], [0, m]], channel_multiplier=-1).then_inc(*made.step(f"l{l}_high"))
            pool.wait_ge(made.sem, made.so_far())
    return corr, level, blocks


KAPPA = float(np.exp(-0.5))


def rwkv_chunks(nc, u, a, sig, kkn, fall, masks, outputs, C):
    corr_mask, level_mask, blocks = masks
    NCH, H, CT = 8, 8, 4
    LEVELS = 7
    with ExitStack() as ctx:
        S = scope(nc, ctx, "chunk")
        early = S.sb("early", [P, 2, CT, P])
        centre, lag = early[:, 0], early[:, 1]
        power = S.sb("power", [P, 3, CT, P])
        ar = S.sb("ar", [P, CT, 2, P])
        kc = S.sb("kc", [P, CT, P])
        bc = S.sb("bc", [P, CT, P])
        vc = S.sb("vc", [P, CT, P])
        rk = power[:, 2]
        edge = S.sb("edge", [P, 8])
        vkb = S.sb("vkb", [P, 3, 512])
        corr = S.sb("corr", [P, H, 4, P])
        part = S.sb("part", [P, H, P])
        inv = S.sb("inv", [P, H, P])
        invT = S.sb("invT", [P, H, P])
        prod = early[:].rearrange("p a c n -> p (a c) n")
        rhs = power[:, 0].rearrange("p c n -> p (c n)")
        sol = power[:, 1].rearrange("p c n -> p (c n)")
        state = S.sb("state", [P, CT, P])
        pairs = S.ps("pairs", [P, 2, 512])
        straight = S.ps("straight", [P, 2, 512])
        crossed = S.ps("crossed", [P, 2, 512])
        mixed = S.ps("mixed", [P, 2, 512])

        groups = range(2)
        level_names = [f"l{l}_{what}{g}" for l in range(1, LEVELS) for what in ("p", "q") for g in groups]
        pe_steps = S.steps("products", ["turn", "bonus"] + [f"corr{h}" for h in range(H)] +
                           ["l0_0", "l0_1", "rhs"] + level_names + ["solve", "state", "y"])
        act_steps = S.steps("act", ["exp_r", "exp_k", "exp_a", "exp_edge", "v", "k", "b", "rhs"] +
                            [f"l{l}_p{g}" for l in range(1, LEVELS) for g in groups] + ["solve", "y"])
        pool_steps = S.steps("pool", ["v"] + [f"part{l}" for l in range(LEVELS)])
        dve_steps = S.steps("vector", ["centre", "lag", "edge_end", "edge_mid", "b0", "r", "k", "b", "a", "rk0", "rk1",
                                       "state_in"] + [f"mask{h}" for h in range(H)] + ["bonus"] +
                            [f"l0_{w}{g}" for g in groups for w in ("t", "s")] +
                            [f"l{l}_{w}{g}" for l in range(1, LEVELS) for g in groups for w in ("s", "t")
                             if not (l == LEVELS - 1 and w == "s")] +
                            ["add0", "add1", "scale0", "scale1"])
        wiped = S.sem("wiped")
        wide = [P, CT, P]

        def channel(v):
            return v.unsqueeze(2).to_broadcast(wide)

        def half(x, l, n):
            return x.rearrange("p h (b two m) -> p h b two m", two=2, m=2 ** l)[:, :, :, n, :]

        def level(x, g, l):
            return x[:, g, 0:256].rearrange("p (h b m) -> p h b m", h=4, m=2 ** l)

        with nc.Block() as block:
            @block.gpsimd
            def _(pool):
                pool.sem_inc(pool_steps.sem, pool_steps.start)
                with pool.Fori(0, NCH) as i:
                    now = ds(i * P, P)
                    pool.wait_ge(dve_steps.sem, dve_steps.value("bonus", i - 1))
                    pool.wait_ge(pe_steps.sem, pe_steps.value("turn", i - 1))
                    pool.wait_ge(pool_steps.sem, pool_steps.so_far(i))
                    pool.tensor_copy(vc[:], u[:, 8:12, now]).then_inc(*pool_steps.step("v"))
                    pool.wait_ge(dve_steps.sem, dve_steps.value(f"mask{H - 1}", i))
                    for l in range(LEVELS):
                        if l >= 1:
                            pool.wait_ge(pe_steps.sem, pe_steps.value("l0_1" if l == 1 else f"l{l - 1}_p1", i))
                            if l == 1:
                                pool.wait_ge(dve_steps.sem, dve_steps.value("l0_s1", i))
                        pool.wait_ge(pool_steps.sem, pool_steps.so_far(i))
                        pool.tensor_tensor(
                            part[:], corr[:, :, 0, :],
                            level_mask[:, l, :].unsqueeze(1).to_broadcast([P, H, P]), ALU.mult).then_inc(*pool_steps.step(f"part{l}"))

            @block.scalar
            def _(act):
                act.sem_inc(act_steps.sem, act_steps.start)
                with act.Fori(0, NCH) as i:
                    act.wait_ge(dve_steps.sem, dve_steps.value("lag", i))
                    act.activation(power[:, 0], centre, ACT.Exp, scale=-KAPPA).then_inc(*act_steps.step("exp_r"))
                    act.activation(power[:, 1], centre, ACT.Exp, scale=KAPPA).then_inc(*act_steps.step("exp_k"))
                    act.activation(power[:, 2], lag, ACT.Exp, scale=-KAPPA).then_inc(*act_steps.step("exp_a"))
                    act.wait_ge(dve_steps.sem, dve_steps.value("edge_mid", i))
                    act.activation(edge[:], edge[:], ACT.Exp, scale=-KAPPA).then_inc(*act_steps.step("exp_edge"))
                    act.wait_ge(pe_steps.sem, pe_steps.value("turn", i))
                    for n, (name, source) in enumerate((("v", straight[:, 0, :]), ("k", straight[:, 1, :]),
                                                        ("b", crossed[:, 0, :]))):
                        act.copy(vkb[:, n, :], source).then_inc(*act_steps.step(name))
                    act.wait_ge(pe_steps.sem, pe_steps.value("rhs", i))
                    act.copy(rhs, mixed[:, 0, :]).then_inc(*act_steps.step("rhs"))
                    for l in range(1, LEVELS):
                        for g in groups:
                            act.wait_ge(pe_steps.sem, pe_steps.value(f"l{l}_p{g}", i))
                            act.copy(prod[:, g * 4:g * 4 + 4, :],
                                     pairs[:, g, :].rearrange("p (h n) -> p h n", n=P)).then_inc(*act_steps.step(f"l{l}_p{g}"))
                    act.wait_ge(pe_steps.sem, pe_steps.value("solve", i))
                    act.copy(sol, mixed[:, 1, :]).then_inc(*act_steps.step("solve"))
                    act.wait_ge(pe_steps.sem, pe_steps.value("y", i))
                    act.copy(outputs[:, :, ds(i * P, P)],
                             mixed[:, 0, :].rearrange("p (c n) -> p c n", n=P)).then_inc(*act_steps.step("y"))
                act.wait_ge(act_steps.sem, act_steps.end(NCH))

            @block.vector
            def _(dve):
                dve.sem_inc(dve_steps.sem, dve_steps.start)
                dve.memset(state[:], 0.0).then_inc(wiped, 1)
                dve.wait_ge(wiped, 1)
                with dve.Fori(0, NCH) as i:
                    now = ds(i * P, P)
                    mid = ds(i * P + 63, 1)
                    L, sg = fall[:, :, now], sig[:, :, now]
                    r, k, av, kk = u[:, 0:4, now], u[:, 4:8, now], a[:, :, now], kkn[:, :, now]
                    dve.wait_ge(dve_steps.sem, dve_steps.so_far(i))
                    dve.tensor_tensor(centre, L, fall[:, :, mid].to_broadcast(wide), ALU.subtract).then_inc(*dve_steps.step("centre"))
                    dve.wait_ge(dve_steps.sem, dve_steps.so_far(i))
                    dve.tensor_tensor(lag, centre, sg, ALU.subtract).then_inc(*dve_steps.step("lag"))
                    dve.tensor_copy(edge[:, 0:4], centre[:, :, P - 1:P].rearrange("p c a -> p (c a)")).then_inc(*dve_steps.step("edge_end"))
                    dve.tensor_copy(edge[:, 4:8], fall[:, :, mid].rearrange("p c a -> p (c a)")).then_inc(*dve_steps.step("edge_mid"))
                    dve.wait_ge(pe_steps.sem, pe_steps.value("y", i - 1))
                    dve.tensor_tensor(bc[:], kk, av, ALU.mult).then_inc(*dve_steps.step("b0"))
                    dve.wait_ge(act_steps.sem, act_steps.value("exp_edge", i))
                    dve.tensor_tensor(ar[:, :, 1, :], r, power[:, 0], ALU.mult).then_inc(*dve_steps.step("r"))
                    dve.tensor_tensor(kc[:], k, power[:, 1], ALU.mult).then_inc(*dve_steps.step("k"))
                    dve.wait_ge(dve_steps.sem, dve_steps.so_far(i))
                    dve.tensor_tensor(bc[:], bc[:], power[:, 1], ALU.mult).then_inc(*dve_steps.step("b"))
                    dve.scalar_tensor_tensor(ar[:, :, 0, :], kk, -1.0, power[:, 2], ALU.mult, ALU.mult).then_inc(*dve_steps.step("a"))
                    dve.wait_ge(dve_steps.sem, dve_steps.so_far(i))
                    dve.tensor_tensor(rk, r, k, ALU.mult).then_inc(*dve_steps.step("rk0"))
                    dve.wait_ge(dve_steps.sem, dve_steps.so_far(i))
                    dve.tensor_tensor(rk, rk, channel(C.vector["r_k"]), ALU.mult).then_inc(*dve_steps.step("rk1"))
                    dve.tensor_tensor(state[:], state[:], channel(edge[:, 4:8]), ALU.mult).then_inc(*dve_steps.step("state_in"))
                    for h in range(H):
                        dve.wait_ge(pe_steps.sem, pe_steps.value(f"corr{h}", i))
                        dve.tensor_tensor(corr[:, h], pairs[:, h % 2, :].rearrange("p (c n) -> p c n", n=P),
                                          corr_mask[:], ALU.mult).then_inc(*dve_steps.step(f"mask{h}"))
                    dve.wait_ge(pe_steps.sem, pe_steps.value("bonus", i))
                    dve.tensor_tensor(r, crossed[:, 1, :].rearrange("p (c n) -> p c n", n=P), vc[:],
                                      ALU.mult).then_inc(*dve_steps.step("bonus"))
                    eye = C.ident[:].unsqueeze(1).to_broadcast([P, 4, P])

                    def four(x, g):
                        return x[:, g * 4:g * 4 + 4, :]

                    def bank(x, g):
                        return x[:, g, :].rearrange("p (h n) -> p h n", n=P)
                    dve.wait_ge(pool_steps.sem, pool_steps.value("part0", i))
                    for g in groups:
                        dve.tensor_tensor(four(invT, g), four(part[:], g), eye, ALU.add).then_inc(*dve_steps.step(f"l0_t{g}"))
                        dve.wait_ge(pe_steps.sem, pe_steps.value(f"l0_{g}", i))
                        dve.tensor_tensor(four(inv, g), bank(straight, g), eye, ALU.add).then_inc(*dve_steps.step(f"l0_s{g}"))
                    for l in range(1, LEVELS):
                        for g in groups:
                            dve.wait_ge(pe_steps.sem, pe_steps.value(f"l{l}_q{g}", i))
                            if g == 0:
                                dve.wait_ge(dve_steps.sem, dve_steps.so_far(i))
                            if l < LEVELS - 1:
                                to = half(four(inv, g), l, 0)
                                dve.tensor_tensor(to, to, level(straight, g, l), ALU.add).then_inc(*dve_steps.step(f"l{l}_s{g}"))
                            to = half(four(invT, g), l, 1)
                            dve.tensor_tensor(to, to, level(crossed, g, l), ALU.add).then_inc(*dve_steps.step(f"l{l}_t{g}"))
                    dve.wait_ge(pe_steps.sem, pe_steps.value("state", i))
                    halves = [slice(0, 64), slice(64, 128)]
                    for n, part_ in enumerate(halves):
                        to = state[part_, :, part_]
                        dve.tensor_tensor(to, to, bank(pairs, 0)[part_, :, part_], ALU.add).then_inc(*dve_steps.step(f"add{n}"))
                    dve.wait_ge(dve_steps.sem, dve_steps.so_far(i))
                    for n, part_ in enumerate(halves):
                        to = state[part_, :, part_]
                        dve.tensor_tensor(to, to, edge[part_, 0:4].unsqueeze(2).to_broadcast([64, 4, 64]),
                                          ALU.mult).then_inc(*dve_steps.step(f"scale{n}"))
                dve.wait_ge(dve_steps.sem, dve_steps.end(NCH))

            @block.tensor
            def _(pe):
                pe.sem_inc(pe_steps.sem, pe_steps.start)
                with pe.Fori(0, NCH) as i:
                    pe.wait_ge(dve_steps.sem, dve_steps.value("state_in", i))
                    pe.wait_ge(pool_steps.sem, pool_steps.value("v", i))
                    for to, source in ((straight[:, 0, :], vc), (straight[:, 1, :], kc), (crossed[:, 0, :], bc)):
                        for c in range(CT):
                            ins = pe.transpose(to[:, c * P:(c + 1) * P], source[:, c, :], C.ident[:])
                    ins.then_inc(*pe_steps.step("turn"))
                    pe.matmul(crossed[:, 1, :], blocks[:], rk.rearrange("p c n -> p (c n)"),
                              start=True, stop=True).then_inc(*pe_steps.step("bonus"))
                    for h in range(H):
                        rows, c = slice(64 * (h % 2), 64 * (h % 2) + 64), h // 2
                        if h >= 2:
                            pe.wait_ge(dve_steps.sem, dve_steps.value(f"mask{h - 2}", i))
                        both = ar[rows, c, :, :].rearrange("p a n -> p (a n)")
                        pe.matmul(pairs[:, h % 2, 0:256], bc[rows, c, :], both, start=True, stop=False, skip_group_check=True)
                        pe.matmul(pairs[:, h % 2, 256:512], kc[rows, c, :], both, start=False, stop=True,
                                  skip_group_check=True).then_inc(*pe_steps.step(f"corr{h}"))
                    pe.wait_ge(act_steps.sem, act_steps.value("b", i))
                    pe.wait_ge(pool_steps.sem, pool_steps.value("part0", i))
                    for g in groups:
                        for j in range(4):
                            ins = pe.matmul(straight[:, g, j * P:(j + 1) * P], part[:, g * 4 + j, :], C.ident[:],
                                            start=(j == 0), stop=(j == 3), skip_group_check=True)
                        ins.then_inc(*pe_steps.step(f"l0_{g}"))
                    for c in range(CT):
                        pe.matmul(mixed[:, 0, c * P:(c + 1) * P], ar[:, c, 0, :], state[:, c, :], start=(c == 0),
                                  stop=False, skip_group_check=True)
                    for h in range(H):
                        ins = pe.matmul(mixed[:, 0, h * 64:(h + 1) * 64], corr[:, h, 2, :], vkb[:, 0, h * 64:(h + 1) * 64],
                                        start=False, stop=(h == H - 1), skip_group_check=True)
                    ins.then_inc(*pe_steps.step("rhs"))
                    for l in range(1, LEVELS):
                        pe.wait_ge(pool_steps.sem, pool_steps.value(f"part{l}", i))
                        for g in groups:
                            pe.wait_ge(dve_steps.sem, dve_steps.value(f"l{l - 1}_s{g}", i))
                            for j in range(4):
                                h = g * 4 + j
                                ins = pe.matmul(pairs[:, g, j * P:(j + 1) * P], part[:, h, :], inv[:, h, :],
                                                start=(j == 0), stop=(j == 3), skip_group_check=True)
                            ins.then_inc(*pe_steps.step(f"l{l}_p{g}"))
                        for g in groups:
                            pe.wait_ge(act_steps.sem, act_steps.value(f"l{l}_p{g}", i))
                            pe.wait_ge(dve_steps.sem, dve_steps.value(f"l{l - 1}_t{g}", i))
                            if l < LEVELS - 1:
                                for j in range(4):
                                    h = g * 4 + j
                                    pe.matmul(level(straight, g, l)[:, j], invT[:, h, :], half(prod[:, h:h + 1, :], l, 0)[:, 0],
                                              start=(j == 0), stop=(j == 3), skip_group_check=True)
                            for j in range(4):
                                h = g * 4 + j
                                ins = pe.matmul(level(crossed, g, l)[:, j], prod[:, h, :], half(invT[:, h:h + 1, :], l, 1)[:, 0],
                                                start=(j == 0), stop=(j == 3), skip_group_check=True)
                            ins.then_inc(*pe_steps.step(f"l{l}_q{g}"))
                    pe.wait_ge(act_steps.sem, act_steps.value("rhs", i))
                    pe.wait_ge(dve_steps.sem, dve_steps.value(f"l{LEVELS - 1}_t1", i))
                    for h in range(H):
                        cols = slice(h * 64, (h + 1) * 64)
                        ins = pe.matmul(mixed[:, 1, cols], invT[:, h, :], rhs[:, cols], start=(h == 0), stop=(h == H - 1),
                                        skip_group_check=True)
                    ins.then_inc(*pe_steps.step("solve"))
                    for c in range(CT):
                        cols = slice(c * P, (c + 1) * P)
                        pe.matmul(pairs[:, 0, cols], vkb[:, 1, cols], vkb[:, 0, cols], start=(c == 0), stop=False,
                                  skip_group_check=True)
                    for c in range(CT):
                        pe.matmul(mixed[:, 0, c * P:(c + 1) * P], ar[:, c, 1, :], state[:, c, :], start=(c == 0),
                                  stop=False, skip_group_check=True)
                    for h in range(H):
                        cols = slice(h * 64, (h + 1) * 64)
                        pe.matmul(mixed[:, 0, cols], corr[:, h, 3, :], vkb[:, 0, cols], start=False, stop=False,
                                  skip_group_check=True)
                    pe.wait_ge(act_steps.sem, act_steps.value("solve", i))
                    for c in range(CT):
                        cols = slice(c * P, (c + 1) * P)
                        ins = pe.matmul(pairs[:, 0, cols], vkb[:, 2, cols], sol[:, cols], start=False, stop=(c == CT - 1),
                                        skip_group_check=True)
                    ins.then_inc(*pe_steps.step("state"))
                    for h in range(H):
                        cols = slice(h * 64, (h + 1) * 64)
                        ins = pe.matmul(mixed[:, 0, cols], corr[:, h, 1, :], sol[:, cols], start=False,
                                        stop=(h == H - 1), skip_group_check=True)
                    ins.then_inc(*pe_steps.step("y"))


def rwkv_outputs(nc, centred, squared, bonus, gate, C):
    with ExitStack() as ctx:
        S = scope(nc, ctx, "routs")
        rstd = S.sb("rstd", [P, 64])
        rows = S.sb("rows", [P, 2, 512])
        cols = S.sb("cols", [P, 2, 4, P])
        flipped = S.ps("flipped", [P, 2, 512])
        pair = ["even", "odd"]
        mean, variance = S.sb("mean", [P, 64]), S.sb("variance", [P, 64])
        stats = S.steps("stats", ["sum", "mean", "subtract", "squares", "var", "rstd"])
        made_squares, rooted = S.sem("made_squares"), S.sem("rooted")
        scaled = S.steps("scaled", pair)
        turned = S.steps("turned", pair)
        gained = S.steps("gained", [f"{j}{c}" for j in pair for c in range(4)])
        gated = S.steps("gated", [j + w for j in pair for w in ("_add", "_gate")])
        with nc.Block() as block:
            @block.vector
            def _(dve):
                dve.sem_inc(stats.sem, stats.start)
                dve.sem_inc(scaled.sem, scaled.start)
                dve.sem_inc(gated.sem, gated.start)
                y = centred.rearrange("p c (g n) -> p c g n", n=64)
                dve.tensor_reduce(mean[:].rearrange("p (c g) -> p c g", c=4), y, AX, ALU.add).then_inc(*stats.step("sum"))
                dve.wait_ge(stats.sem, stats.so_far())
                dve.tensor_scalar(mean[:], mean[:], 1.0 / 64, None, ALU.mult).then_inc(*stats.step("mean"))
                dve.wait_ge(stats.sem, stats.so_far())
                dve.tensor_tensor(y, y, mean[:].rearrange("p (c g) -> p c g", c=4).unsqueeze(3).to_broadcast([P, 4, 16, 64]),
                                  ALU.subtract).then_inc(*stats.step("subtract"))
                dve.wait_ge(made_squares, 1)
                dve.tensor_reduce(variance[:].rearrange("p (c g) -> p c g", c=4), squared.rearrange("p c (g n) -> p c g n", n=64),
                                  AX, ALU.add).then_inc(*stats.step("squares"))
                dve.wait_ge(stats.sem, stats.so_far())
                dve.tensor_scalar(variance[:], variance[:], 1.0 / 64, 64e-5, ALU.mult, ALU.add).then_inc(*stats.step("var"))
                dve.wait_ge(rooted, 1)
                dve.reciprocal(rstd[:], variance[:]).then_inc(*stats.step("rstd"))
                dve.wait_ge(stats.sem, stats.so_far())
                with dve.Fori(0, 4) as i:
                    for j in range(2):
                        t = 2 * i + j
                        dve.wait_ge(turned.sem, turned.value(pair[j], i - 1))
                        dve.tensor_tensor(
                            rows[:, j, :].rearrange("p (c h n) -> p c h n", h=2, n=64),
                            centred[:, :, ds(t * P, P)].rearrange("p c (h n) -> p c h n", n=64),
                            rstd[:].rearrange("p (c g) -> p c g", c=4)[:, :, ds(2 * t, 2)].unsqueeze(3).to_broadcast([P, 4, 2, 64]),
                            ALU.mult).then_inc(*scaled.step(pair[j]))
                    for j in range(2):
                        now = ds((2 * i + j) * P, P)
                        dve.wait_ge(gained.sem, gained.value(f"{pair[j]}3", i))
                        dve.tensor_tensor(cols[:, j], cols[:, j], bonus[:, :, now], ALU.add).then_inc(*gated.step(pair[j] + "_add"))
                        dve.wait_ge(gated.sem, gated.so_far(i))
                        dve.tensor_tensor(gate[:, :, now], cols[:, j], gate[:, :, now], ALU.mult).then_inc(*gated.step(pair[j] + "_gate"))
                dve.wait_ge(gated.sem, gated.end(4))

            @block.scalar
            def _(act):
                act.sem_inc(gained.sem, gained.start)
                act.wait_ge(stats.sem, stats.value("subtract"))
                act.activation(squared, centred, ACT.Square).then_inc(made_squares, 1)
                act.wait_ge(stats.sem, stats.value("var"))
                act.activation(variance[:], variance[:], ACT.Sqrt).then_inc(rooted, 1)
                with act.Fori(0, 4) as i:
                    for j in range(2):
                        act.wait_ge(turned.sem, turned.value(pair[j], i))
                        act.wait_ge(gated.sem, gated.value(pair[j] + "_gate", i - 1))
                        for c in range(4):
                            act.activation(cols[:, j, c, :], flipped[:, j, c * P:(c + 1) * P], ACT.Identity,
                                           bias=C.vector["lnx_b"][:, c:c + 1],
                                           scale=C.vector["lnx_g"][:, c:c + 1]).then_inc(*gained.step(f"{pair[j]}{c}"))

            @block.tensor
            def _(pe):
                pe.sem_inc(turned.sem, turned.start)
                with pe.Fori(0, 4) as i:
                    for j in range(2):
                        pe.wait_ge(scaled.sem, scaled.value(pair[j], i))
                        pe.wait_ge(gained.sem, gained.value(f"{pair[j]}3", i - 1))
                        for c in range(4):
                            ins = pe.transpose(flipped[:, j, c * P:(c + 1) * P], rows[:, j, c * P:(c + 1) * P], C.ident[:])
                        ins.then_inc(*turned.step(pair[j]))


def add_projection(nc, name, lhs, w, x, load=None):
    D = 1024
    with ExitStack() as ctx:
        S = scope(nc, ctx, name)
        weights = S.sb("weights", [P, 8, D])
        product = S.ps("product", [P, 3, D])
        w_in = [S.sem(f"w_in{j}") for j in range(2)]
        x_in = S.sem("x_in")
        multiplied = S.steps("multiplied", ["tile"], back=3)
        added = S.steps("added", ["tile"], back=3)
        with nc.Block() as block:
            @block.sync
            def _(sp):
                for j in range(2):
                    sp.dma_start(weights[:, 4 * j:4 * j + 4, :], w[j * 512:(j + 1) * 512, :]
                                 .rearrange("(k p) n -> p k n", p=P)).then_inc(w_in[j], 16)
                if load is not None:
                    sp.dma_start(x[:].rearrange("p (t n) -> p t n", n=D),
                                 load.rearrange("(t p) n -> p t n", p=P)).then_inc(x_in, 16)

            @block.tensor
            def _(pe):
                pe.sem_inc(multiplied.sem, multiplied.start)
                for t in range(8):
                    pe.wait_ge(added.sem, added.value("tile", t - 3))
                    for half in range(2):
                        for k in range(8):
                            if t == 0 and half == 0 and k % 4 == 0:
                                pe.wait_ge(w_in[k // 4], 16)
                            ins = pe.matmul(product[:, t % 3, half * 512:(half + 1) * 512], lhs[:, k, t * P:(t + 1) * P],
                                            weights[:, k, half * 512:(half + 1) * 512], start=(k == 0), stop=(k == 7))
                    ins.then_inc(*multiplied.step("tile"))

            @block.vector
            def _(dve):
                dve.sem_inc(added.sem, added.start)
                if load is not None:
                    dve.wait_ge(x_in, 16)
                for t in range(8):
                    dve.wait_ge(multiplied.sem, multiplied.value("tile", t))
                    rows = x[:, t * D:(t + 1) * D]
                    dve.tensor_tensor(rows, rows, product[:, t % 3, :], ALU.add).then_inc(*added.step("tile"))
                dve.wait_ge(added.sem, added.end(8))


def cross_keys_values(nc, w, memT, kT, v):
    with ExitStack() as ctx:
        S = scope(nc, ctx, "ckv")
        weights = S.sb("weights", [P, 2, 8, 512])
        product = S.ps("product", [P, 2, 512])
        w_in = [S.sem(f"w_in{j}") for j in range(2)]
        parts = [("k", n) for n in range(4)] + [("v", n) for n in range(4)]
        multiplied = S.steps("multiplied", ["part"], back=2)
        copied = S.steps("copied", ["part"], back=2)
        with nc.Block() as block:
            @block.sync
            def _(sp):
                for j in range(4):
                    if j >= 2:
                        sp.wait_ge(multiplied.sem, multiplied.value("part", 2 * (j - 2) + 1))
                    sp.dma_start(weights[:, j % 2], w[:, j * 512:(j + 1) * 512]
                                 .rearrange("(k p) n -> p k n", p=P)).then_inc(w_in[j % 2], 16)

            @block.tensor
            def _(pe):
                pe.sem_inc(multiplied.sem, multiplied.start)
                for n, (kind, m) in enumerate(parts):
                    slot = (n // 2) % 2
                    if n % 2 == 0:
                        pe.wait_ge(w_in[slot], 16 * (n // 4 + 1))
                    pe.wait_ge(copied.sem, copied.value("part", n - 2))
                    for c in range(2 if kind == "k" else 1):
                        for k in range(8):
                            if kind == "k":
                                col = (2 * m + c) % 4 * P
                                ins = pe.matmul(product[:, n % 2, c * 256:(c + 1) * 256],
                                                weights[:, slot, k, col:col + P], memT[:, k, :],
                                                start=(k == 0), stop=(k == 7))
                            else:
                                ins = pe.matmul(product[:, n % 2, :], memT[:, k, (m % 2) * P:(m % 2 + 1) * P],
                                                weights[:, slot, k, :], start=(k == 0), stop=(k == 7))
                    ins.then_inc(*multiplied.step("part"))

            @block.scalar
            def _(act):
                act.sem_inc(copied.sem, copied.start)
                for n, (kind, m) in enumerate(parts):
                    act.wait_ge(multiplied.sem, multiplied.value("part", n))
                    to = (kT[:, 2 * m:2 * m + 2, :].rearrange("p c n -> p (c n)") if kind == "k"
                          else v[:, m % 2, (m // 2) * 512:(m // 2 + 1) * 512])
                    act.copy(to, product[:, n % 2, :]).then_inc(*copied.step("part"))
                act.wait_ge(copied.sem, copied.end(len(parts)))


def cross_attention(nc, qT, kT, v, oT, C):
    H, M = 4, 256
    with ExitStack() as ctx:
        S = scope(nc, ctx, "cross")
        prob = S.sb("prob", [P, 2, H * M])
        probT = S.sb("probT", [P, 2 * H, P])
        high = S.sb("high", [P, 2, H])
        total = S.sb("total", [P, 2, H])
        scores = S.ps("scores", [P, 2, H * M])
        flipped = S.ps("flipped", [P, 2 * H, P])
        mixed = S.ps("mixed", [P, 8, P])
        scored = S.steps("scored", ["tile"])
        turned = S.steps("turned", ["tile"])
        valued = S.steps("valued", ["tile"])
        topped = S.steps("topped", ["max", "negate"], back=2)
        raised = S.steps("raised", [f"exp{h}" for h in range(H)], back=2)
        divided = S.steps("divided", ["reciprocal", "divide"], back=2)
        copied = S.steps("copied", ["weights"])
        stored = S.steps("stored", ["tile"])
        with nc.Block() as block:
            @block.tensor
            def _(pe):
                for s in (scored, turned, valued):
                    pe.sem_inc(s.sem, s.start)

                def score(t):
                    pe.wait_ge(raised.sem, raised.value(f"exp{H - 1}", t - 2))
                    for h in range(H):
                        for c in range(2):
                            ins = pe.matmul(scores[:, t % 2, h * M:(h + 1) * M], qT[:, 2 * h + c, t * P:(t + 1) * P],
                                            kT[:, 2 * h + c, :], start=(c == 0), stop=(c == 1))
                    ins.then_inc(*scored.step("tile"))

                def apply(t):
                    pe.wait_ge(divided.sem, divided.value("divide", t))
                    pe.wait_ge(copied.sem, copied.value("weights", t - 1))
                    for n in range(2 * H):
                        ins = pe.transpose(flipped[:, n, :], prob[:, t % 2, n * P:(n + 1) * P], C.ident[:])
                    ins.then_inc(*turned.step("tile"))
                    pe.wait_ge(copied.sem, copied.value("weights", t))
                    pe.wait_ge(stored.sem, stored.value("tile", t - 1))
                    for n in range(8):
                        for m in range(2):
                            ins = pe.matmul(mixed[:, n, :], v[:, m, n * P:(n + 1) * P], probT[:, n // 2 * 2 + m, :],
                                            start=(m == 0), stop=(m == 1))
                    ins.then_inc(*valued.step("tile"))
                for t in range(9):
                    if t < 8:
                        score(t)
                    if t >= 1:
                        apply(t - 1)

            @block.vector
            def _(dve):
                for s in (topped, divided, stored):
                    dve.sem_inc(s.sem, s.start)

                def top(t):
                    dve.wait_ge(scored.sem, scored.value("tile", t))
                    topped.round()
                    dve.wait_ge(raised.sem, raised.value(f"exp{H - 1}", t - 2))
                    dve.wait_ge(topped.sem, topped.so_far(t))
                    dve.tensor_reduce(high[:, t % 2, :], scores[:, t % 2, :].rearrange("p (h m) -> p h m", h=H),
                                      AX, ALU.max).then_inc(*topped.step("max"))
                    dve.wait_ge(topped.sem, topped.so_far(t))
                    dve.tensor_scalar(high[:, t % 2, :], high[:, t % 2, :], -1.0, None, ALU.mult).then_inc(*topped.step("negate"))

                def divide(t):
                    dve.wait_ge(raised.sem, raised.value(f"exp{H - 1}", t))
                    divided.round()
                    dve.reciprocal(total[:, t % 2, :], total[:, t % 2, :]).then_inc(*divided.step("reciprocal"))
                    dve.wait_ge(divided.sem, divided.so_far(t))
                    part = prob[:, t % 2, :].rearrange("p (h m) -> p h m", h=H)
                    dve.tensor_tensor(part, part, total[:, t % 2, :].unsqueeze(2).to_broadcast([P, H, M]),
                                      ALU.mult).then_inc(*divided.step("divide"))

                def store(t):
                    dve.wait_ge(valued.sem, valued.value("tile", t))
                    dve.tensor_copy(oT[:, :, t * P:(t + 1) * P], mixed[:]).then_inc(*stored.step("tile"))
                for t in range(9):
                    if t < 8:
                        top(t)
                    if t >= 2:
                        store(t - 2)
                    if t >= 1:
                        divide(t - 1)
                store(7)
                dve.wait_ge(stored.sem, stored.end(8))

            @block.scalar
            def _(act):
                act.sem_inc(raised.sem, raised.start)
                act.sem_inc(copied.sem, copied.start)
                for t in range(9):
                    if t < 8:
                        act.wait_ge(topped.sem, topped.value("negate", t))
                        act.wait_ge(turned.sem, turned.value("tile", t - 2)) if t >= 2 else None
                        act.wait_ge(divided.sem, divided.value("divide", t - 2))
                        for h in range(H):
                            cols = slice(h * M, (h + 1) * M)
                            act.activation(prob[:, t % 2, cols], scores[:, t % 2, cols], ACT.Exp,
                                           bias=high[:, t % 2, h:h + 1],
                                           accum_out=total[:, t % 2, h:h + 1]).then_inc(*raised.step(f"exp{h}"))
                    if t >= 1:
                        act.wait_ge(turned.sem, turned.value("tile", t - 1))
                        act.wait_ge(valued.sem, valued.value("tile", t - 2))
                        act.copy(probT[:], flipped[:]).then_inc(*copied.step("weights"))


NE, TOPK, T_ALL = 32, 4, 1024
WINDOW = 176
WINDOWS = NE + NE // 8 * T_ALL // WINDOW
ROWS = -(-(WINDOWS + 2) * WINDOW // P) * P


def route(nc, I, hT, row_token, R, C):
    TT = 8
    with ExitStack() as ctx:
        S = scope(nc, ctx, "route")
        weights = S.sb("weights", [P, 8, NE])
        base = S.sb("base", [P, NE])
        logits = S.sb("logits", [P, TT, NE])
        best = S.sb("best", [P, TT, 8])
        index = S.sb("index", [P, TT, 8], U32)
        index_f = S.sb("index_f", [P, TT, TOPK])
        number = S.sb("number", [P, NE])
        chosen = S.sb("chosen", [P, TT, TOPK, NE])
        member = S.sb("member", [P, TT, NE])
        before = S.sb("before", [P, TT + 1, NE])
        earlier = S.sb("earlier", [P, P])
        ones = S.sb("ones", [P, P])
        rank = S.sb("rank", [P, TT, NE])
        place = S.sb("place", [P, TT, NE])
        spot = S.sb("spot", [P, TT, TOPK, NE])
        dest = S.sb("dest", [P, TT * TOPK])
        token = S.sb("token", [P, TT], I32)
        zeros = S.sb("zeros", [P, ROWS // P], I32)
        blocks = S.sb("blocks", [P, NE])
        blocks_i = S.sb("blocks_i", [P, NE], I32)
        first = S.sb("first", [P, NE + 2])
        lead = S.sb("lead", [P, TT])
        total = S.sb("total", [P, TT])
        product = S.ps("product", [P, TT * NE])
        counted = S.ps("counted", [P, 2, 512])
        w_in, base_in, cleared, scattered = S.sem("w_in"), S.sem("base_in"), S.sem("cleared"), S.sem("scattered")
        made = S.steps("made", ["zeros", "number", "token", "ones", "earlier", "triangle"])
        multiplied = S.steps("multiplied", ["logits", "rank", "count"])
        raised = S.sem("raised")
        names = (["logits"] + [f"{w}{t}" for t in range(TT) for w in ("best", "index")] +
                 ["float", "lead", "chosen", "member", "none"] + [f"before{t}" for t in range(TT)] +
                 ["rank", "round", "int", "least", "zero", "scan", "start", "place", "spot", "dest", "row",
                  "unused", "first", "gate_sum", "gate_inverse", "gate"])
        sorted_ = S.steps("sorted", names)
        with nc.Block() as block:
            @block.gpsimd
            def _(pool):
                pool.sem_inc(made.sem, made.start)
                pool.memset(zeros[:], 0).then_inc(*made.step("zeros"))
                pool.wait_ge(made.sem, made.so_far())
                pool.iota(number[:], pattern=[[1, NE]], base=0, channel_multiplier=0,
                          allow_small_or_imprecise_dtypes=True).then_inc(*made.step("number"))
                pool.wait_ge(made.sem, made.so_far())
                pool.iota(token[:], pattern=[[P, TT]], base=0, channel_multiplier=1).then_inc(*made.step("token"))
                pool.wait_ge(made.sem, made.so_far())
                pool.memset(ones[:], 1.0).then_inc(*made.step("ones"))
                pool.wait_ge(made.sem, made.so_far())
                pool.memset(earlier[:], 1.0).then_inc(*made.step("earlier"))
                pool.wait_ge(made.sem, made.so_far())
                pool.affine_select(out=earlier[:], in_=earlier[:], compare_op=ALU.is_ge, fill=0.0,
                                   base=-1, pattern=[[1, P]], channel_multiplier=-1).then_inc(*made.step("triangle"))
                pool.wait_ge(cleared, 16)
                pool.wait_ge(sorted_.sem, sorted_.value("row"))
                for n in range(TT * TOPK):
                    pool.indirect_dma_start(row_token, bass.IndirectOffsetOnAxis(ap=R.row[:, n:n + 1], axis=0),
                                            token[:, n // TOPK:n // TOPK + 1], None).then_inc(scattered, 16)
                pool.wait_ge(scattered, 16 * TT * TOPK)

            @block.sync
            def _(sp):
                sp.dma_start(weights[:], I["w_router"][0].rearrange("(k p) n -> p k n", p=P)).then_inc(w_in, 16)
                sp.dma_start(base[:], row_to_all(I["b_router"][0])).then_inc(base_in, 16)
                sp.wait_ge(made.sem, made.value("zeros"))
                sp.dma_start(row_token.rearrange("(p n) a -> p (n a)", p=P), zeros[:]).then_inc(cleared, 16)

            @block.tensor
            def _(pe):
                pe.sem_inc(multiplied.sem, multiplied.start)
                pe.wait_ge(w_in, 16)
                for t in range(TT):
                    for k in range(8):
                        ins = pe.matmul(product[:, t * NE:(t + 1) * NE], hT[:, k, t * P:(t + 1) * P], weights[:, k, :],
                                        start=(k == 0), stop=(k == 7))
                ins.then_inc(*multiplied.step("logits"))
                pe.wait_ge(sorted_.sem, sorted_.value(f"before{TT - 1}"))
                pe.wait_ge(made.sem, made.value("triangle"))
                pe.matmul(counted[:, 0, 0:TT * NE], earlier[:], member[:].rearrange("p t e -> p (t e)"), start=True, stop=False)
                pe.matmul(counted[:, 0, 0:TT * NE], ones[:],
                          before[:, 0:TT, :].rearrange("p t e -> p (t e)"), start=False, stop=True).then_inc(*multiplied.step("rank"))
                pe.matmul(counted[:, 1, 0:NE], ones[:], before[:, TT, :], start=True, stop=True).then_inc(*multiplied.step("count"))

            @block.scalar
            def _(act):
                act.wait_ge(sorted_.sem, sorted_.value("lead"))
                act.activation(R.gate[:], R.gate[:], ACT.Exp).then_inc(raised, 1)

            @block.vector
            def _(dve):
                dve.sem_inc(sorted_.sem, sorted_.start)
                dve.wait_ge(base_in, 16)
                dve.wait_ge(multiplied.sem, multiplied.value("logits"))
                dve.tensor_tensor(logits[:], product[:].rearrange("p (t e) -> p t e", e=NE),
                          base[:].unsqueeze(1).to_broadcast([P, TT, NE]), ALU.add).then_inc(*sorted_.step("logits"))
                dve.wait_ge(sorted_.sem, sorted_.so_far())
                for t in range(TT):
                    dve.max(best[:, t, :], logits[:, t, :]).then_inc(*sorted_.step(f"best{t}"))
                    dve.wait_ge(sorted_.sem, sorted_.so_far())
                    dve.max_index(index[:, t, :], best[:, t, :], logits[:, t, :]).then_inc(*sorted_.step(f"index{t}"))
                dve.wait_ge(sorted_.sem, sorted_.so_far())
                dve.tensor_copy(index_f[:], index[:, :, 0:TOPK]).then_inc(*sorted_.step("float"))
                dve.tensor_tensor(R.gate[:].rearrange("p (t j) -> p t j", j=TOPK), best[:, :, 0:TOPK],
                          best[:, :, 0:1].to_broadcast([P, TT, TOPK]), ALU.subtract).then_inc(*sorted_.step("lead"))
                dve.wait_ge(sorted_.sem, sorted_.so_far())
                dve.wait_ge(made.sem, made.value("token"))
                dve.tensor_tensor(chosen[:], number[:].unsqueeze(1).unsqueeze(1).to_broadcast([P, TT, TOPK, NE]),
                          index_f[:].unsqueeze(3).to_broadcast([P, TT, TOPK, NE]), ALU.is_equal).then_inc(*sorted_.step("chosen"))
                dve.wait_ge(sorted_.sem, sorted_.so_far())
                dve.tensor_reduce(member[:], chosen[:].rearrange("p t j e -> p t e j"), AX, ALU.add).then_inc(*sorted_.step("member"))
                dve.memset(before[:, 0, :], 0.0).then_inc(*sorted_.step("none"))
                for t in range(TT):
                    dve.wait_ge(sorted_.sem, sorted_.so_far())
                    dve.tensor_tensor(before[:, t + 1, :], before[:, t, :], member[:, t, :], ALU.add).then_inc(*sorted_.step(f"before{t}"))
                dve.wait_ge(multiplied.sem, multiplied.value("count"))
                dve.tensor_copy(rank[:], counted[:, 0, 0:TT * NE].rearrange("p (t e) -> p t e", e=NE)).then_inc(*sorted_.step("rank"))
                dve.wait_ge(sorted_.sem, sorted_.so_far())
                dve.tensor_scalar(blocks[:], counted[:, 1, 0:NE], 1.0 / WINDOW, (WINDOW - 1) / (2 * WINDOW),
                                  ALU.mult, ALU.add).then_inc(*sorted_.step("round"))
                dve.wait_ge(sorted_.sem, sorted_.so_far())
                dve.tensor_copy(blocks_i[:], blocks[:]).then_inc(*sorted_.step("int"))
                dve.wait_ge(sorted_.sem, sorted_.so_far())
                dve.tensor_scalar(blocks[:], blocks_i[:], 1.0, None, ALU.max).then_inc(*sorted_.step("least"))
                dve.memset(first[:], 0.0).then_inc(*sorted_.step("zero"))
                dve.wait_ge(sorted_.sem, sorted_.so_far())
                dve.tensor_tensor_scan(first[:, 1:NE + 1], ones[:, 0:NE], blocks[:], 0.0, ALU.mult, ALU.add).then_inc(*sorted_.step("scan"))
                dve.wait_ge(sorted_.sem, sorted_.so_far())
                dve.tensor_scalar(blocks[:], first[:, 0:NE], float(WINDOW), float(WINDOW), ALU.mult, ALU.add).then_inc(*sorted_.step("start"))
                dve.wait_ge(sorted_.sem, sorted_.so_far())
                dve.tensor_tensor(place[:], rank[:], blocks[:].unsqueeze(1).to_broadcast([P, TT, NE]), ALU.add).then_inc(*sorted_.step("place"))
                dve.wait_ge(sorted_.sem, sorted_.so_far())
                dve.tensor_tensor(spot[:], chosen[:], place[:].unsqueeze(2).to_broadcast([P, TT, TOPK, NE]), ALU.mult).then_inc(*sorted_.step("spot"))
                dve.wait_ge(sorted_.sem, sorted_.so_far())
                dve.tensor_reduce(dest[:], spot[:].rearrange("p t j e -> p (t j) e"), AX, ALU.add).then_inc(*sorted_.step("dest"))
                dve.wait_ge(sorted_.sem, sorted_.so_far())
                dve.tensor_copy(R.row[:], dest[:]).then_inc(*sorted_.step("row"))
                dve.tensor_scalar(first[:, NE + 1:NE + 2], first[:, NE:NE + 1], -1.0, WINDOWS + 1.0, ALU.mult, ALU.add).then_inc(*sorted_.step("unused"))
                dve.wait_ge(sorted_.sem, sorted_.so_far())
                dve.tensor_copy(R.first[:], first[:]).then_inc(*sorted_.step("first"))
                dve.wait_ge(raised, 1)
                gates = R.gate[:].rearrange("p (t j) -> p t j", j=TOPK)
                dve.tensor_reduce(total[:], gates, AX, ALU.add).then_inc(*sorted_.step("gate_sum"))
                dve.wait_ge(sorted_.sem, sorted_.so_far())
                dve.reciprocal(total[:], total[:]).then_inc(*sorted_.step("gate_inverse"))
                dve.wait_ge(sorted_.sem, sorted_.so_far())
                dve.tensor_tensor(gates, gates, total[:].unsqueeze(2).to_broadcast([P, TT, TOPK]), ALU.mult).then_inc(*sorted_.step("gate"))
                dve.wait_ge(sorted_.sem, sorted_.so_far())


def turn_biases(nc, I, R, C):
    with ExitStack() as ctx:
        S = scope(nc, ctx, "biases")
        rows = S.sb("rows", [NE, 3072])
        flipped = S.ps("flipped", [P, 2, 512])
        loaded, turned, copied = S.sem("loaded"), S.sem("turned"), S.sem("copied")
        with nc.Block() as block:
            @block.sync
            def _(sp):
                sp.dma_start(rows[:, 0:2048], I["b1"][0]).then_inc(loaded, 16)
                sp.dma_start(rows[:, 2048:3072], I["b2"][0]).then_inc(loaded, 16)

            @block.tensor
            def _(pe):
                pe.wait_ge(loaded, 32)
                for n in range(24):
                    if n < 16:
                        source = rows[:, (n // 2) * 256:(n // 2 + 1) * 256].rearrange("e (p two) -> e two p", two=2)[:, n % 2, :]
                    else:
                        source = rows[:, 2048 + (n - 16) * P:2048 + (n - 15) * P]
                    ins = pe.transpose(flipped[:, n // 16, (n % 16) * NE:(n % 16 + 1) * NE], source, C.ident[0:NE, 0:NE])
                ins.then_inc(turned, 1)

            @block.vector
            def _(dve):
                dve.wait_ge(turned, 1)
                dve.tensor_copy(R.bias[:, 0:16, :], flipped[:, 0, :].rearrange("p (n e) -> p n e", e=NE)).then_inc(copied, 1)
                dve.tensor_copy(R.bias[:, 16:24, :], flipped[:, 1, 0:8 * NE].rearrange("p (n e) -> p n e", e=NE)).then_inc(copied, 1)
                dve.wait_ge(copied, 2)


def experts(nc, I, h_rows, row_token, y_rows, spare, R, C):
    D, PARTS, HALVES, SLOTS = 1024, 6, 12, 4
    LIMIT, ALPHA = 7.0, 1.702
    N, N2 = WINDOW, WINDOW - P
    FULL = 256
    SPLIT = 6
    with ExitStack() as ctx:
        S = scope(nc, ctx, "experts")
        raw = [spare[:, 4 * n:4 * n + 4, :].rearrange("p a (b n) -> p (a b) n", n=512) for n in range(2)]
        raw.append(S.sb("raw", [P, 8, 512])[:])
        high = S.sb("high", [P, SLOTS, 8, 256], F32R)
        low = S.sb("low", [P, SLOTS, 8, 256], F32R)
        index = S.sb("index", [P, 2], I32)
        x = S.sb("x", [P, D])
        x2 = S.sb("x2", [N2, D])
        xs = S.sb("xs", [P, 8, 2, N], F32R)
        hs = S.sb("hs", [P, 8, 2, N], F32R)
        glu = S.sb("glu", [P, 2, 2, N])
        lin = S.sb("lin", [P, 2, 2, N])
        sig = S.sb("sig", [P, 2, 2, N])
        bias = S.sb("bias", [P, 24])
        yT = S.sb("yT", [P, 8, N])
        spark = S.sb("spark", [1, 2])
        y = S.sb("y", [P, D])
        y2 = S.sb("y2", [N2, D])
        up = S.ps("up", [P, 2, 2, 512])
        down = S.ps("down", [P, 4, 512])
        loaded = [S.sem(f"loaded{n}") for n in range(3)]
        index_in, x_in, y_out = S.sem("index_in"), S.sem("x_in"), S.sem("y_out")
        blanked, blank_out, cleared = S.sem("blanked"), S.sem("blank_out"), S.sem("cleared")
        held = S.sem("held")
        AHEAD = SLOTS - 1
        halves = [f"half{h}" for h in range(HALVES)]
        pe_steps = S.steps("multiplied", [f"up{u}" for u in range(8)] + [f"down{n}" for n in range(8)])
        pe_x = S.steps("x_turned", ["first", "second"])
        pe_y = S.steps("y_turned", ["y"])
        act_high = S.steps("high_made", halves)
        dve_low = S.steps("low_made", halves)
        pool_low = S.steps("low_made_too", halves)
        act_hidden = S.steps("act_hidden", ["set"] + [f"{w}{c}" for c in range(4) for w in ("glu0_", "lin0_", "glu1_", "lin1_", "sig")])
        act_xh = S.steps("xh_made", ["first", "second"])
        act_y = S.steps("act_y", ["y", "y2"] + [f"d{n}" for n in range(8)])
        dve_hidden = S.steps("hidden", ["bias"] + [f"{w}{c}" for c in range(4)
                                                   for w in ("glu0_", "lin0_", "glu1_", "lin1_", "min", "clip", "both",
                                                             "hid", "high", "low")])
        dve_xl = S.steps("xl_made", ["first", "second"])
        dve_y = S.steps("dve_y", ["y", "y2"] + [f"d{n}" for n in range(8)])

        def windows_of(eng, e):
            lo = eng.value_load(R.first[0:1, ds(e, 1)], min_val=0, max_val=WINDOWS)
            hi = eng.value_load(R.first[0:1, ds(e + 1, 1)], min_val=1, max_val=WINDOWS)
            return lo, hi

        def two(bank):
            return bank[:, 0:2 * N].rearrange("p (a n) -> p a n", n=N)

        def used(h):
            return f"up{h}" if h < 8 else f"down{2 * h - 15}"

        def free(h):
            return (h - SLOTS, 0) if h >= SLOTS else (h - SLOTS + HALVES, -1)

        def piece(h, tiles):
            return raw[h // 2 % 3][:, tiles, (h % 2) * 256:(h % 2 + 1) * 256]

        with nc.Block() as block:
            @block.sync
            def _(sp):
                sp.sem_inc(blank_out, 16)

                def load(e, c, r):
                    name, back = (halves[2 * c - 5], 0) if c >= 3 else (halves[2 * c + 7], -1)
                    sp.wait_ge(act_high.sem, act_high.value(name, r + back))
                    sp.wait_ge(dve_low.sem, dve_low.value(name, r + back))
                    sp.wait_ge(pool_low.sem, pool_low.value(name, r + back))
                    if c < 4:
                        source = I["w1"][0][ds(e, 1), :, c * 512:(c + 1) * 512]
                    else:
                        source = I["w2"][0][ds(e, 1), :, (c - 4) * 512:(c - 3) * 512]
                    sp.dma_start(raw[c % 3], source.rearrange("a (k p) n -> p (a k) n", p=P)).then_inc(loaded[c % 3], 16)

                def store(r):
                    sp.wait_ge(act_y.sem, act_y.value("y2", r))
                    sp.wait_ge(dve_y.sem, dve_y.value("y2", r))
                    at = (r * N).with_bounds(min_val=0, max_val=WINDOWS * N)
                    sp.dma_start(y_rows[ds(at, P), :], y[:]).then_inc(y_out, 16)
                    sp.dma_start(y_rows[ds(at + P, N2), :], y2[:]).then_inc(y_out, 16)
                with sp.Fori(0, NE) as e:
                    lo, hi = windows_of(sp, e)
                    with sp.Fori(lo, hi) as r:
                        for c in range(PARTS):
                            load(e, c, r)
                            if c == 4:
                                store(r)
                last = sp.value_load(R.first[0:1, NE:NE + 1], min_val=1, max_val=WINDOWS)
                load(0, 0, last)
                load(0, 1, last)
                store(last)
                sp.wait_ge(blanked, 2)
                with sp.Fori(last, WINDOWS + 1) as r:
                    at = (r * N + N).with_bounds(min_val=0, max_val=(WINDOWS + 1) * N)
                    sp.dma_start(y_rows[ds(at, P), :], y[:]).then_inc(blank_out, 16)
                    sp.dma_start(y_rows[ds(at + P, N2), :], y2[:]).then_inc(blank_out, 16)
                unused = sp.value_load(R.first[0:1, NE + 1:NE + 2], min_val=1, max_val=WINDOWS + 1)
                sp.wait_ge(blank_out, unused * 32 + 16)
                sp.sem_inc(held, 1)

            @block.gpsimd
            def _(pool):
                pool.sem_inc(pool_low.sem, pool_low.start)

                def gather(r):
                    row = N if isinstance(r, int) else (r * N + N).with_bounds(min_val=0, max_val=(WINDOWS + 1) * N)
                    pool.wait_ge(pe_x.sem, pe_x.value("second", r - 1))
                    pool.dma_start(index[:, 0:1], row_token[ds(row, P), :],
                                   allow_slow_non_contiguous=True).then_inc(index_in, 16)
                    pool.dma_start(index[0:N2, 1:2], row_token[ds(row + P, N2), :],
                                   allow_slow_non_contiguous=True).then_inc(index_in, 16)
                    pool.wait_ge(index_in, r * 32 + 32)
                    pool.sem_inc(held, 1)
                    for to, where in ((x[:], index[:, 0:1]), (x2[:], index[0:N2, 1:2])):
                        pool.indirect_dma_start(to, None, h_rows,
                                                bass.IndirectOffsetOnAxis(ap=where, axis=0)).then_inc(x_in, 16)

                def low_part(h, r):
                    place, back = free(h)
                    pool.wait_ge(act_high.sem, act_high.value(halves[h], r))
                    pool.wait_ge(pe_steps.sem, pe_steps.value(used(place), r + back))
                    if h == 0:
                        pool_low.round()
                    pool.wait_ge(pool_low.sem, pool_low.so_far(r))
                    pool.tensor_tensor(low[:, h % SLOTS, SPLIT:8, :], piece(h, slice(SPLIT, 8)),
                                       high[:, h % SLOTS, SPLIT:8, :].bitcast(F32), ALU.subtract).then_inc(*pool_low.step(halves[h]))
                gather(0)
                for h in range(AHEAD):
                    low_part(h, 0)
                with pool.Fori(0, NE) as e:
                    lo, hi = windows_of(pool, e)
                    with pool.Fori(lo, hi) as r:
                        for u in range(HALVES):
                            low_part((u + AHEAD) % HALVES, r + (u + AHEAD) // HALVES)
                            if u == 1:
                                gather(r + 1)

            @block.scalar
            def _(act):
                for s in (act_high, act_hidden, act_xh, act_y):
                    act.sem_inc(s.sem, s.start)

                def high_part(h, r):
                    c = h // 2
                    place, back = free(h)
                    if h == 0:
                        act_high.round()
                    act.wait_ge(loaded[c % 3], 16 * (2 * r + c // 3 + 1))
                    act.wait_ge(pe_steps.sem, pe_steps.value(used(place), r + back))
                    act.wait_ge(dve_low.sem, dve_low.value(halves[place], r + back))
                    act.wait_ge(pool_low.sem, pool_low.value(halves[place], r + back))
                    act.copy(high[:, h % SLOTS], piece(h, slice(0, 8))).then_inc(*act_high.step(halves[h]))

                def x_high(r):
                    act_xh.round()
                    for n, name in enumerate(("first", "second")):
                        act.wait_ge(pe_x.sem, pe_x.value(name, r))
                        for b in range(2):
                            ins = act.copy(xs[:, 4 * n + 2 * b:4 * n + 2 * b + 2, 0, :], two(up[:, n, b, :]))
                        ins.then_inc(*act_xh.step(name))

                def take_y(r):
                    act_y.round()
                    act.wait_ge(pe_y.sem, pe_y.value("y", r))
                    act.wait_ge(y_out, r * 32 + 32)
                    act.copy(y[:, 0:512], down[:, 0, :]).then_inc(*act_y.step("y"))
                    act.copy(y2[:, 0:512], down[0:N2, 2, :]).then_inc(*act_y.step("y2"))
                for h in range(AHEAD):
                    high_part(h, 0)
                x_high(0)
                act.wait_ge(cleared, 2)
                with act.Fori(0, NE) as e:
                    lo, hi = windows_of(act, e)
                    with act.Fori(lo, hi) as r:
                        act_hidden.round()
                        act.wait_ge(act_hidden.sem, act_hidden.so_far(r))
                        act.activation(spark[:, 1:2], spark[:, 0:1], ACT.Sigmoid).then_inc(*act_hidden.step("set"))
                        for u in range(HALVES):
                            high_part((u + AHEAD) % HALVES, r + (u + AHEAD) // HALVES)
                            c, j = u // 2, u % 2
                            if u < 8:
                                if j == 0:
                                    act.wait_ge(dve_hidden.sem, dve_hidden.value(f"low{c - 2}" if c >= 2 else "bias", r))
                                act.wait_ge(pe_steps.sem, pe_steps.value(f"up{u}", r))
                                for l, to, w in ((0, glu, "glu"), (1, lin, "lin")):
                                    n = 2 * u + l
                                    act.activation(to[:, c % 2, j, :], up[:, j, l, N:2 * N], ACT.Identity,
                                                   bias=bias[:, n:n + 1]).then_inc(*act_hidden.step(f"{w}{j}_{c}"))
                                if j == 1:
                                    act.wait_ge(dve_hidden.sem, dve_hidden.value(f"min{c}", r))
                                    act.activation(sig[:, c % 2], glu[:, c % 2], ACT.Sigmoid, scale=ALPHA
                                                   ).then_inc(*act_hidden.step(f"sig{c}"))
                                if u == 1:
                                    take_y(r)
                            else:
                                if u == 8:
                                    x_high(r + 1)
                                    act.wait_ge(pe_y.sem, pe_y.value("y", r))
                                for n in (2 * u - 16, 2 * u - 15):
                                    act.wait_ge(pe_steps.sem, pe_steps.value(f"down{n}", r))
                                    act.activation(yT[:, n, :], down[:, n % 4, N:2 * N], ACT.Identity,
                                                   bias=bias[:, 16 + n:17 + n]).then_inc(*act_y.step(f"d{n}"))
                last = act.value_load(R.first[0:1, NE:NE + 1], min_val=1, max_val=WINDOWS)
                take_y(last)

            @block.vector
            def _(dve):
                for s in (dve_low, dve_hidden, dve_xl, dve_y):
                    dve.sem_inc(s.sem, s.start)
                dve.sem_inc(y_out, 32)

                def low_part(h, r):
                    place, back = free(h)
                    if h == 0:
                        dve_low.round()
                    dve.wait_ge(act_high.sem, act_high.value(halves[h], r))
                    dve.wait_ge(pe_steps.sem, pe_steps.value(used(place), r + back))
                    dve.tensor_tensor(low[:, h % SLOTS, 0:SPLIT, :], piece(h, slice(0, SPLIT)),
                                      high[:, h % SLOTS, 0:SPLIT, :].bitcast(F32), ALU.subtract).then_inc(*dve_low.step(halves[h]))

                def x_low(r):
                    dve_xl.round()
                    for n, name in enumerate(("first", "second")):
                        dve.wait_ge(act_xh.sem, act_xh.value(name, r))
                        for b in range(2):
                            at = slice(4 * n + 2 * b, 4 * n + 2 * b + 2)
                            ins = dve.tensor_tensor(xs[:, at, 1, :], two(up[:, n, b, :]), xs[:, at, 0, :].bitcast(F32), ALU.subtract)
                        ins.then_inc(*dve_xl.step(name))

                def take_y(r):
                    dve_y.round()
                    dve.wait_ge(pe_y.sem, pe_y.value("y", r))
                    dve.wait_ge(y_out, r * 32 + 32)
                    dve.tensor_copy(y[:, 512:1024], down[:, 1, :]).then_inc(*dve_y.step("y"))
                    dve.tensor_copy(y2[:, 512:1024], down[0:N2, 3, :]).then_inc(*dve_y.step("y2"))
                dve.memset(yT[:], 0.0).then_inc(cleared, 1)
                dve.memset(spark[:], 0.0).then_inc(cleared, 1)
                for h in range(AHEAD):
                    low_part(h, 0)
                x_low(0)
                with dve.Fori(0, NE) as e:
                    lo, hi = windows_of(dve, e)
                    with dve.Fori(lo, hi) as r:
                        dve.wait_ge(dve_y.sem, dve_y.value("d7", r - 1))
                        dve_hidden.round()
                        dve.tensor_copy(bias[:], R.bias[:, :, ds(e, 1)].rearrange("p n a -> p (n a)")
                                        ).then_inc(*dve_hidden.step("bias"))
                        for u in range(HALVES):
                            low_part((u + AHEAD) % HALVES, r + (u + AHEAD) // HALVES)
                            c, j, s = u // 2, u % 2, u // 2 % 2
                            if u >= 8:
                                if u == 8:
                                    x_low(r + 1)
                                for n in (2 * u - 16, 2 * u - 15):
                                    dve.wait_ge(act_y.sem, act_y.value(f"d{n}", r))
                                    dve.tensor_tensor(yT[:, n, :], down[:, n % 4, 0:N], yT[:, n, :], ALU.add
                                                      ).then_inc(*dve_y.step(f"d{n}"))
                                continue
                            for l, to, w in ((0, glu, "glu"), (1, lin, "lin")):
                                dve.wait_ge(act_hidden.sem, act_hidden.value(f"{w}{j}_{c}", r))
                                dve.tensor_tensor(to[:, s, j, :], up[:, j, l, 0:N], to[:, s, j, :],
                                                  ALU.add).then_inc(*dve_hidden.step(f"{w}{j}_{c}"))
                            if j == 0:
                                continue
                            dve.wait_ge(dve_hidden.sem, dve_hidden.so_far(r))
                            dve.tensor_scalar(glu[:, s], glu[:, s], LIMIT, None, ALU.min).then_inc(*dve_hidden.step(f"min{c}"))
                            dve.tensor_scalar(lin[:, s], lin[:, s], -LIMIT, LIMIT, ALU.max, ALU.min).then_inc(*dve_hidden.step(f"clip{c}"))
                            dve.wait_ge(dve_hidden.sem, dve_hidden.so_far(r))
                            dve.scalar_tensor_tensor(lin[:, s], lin[:, s], 1.0, glu[:, s], ALU.add, ALU.mult
                                                     ).then_inc(*dve_hidden.step(f"both{c}"))
                            dve.wait_ge(act_hidden.sem, act_hidden.value(f"sig{c}", r))
                            dve.wait_ge(dve_hidden.sem, dve_hidden.so_far(r))
                            dve.tensor_tensor(sig[:, s], lin[:, s], sig[:, s], ALU.mult).then_inc(*dve_hidden.step(f"hid{c}"))
                            dve.wait_ge(dve_hidden.sem, dve_hidden.so_far(r))
                            if c == 0:
                                dve.wait_ge(pe_steps.sem, pe_steps.value("down7", r - 1))
                            dve.tensor_copy(hs[:, 2 * c:2 * c + 2, 0, :], sig[:, s]).then_inc(*dve_hidden.step(f"high{c}"))
                            dve.wait_ge(dve_hidden.sem, dve_hidden.so_far(r))
                            dve.tensor_tensor(hs[:, 2 * c:2 * c + 2, 1, :], sig[:, s], hs[:, 2 * c:2 * c + 2, 0, :].bitcast(F32),
                                              ALU.subtract).then_inc(*dve_hidden.step(f"low{c}"))
                            if c == 0:
                                take_y(r)
                last = dve.value_load(R.first[0:1, NE:NE + 1], min_val=1, max_val=WINDOWS)
                take_y(last)
                dve.wait_ge(y_out, last * 32 + 64)
                dve.memset(y[:], 0.0).then_inc(blanked, 1)
                dve.memset(y2[:], 0.0).then_inc(blanked, 1)

            @block.tensor
            def _(pe):
                for s in (pe_steps, pe_x, pe_y):
                    pe.sem_inc(s.sem, s.start)

                def turn_x(r):
                    pe_x.round()
                    pe.wait_ge(x_in, r * 32 + 32)
                    for n, name in enumerate(("first", "second")):
                        pe.wait_ge(dve_hidden.sem, dve_hidden.value(f"lin{n}_3", r - 1))
                        for k in range(4 * n, 4 * n + 4):
                            bank = up[:, n, (k % 4) // 2, :]
                            pe.transpose(bank[:, (k % 2) * N:(k % 2) * N + P], x[:, k * P:(k + 1) * P], C.ident[:])
                            ins = pe.transpose(bank[:, (k % 2) * N + P:(k % 2 + 1) * N], x2[:, k * P:(k + 1) * P],
                                               C.ident[0:N2, 0:N2])
                        ins.then_inc(*pe_x.step(name))

                def product(to, wh, wl, moving, start, stop):
                    pe.matmul(to[:, 0:2 * N], wh, moving.rearrange("p a n -> p (a n)"), start=start, stop=False,
                              skip_group_check=True)
                    return pe.matmul(to[:, 0:FULL], wl, moving.rearrange("p a n -> p (a n)")[:, 0:FULL], start=False,
                                     stop=stop, skip_group_check=True)

                def half_ready(h, r):
                    pe.wait_ge(act_high.sem, act_high.value(halves[h], r))
                    pe.wait_ge(dve_low.sem, dve_low.value(halves[h], r))
                    pe.wait_ge(pool_low.sem, pool_low.value(halves[h], r))

                def turn_y(r):
                    pe.wait_ge(dve_y.sem, dve_y.value("d7", r - 1))
                    for n in range(8):
                        at = slice((n % 4) * P, (n % 4 + 1) * P)
                        pe.transpose(down[:, n // 4, at], yT[:, n, 0:P], C.ident[:])
                        ins = pe.transpose(down[0:N2, 2 + n // 4, at], yT[:, n, P:N], C.ident[:])
                    ins.then_inc(*pe_y.step("y"))
                pe.wait_ge(cleared, 2)
                turn_x(0)
                with pe.Fori(0, NE) as e:
                    lo, hi = windows_of(pe, e)
                    with pe.Fori(lo, hi) as r:
                        pe_steps.round()
                        pe.wait_ge(dve_xl.sem, dve_xl.value("second", r))
                        for u in range(8):
                            half_ready(u, r)
                            if u >= 2:
                                pe.wait_ge(dve_hidden.sem, dve_hidden.value(f"lin{u % 2}_{u // 2 - 1}", r))
                            for l in range(2):
                                for k in range(8):
                                    ins = product(up[:, u % 2, l, :], high[:, u % SLOTS, k, l:256:2],
                                                  low[:, u % SLOTS, k, l:256:2], xs[:, k], k == 0, k == 7)
                            ins.then_inc(*pe_steps.step(f"up{u}"))
                            if u == 1:
                                turn_y(r)
                        turn_x(r + 1)
                        for u in range(8, HALVES):
                            half_ready(u, r)
                            if u == 8:
                                pe.wait_ge(dve_y.sem, dve_y.value("y2", r))
                                pe.wait_ge(act_y.sem, act_y.value("y2", r))
                            for ks in ((range(0, 6), range(6, 8)) if u == 8 else (range(0, 8),)):
                                if u == 8:
                                    pe.wait_ge(dve_hidden.sem, dve_hidden.value("low2" if ks[0] == 0 else "low3", r))
                                for n in (2 * u - 16, 2 * u - 15):
                                    if n >= 4:
                                        pe.wait_ge(dve_y.sem, dve_y.value(f"d{n - 4}", r))
                                    cols = slice(P * (n % 2), P * (n % 2 + 1))
                                    for k in ks:
                                        ins = product(down[:, n % 4, :], high[:, u % SLOTS, k, cols],
                                                      low[:, u % SLOTS, k, cols], hs[:, k], k == 0, k == 7)
                                    if ks[-1] == 7:
                                        ins.then_inc(*pe_steps.step(f"down{n}"))
                last = pe.value_load(R.first[0:1, NE:NE + 1], min_val=1, max_val=WINDOWS)
                turn_y(last)


def combine(nc, I, x, y_rows, out, R, C):
    D, TT, SLOTS = 1024, 8, 8
    with ExitStack() as ctx:
        S = scope(nc, ctx, "combine")
        rows = S.sb("rows", [P, SLOTS, D])
        gains = S.sb("gains", [P, D])
        junk = S.sb("junk", [P, D])
        stat = S.sb("stat", [P, 4, TT])
        gathered = [S.sem(f"gathered{n}") for n in range(SLOTS)]
        gain_in, stored = S.sem("gain_in"), S.sem("stored")
        added = S.steps("added", [f"add{j}" for j in range(TOPK)])
        squared = S.steps("squared", ["sum", "root"], back=1)
        scaled = S.steps("scaled", ["mean", "inverse", "scale"], back=1)
        N = TT * TOPK
        with nc.Block() as block:
            @block.gpsimd
            def _(pool):
                for n in range(N):
                    if n >= SLOTS:
                        pool.wait_ge(added.sem, added.value(f"add{n % TOPK}", n // TOPK - SLOTS // TOPK))
                    pool.indirect_dma_start(rows[:, n % SLOTS, :], None, y_rows,
                                            bass.IndirectOffsetOnAxis(ap=R.row[:, n:n + 1], axis=0)).then_inc(gathered[n % SLOTS], 16)

            @block.vector
            def _(dve):
                dve.sem_inc(added.sem, added.start)
                dve.sem_inc(scaled.sem, scaled.start)
                dve.wait_ge(gain_in, 16)

                def add(t):
                    tile = x[:, t * D:(t + 1) * D]
                    added.round()
                    for j in range(TOPK):
                        n = t * TOPK + j
                        dve.wait_ge(gathered[n % SLOTS], 16 * (n // SLOTS + 1))
                        dve.wait_ge(added.sem, added.so_far(t))
                        dve.scalar_tensor_tensor(tile, rows[:, n % SLOTS, :], R.gate[:, n:n + 1], tile,
                                                 ALU.mult, ALU.add).then_inc(*added.step(f"add{j}"))

                def scale(t):
                    tile = x[:, t * D:(t + 1) * D]
                    scaled.round()
                    dve.wait_ge(squared.sem, squared.value("sum", t))
                    dve.tensor_scalar(stat[:, 1, t:t + 1], stat[:, 0, t:t + 1], 1.0 / D, EPS, ALU.mult, ALU.add).then_inc(*scaled.step("mean"))
                    dve.wait_ge(squared.sem, squared.value("root", t))
                    dve.reciprocal(stat[:, 3, t:t + 1], stat[:, 2, t:t + 1]).then_inc(*scaled.step("inverse"))
                    dve.wait_ge(scaled.sem, scaled.so_far(t))
                    dve.scalar_tensor_tensor(tile, tile, stat[:, 3, t:t + 1], gains[:], ALU.mult, ALU.mult).then_inc(*scaled.step("scale"))
                for t in range(TT + 1):
                    if t < TT:
                        add(t)
                    if t >= 1:
                        scale(t - 1)

            @block.scalar
            def _(act):
                act.sem_inc(squared.sem, squared.start)
                for t in range(TT):
                    act.wait_ge(added.sem, added.value(f"add{TOPK - 1}", t))
                    squared.round()
                    act.wait_ge(squared.sem, squared.so_far(t))
                    act.activation(junk[:], x[:, t * D:(t + 1) * D], ACT.Square,
                                   accum_out=stat[:, 0, t:t + 1]).then_inc(*squared.step("sum"))
                    act.wait_ge(scaled.sem, scaled.value("mean", t))
                    act.activation(stat[:, 2, t:t + 1], stat[:, 1, t:t + 1], ACT.Sqrt).then_inc(*squared.step("root"))

            @block.sync
            def _(sp):
                sp.dma_start(gains[:], row_to_all(I["norm_final_g"])).then_inc(gain_in, 16)
                for t in range(TT):
                    sp.wait_ge(scaled.sem, scaled.value("scale", t))
                    sp.dma_start(out[0, t * P:(t + 1) * P, :], x[:, t * D:(t + 1) * D]).then_inc(stored, 16)
                sp.wait_ge(stored, 16 * TT)


LAMBDA_INIT = 0.8 - 0.6


class Constants:
    def __init__(self):
        self.vector = {}


def build(nc, I, out, stop=99):
    C = Constants()
    Scope.spent = []
    with ExitStack() as top:
        G = scope(nc, top, "g")
        make_constants(nc, G, C)
        load_vectors(nc, G, I, C)
        across = G.sb("across", [P, 8, 1024])
        yT, oT = across[:, 0:4, :], across[:, 4:8, :]
        with ExitStack() as mix:
            M = scope(nc, mix, "m")
            hT = M.sb("hT", [P, 8, 1024])
            with ExitStack() as c:
                S = scope(nc, c, "xs")
                x = S.sb("x", [P, 8 * 1024])
                normalise(nc, "norm_mix", x, 8, I["norm_mix_g"][0], hT, C, load=I["x"][0])
            if stop < 1:
                return
            w_in = I["w_in"][0]
            with ExitStack() as c:
                S = scope(nc, c, "diff")
                qk = S.sb("qk", [P, 8, 1024])
                v = S.sb("v", [P, 8, 512])
                project_channels(nc, "diff_qk", w_in[:, 1824:2848], 2, hT, qk, scale=C.qk_scale)
                diff_values(nc, w_in[:, 2848:3360], hT, v)
                diff_attention(nc, qk[:, 0:4, :], qk[:, 4:8, :], v, oT, C)
            recycle(nc)
            if stop < 2:
                return
            with ExitStack() as c:
                S = scope(nc, c, "rwkv")
                masks = rwkv_masks(nc, S)
                u = S.sb("u", [P, 12, 1024])
                sig = S.sb("sig", [P, 4, 1024])
                a = S.sb("a", [P, 4, 1024])
                project_channels(nc, "rkv", w_in[:, 0:1536], 3, hT, u, mu=C.vector["mu"])
                rwkv_low_rank(nc, I, hT, u, sig, a, yT, C)
                if stop < 3:
                    return
                kkn, fall = hT[:, 0:4, :], hT[:, 4:8, :]
                rwkv_keys(nc, u, a, sig, kkn, fall, masks[2], C)
                rwkv_chunks(nc, u, a, sig, kkn, fall, masks, u[:, 4:8, :], C)
                rwkv_outputs(nc, u[:, 4:8, :], a[:], u[:, 0:4, :], yT, C)
            if stop < 4:
                return
        recycle(nc)
        x = G.sb("x", [P, 8 * 1024])
        add_projection(nc, "w_out", across, I["w_out"][0], x, load=I["x"][0])
        if stop < 5:
            return
        with ExitStack() as c:
            S = scope(nc, c, "cr")
            memT = S.sb("memT", [P, 8, 256])
            kT = S.sb("kT", [P, 8, 256])
            v = S.sb("v", [P, 2, 1024])
            qT = S.sb("qT", [P, 8, 1024])
            with ExitStack() as c2:
                mem = scope(nc, c2, "mem").sb("rows", [P, 2 * 1024])
                normalise(nc, "norm_mem", mem, 2, I["norm_mem_g"][0], memT, C, load=I["mem"][0])
            cross_keys_values(nc, I["w_ckv"][0], memT, kT, v)
            normalise(nc, "norm_cross", x, 8, I["norm_cross_g"][0], across, C)
            project_channels(nc, "cross_q", I["w_cq"][0], 2, across, qT, scale=C.cross_scale)
            cross_attention(nc, qT, kT, v, across, C)
        add_projection(nc, "w_co", across, I["w_co"][0], x)
        if stop < 6:
            return
        recycle(nc)
        R = Constants()
        R.gate = G.sb("gate", [P, 8 * TOPK])
        R.row = G.sb("row", [P, 8 * TOPK], I32)
        R.first = G.sb("first", [P, NE + 2], I32)
        h_rows = nc.dram_tensor("h_rows", [T_ALL, 1024], F32).ap()
        row_token = nc.dram_tensor("row_token", [ROWS, 1], I32).ap()
        y_rows = nc.dram_tensor("y_rows", [(WINDOWS + 2) * WINDOW, 1024], F32).ap()
        R.bias = G.sb("bias", [P, 24, NE])
        normalise(nc, "norm_ffn", x, 8, I["norm_ffn_g"][0], across, C, keep=h_rows)
        turn_biases(nc, I, R, C)
        route(nc, I, across, row_token, R, C)
        if stop < 8:
            return
        experts(nc, I, h_rows, row_token, y_rows, across, R, C)
        combine(nc, I, x, y_rows, out, R, C)


_OUT = (1, 1024, 1024)


def kernel(**inputs):
    import numpy as _np
    import concourse.bacc as _bacc
    from concourse import mybir as _mybir
    from concourse.bass_utils import run_bass_kernel_spmd as _run

    nc = _bacc.Bacc("TRN2", target_bir_lowering=False, num_devices=1)
    arrays, given = {}, {}
    for name, value in inputs.items():
        a = _np.ascontiguousarray(value)
        arrays[f"in_{name}_dram"] = a
        given[name] = nc.dram_tensor(f"in_{name}_dram", a.shape, _mybir.dt.from_np(a.dtype), kind="ExternalInput").ap()
    out = nc.dram_tensor("out_dram", _OUT, _mybir.dt.from_np(_np.dtype("float32")), kind="ExternalOutput").ap()
    build(nc, given, out)
    r = _run(nc, [arrays], core_ids=[0])
    return r.results[0]["out_dram"]
```
